# Optimizing a Trainium2 kernel written in Bass

```python
import jax, jax.numpy as jnp
from jax import lax
import numpy as np
import math
import jax
import jax.numpy as jnp

D_MODEL = 1024
BATCH = 1
SEQ = 512
DEPTH = 2

GRID_W = 64
MIX_WIDTH = 2 * D_MODEL
FOURIER_WIDTH = MIX_WIDTH // 2
N_FOURIER_GROUPS = 4
FOURIER_GROUP = FOURIER_WIDTH // N_FOURIER_GROUPS
ATTN_WIDTH = MIX_WIDTH - FOURIER_WIDTH
HEAD_DIM = 128
N_Q_HEADS = ATTN_WIDTH // HEAD_DIM
N_KV_HEADS = 2
Q_PER_KV = N_Q_HEADS // N_KV_HEADS
KV_WIDTH = N_KV_HEADS * HEAD_DIM
Q_BLOCK = 128
ROPE_THETA = 10000.0
ROPE_AXIS_DIM = HEAD_DIM // 2
RNN_WIDTH = MIX_WIDTH
N_RNN_BLOCKS = 16
RNN_BLOCK = RNN_WIDTH // N_RNN_BLOCKS
CONV_WIDTH = 4
CONV_LEFT = 2
RG_LRU_C = 8.0
NORM_EPS = 1e-6
EVEN_IN_WIDTH = 2 * FOURIER_WIDTH + ATTN_WIDTH + 2 * KV_WIDTH + ATTN_WIDTH
EVEN_SPLITS = (FOURIER_WIDTH,
               2 * FOURIER_WIDTH,
               2 * FOURIER_WIDTH + ATTN_WIDTH,
               2 * FOURIER_WIDTH + ATTN_WIDTH + KV_WIDTH,
               2 * FOURIER_WIDTH + ATTN_WIDTH + 2 * KV_WIDTH)


def rms_norm(x, g):
    xf = x.astype(jnp.float32)
    y = xf * lax.rsqrt(jnp.mean(xf * xf, axis=-1, keepdims=True) + NORM_EPS)
    return (y * g.astype(jnp.float32)).astype(x.dtype)

def axial_rope_tables(seq_len):
    rows = seq_len // GRID_W
    row = jnp.broadcast_to(jnp.arange(rows)[:, None], (rows, GRID_W)).reshape(-1).astype(jnp.float32)
    col = jnp.broadcast_to(jnp.arange(GRID_W)[None, :], (rows, GRID_W)).reshape(-1).astype(jnp.float32)
    inv_freq = ROPE_THETA ** (-jnp.arange(0, ROPE_AXIS_DIM, 2, dtype=jnp.float32) / ROPE_AXIS_DIM)
    ang_r = row[:, None] * inv_freq[None, :]
    ang_c = col[:, None] * inv_freq[None, :]
    return (jnp.cos(ang_r), jnp.sin(ang_r), jnp.cos(ang_c), jnp.sin(ang_c))

def rope_half(x, cos, sin):
    x1, x2 = jnp.split(x, 2, axis=-1)
    c = cos[:, None, :]
    s = sin[:, None, :]
    return jnp.concatenate([x1 * c - x2 * s, x1 * s + x2 * c], axis=-1)

def axial_rope(x, tables):
    cos_r, sin_r, cos_c, sin_c = tables
    xf = x.astype(jnp.float32)
    x_row, x_col = jnp.split(xf, 2, axis=-1)
    out = jnp.concatenate([rope_half(x_row, cos_r, sin_r), rope_half(x_col, cos_c, sin_c)], axis=-1)
    return out.astype(x.dtype)

def blocked_attention(q, k, v):
    b, s = q.shape[0], q.shape[1]
    n_blocks = s // Q_BLOCK
    qb = q.reshape(b, n_blocks, Q_BLOCK, N_KV_HEADS, Q_PER_KV, HEAD_DIM).transpose(1, 0, 2, 3, 4, 5)
    scale = HEAD_DIM ** -0.5

    def one_block(q_blk):
        scores = jnp.einsum('bqhgd,bkhd->bhgqk', q_blk, k,
                            preferred_element_type=jnp.float32) * scale
        probs = jax.nn.softmax(scores, axis=-1).astype(v.dtype)
        return jnp.einsum('bhgqk,bkhd->bqhgd', probs, v)

    out = lax.map(one_block, qb)
    return out.transpose(1, 0, 2, 3, 4, 5).reshape(b, s, N_Q_HEADS * HEAD_DIM)

def fourier_attention_layer(x, norm_g, w_in, fourier_w, q_gain, k_gain, w_out, rope):
    b, s, _ = x.shape
    h = rms_norm(x, norm_g)
    proj = h @ w_in
    f_in, f_gate, q, k, v, a_gate = jnp.split(proj, EVEN_SPLITS, axis=-1)
    fg = f_in.astype(jnp.float32).reshape(b, s, N_FOURIER_GROUPS, FOURIER_GROUP)
    fmix = jnp.fft.fftn(fg, axes=(1, 3), norm="ortho").real.astype(x.dtype)
    fmix = jnp.einsum('bsgc,gce->bsge', fmix, fourier_w).reshape(b, s, FOURIER_WIDTH)
    f_out = fmix * jax.nn.silu(f_gate)
    q = rms_norm(q.reshape(b, s, N_Q_HEADS, HEAD_DIM), q_gain)
    k = rms_norm(k.reshape(b, s, N_KV_HEADS, HEAD_DIM), k_gain)
    v = v.reshape(b, s, N_KV_HEADS, HEAD_DIM)
    q = axial_rope(q, rope)
    k = axial_rope(k, rope)
    a_out = blocked_attention(q, k, v) * jax.nn.silu(a_gate)
    return x + jnp.concatenate([f_out, a_out], axis=-1) @ w_out

def rglru_scan(xc, w_a, b_a, w_x, b_x, lam, reverse):
    b, s, _ = xc.shape
    xb = xc.astype(jnp.float32).reshape(b, s, N_RNN_BLOCKS, RNN_BLOCK)
    r = jax.nn.sigmoid(jnp.einsum('bshc,hce->bshe', xb, w_a.astype(jnp.float32)) + b_a).reshape(b, s, RNN_WIDTH)
    i = jax.nn.sigmoid(jnp.einsum('bshc,hce->bshe', xb, w_x.astype(jnp.float32)) + b_x).reshape(b, s, RNN_WIDTH)
    log_a = -RG_LRU_C * r * jax.nn.softplus(-lam.astype(jnp.float32))
    a = jnp.exp(log_a)
    u = jnp.sqrt(-jnp.expm1(2.0 * log_a)) * (i * xb.reshape(b, s, RNN_WIDTH))

    def combine(left, right):
        a1, h1 = left
        a2, h2 = right
        return a1 * a2, a2 * h1 + h2

    _, hseq = lax.associative_scan(combine, (a, u), reverse=reverse, axis=1)
    return hseq

def rglru_layer(x, norm_g, w_in, conv_w, conv_b, w_a, b_a, w_x, b_x, lam, w_out):
    s = x.shape[1]
    h = rms_norm(x, norm_g)
    xr, gate = jnp.split(h @ w_in, 2, axis=-1)
    xp = jnp.pad(xr, ((0, 0), (CONV_LEFT, CONV_WIDTH - 1 - CONV_LEFT), (0, 0)))
    xc = conv_b + xp[:, 0:s] * conv_w[0]
    for j in range(1, CONV_WIDTH):
        xc = xc + xp[:, j:j + s] * conv_w[j]
    y = (rglru_scan(xc, w_a[0], b_a[0], w_x[0], b_x[0], lam[0], reverse=False)
         + rglru_scan(xc, w_a[1], b_a[1], w_x[1], b_x[1], lam[1], reverse=True))
    return x + (y.astype(x.dtype) * jax.nn.silu(gate)) @ w_out

def first_inputs(seed: int = 0) -> dict:
    key = jax.random.key(seed)
    ks = jax.random.split(key, 20)
    n_even = (DEPTH + 1) // 2
    n_odd = DEPTH // 2

    def nrm(k, shape, scale):
        return jax.random.normal(k, shape, jnp.float32) * scale

    x = nrm(ks[0], (BATCH, SEQ, D_MODEL), 1.0)
    even_norm = 1.0 + nrm(ks[1], (n_even, D_MODEL), 0.02)
    even_w_in = nrm(ks[2], (n_even, D_MODEL, EVEN_IN_WIDTH), D_MODEL ** -0.5)
    fourier_w = nrm(ks[3], (n_even, N_FOURIER_GROUPS, FOURIER_GROUP, FOURIER_GROUP), FOURIER_GROUP ** -0.5)
    q_gain = 1.0 + nrm(ks[4], (n_even, HEAD_DIM), 0.02)
    k_gain = 1.0 + nrm(ks[5], (n_even, HEAD_DIM), 0.02)
    even_w_out = nrm(ks[6], (n_even, MIX_WIDTH, D_MODEL), MIX_WIDTH ** -0.5)
    odd_norm = 1.0 + nrm(ks[7], (n_odd, D_MODEL), 0.02)
    odd_w_in = nrm(ks[8], (n_odd, D_MODEL, 2 * RNN_WIDTH), D_MODEL ** -0.5)
    conv_w = nrm(ks[9], (n_odd, CONV_WIDTH, RNN_WIDTH), CONV_WIDTH ** -0.5)
    conv_b = nrm(ks[10], (n_odd, RNN_WIDTH), 0.01)
    gate_a_w = nrm(ks[11], (n_odd, 2, N_RNN_BLOCKS, RNN_BLOCK, RNN_BLOCK), RNN_BLOCK ** -0.5)
    gate_a_b = nrm(ks[12], (n_odd, 2, N_RNN_BLOCKS, RNN_BLOCK), 0.01)
    gate_x_w = nrm(ks[13], (n_odd, 2, N_RNN_BLOCKS, RNN_BLOCK, RNN_BLOCK), RNN_BLOCK ** -0.5)
    gate_x_b = nrm(ks[14], (n_odd, 2, N_RNN_BLOCKS, RNN_BLOCK), 0.01)
    a_pow = jax.random.uniform(ks[15], (n_odd, 2, RNN_WIDTH), jnp.float32, minval=0.9, maxval=0.999)
    a0 = a_pow ** (1.0 / RG_LRU_C)
    rglru_lambda = jnp.log(a0) - jnp.log1p(-a0)
    odd_w_out = nrm(ks[16], (n_odd, RNN_WIDTH, D_MODEL), RNN_WIDTH ** -0.5)
    final_norm = 1.0 + nrm(ks[17], (D_MODEL,), 0.02)
    return {"x": x, "even_norm": even_norm, "even_w_in": even_w_in, "fourier_w": fourier_w,
            "q_gain": q_gain, "k_gain": k_gain, "even_w_out": even_w_out,
            "odd_norm": odd_norm, "odd_w_in": odd_w_in, "conv_w": conv_w, "conv_b": conv_b,
            "gate_a_w": gate_a_w, "gate_a_b": gate_a_b, "gate_x_w": gate_x_w, "gate_x_b": gate_x_b,
            "rglru_lambda": rglru_lambda, "odd_w_out": odd_w_out, "final_norm": final_norm}

def first_block(x, even_norm, even_w_in, fourier_w, q_gain, k_gain, even_w_out,
              odd_norm, odd_w_in, conv_w, conv_b, gate_a_w, gate_a_b, gate_x_w, gate_x_b,
              rglru_lambda, odd_w_out, final_norm):
    rope = axial_rope_tables(x.shape[1])
    h = x
    for layer in range(DEPTH):
        i = layer // 2
        if layer % 2 == 0:
            h = fourier_attention_layer(h, even_norm[i], even_w_in[i], fourier_w[i],
                                        q_gain[i], k_gain[i], even_w_out[i], rope)
        else:
            h = rglru_layer(h, odd_norm[i], odd_w_in[i], conv_w[i], conv_b[i],
                            gate_a_w[i], gate_a_b[i], gate_x_w[i], gate_x_b[i],
                            rglru_lambda[i], odd_w_out[i])
    return rms_norm(h, final_norm)


DEPTH_2 = 1

CHUNK = 64
EPS = 1e-6

GDN_HEADS = 8
GDN_DK = 128
GDN_DV = 128
GDN_QK_W = GDN_HEADS * GDN_DK
GDN_V_W = GDN_HEADS * GDN_DV
CONV_K = 4

HGRN_HEADS = 8
HGRN_DK = 128
HGRN_DV = 128
HGRN_K_W = HGRN_HEADS * HGRN_DK
HGRN_V_W = HGRN_HEADS * HGRN_DV

N_MEM = 256
XA_HEADS = 4
XA_DH = D_MODEL // XA_HEADS

N_GROUPS = 4
EXP_PER_GROUP = 8
N_EXPERTS = N_GROUPS * EXP_PER_GROUP
TOP_K = 2
D_FF_EXPERT = 512
MOE_BLOCK = 256

IN_SPLITS = (2 * GDN_QK_W + GDN_V_W, GDN_HEADS, GDN_HEADS, GDN_V_W,
             HGRN_K_W, HGRN_K_W, HGRN_V_W, HGRN_V_W, D_MODEL, D_MODEL)
IN_COLS = 2 * GDN_QK_W + 2 * GDN_V_W + 2 * GDN_HEADS + 2 * HGRN_K_W + 2 * HGRN_V_W + 2 * D_MODEL


def rmsnorm(x, w):
    xf = x.astype(jnp.float32)
    xf = xf * lax.rsqrt(jnp.mean(xf * xf, axis=-1, keepdims=True) + EPS)
    return (xf * w.astype(jnp.float32)).astype(x.dtype)

def l2norm(x):
    xf = x.astype(jnp.float32)
    return (xf * lax.rsqrt(jnp.sum(xf * xf, axis=-1, keepdims=True) + EPS)).astype(x.dtype)

def split_cols(t, sizes):
    out, start = [], 0
    for n in sizes:
        out.append(t[..., start:start + n])
        start += n
    return out

def causal_depthwise_conv(x, w):
    k, c = w.shape
    return lax.conv_general_dilated(
        x, w[:, None, :].astype(x.dtype), window_strides=(1,), padding=[(k - 1, 0)],
        dimension_numbers=('NWC', 'WIO', 'NWC'), feature_group_count=c)

def to_chunks(t):
    b, s, h, d = t.shape
    return t.reshape(b, s // CHUNK, CHUNK, h, d).transpose(0, 3, 1, 2, 4)

def scalar_chunks(t):
    b, s, h = t.shape
    return t.reshape(b, s // CHUNK, CHUNK, h).transpose(0, 3, 1, 2)

def from_chunks(t):
    b, h, n, c, d = t.shape
    return t.transpose(0, 2, 3, 1, 4).reshape(b, n * c, h, d)

def gated_delta_rule(q, k, v, g, beta):
    c = q.shape[-2]
    dk = q.shape[-1]
    dv = v.shape[-1]
    q = q * dk ** -0.5
    causal = jnp.tril(jnp.ones((c, c), dtype=bool))
    strict = jnp.tril(jnp.ones((c, c), dtype=bool), -1)
    cum = jnp.cumsum(g, axis=-1)
    decay = jnp.exp(jnp.where(causal, cum[..., :, None] - cum[..., None, :], -jnp.inf))
    kb = k * beta[..., None]
    a_low = jnp.where(strict, jnp.einsum('bhnid,bhnjd->bhnij', kb, k) * decay, 0.0)
    eye = jnp.eye(c, dtype=q.dtype)
    rhs = jnp.concatenate([v * beta[..., None], kb * jnp.exp(cum)[..., None]], axis=-1)
    sol = lax.linalg.triangular_solve(eye + a_low, rhs, left_side=True, lower=True)
    u, w = sol[..., :dv], sol[..., dv:]
    qk_intra = jnp.where(causal, jnp.einsum('bhnid,bhnjd->bhnij', q, k) * decay, 0.0)
    q_dec = q * jnp.exp(cum)[..., None]
    last = cum[..., -1:]
    k_dec = k * jnp.exp(last - cum)[..., None]
    chunk_decay = jnp.exp(last[..., 0])

    def step(state, xs):
        qi, wi, ui, ki, ai, di = xs
        v_new = ui - jnp.einsum('bhcd,bhde->bhce', wi, state)
        o = jnp.einsum('bhcd,bhde->bhce', qi, state) + jnp.einsum('bhij,bhje->bhie', ai, v_new)
        state = state * di[..., None, None] + jnp.einsum('bhcd,bhce->bhde', ki, v_new)
        return state, o

    b, h = q.shape[0], q.shape[1]
    s0 = jnp.zeros((b, h, dk, dv), q.dtype)
    xs = tuple(jnp.moveaxis(t, 2, 0) for t in (q_dec, w, u, k_dec, qk_intra, chunk_decay))
    _, o = lax.scan(step, s0, xs)
    return jnp.moveaxis(o, 0, 2)

def hgrn2_chunked(q, k, v, log_f):
    c = q.shape[-2]
    causal = jnp.tril(jnp.ones((c, c), dtype=bool))
    cum = jnp.cumsum(log_f, axis=-2)
    q_in = q * jnp.exp(cum)
    k_in = k * jnp.exp(-cum)
    intra = jnp.where(causal, jnp.einsum('bhnid,bhnjd->bhnij', q_in, k_in), 0.0)
    last = cum[..., -1:, :]
    k_dec = k * jnp.exp(last - cum)
    chunk_decay = jnp.exp(last[..., 0, :])

    def step(state, xs):
        qi, ki, vi, ai, di = xs
        o = jnp.einsum('bhcd,bhde->bhce', qi, state) + jnp.einsum('bhij,bhje->bhie', ai, vi)
        state = di[..., :, None] * state + jnp.einsum('bhcd,bhce->bhde', ki, vi)
        return state, o

    b, h, _, _, dk = q.shape
    dv = v.shape[-1]
    s0 = jnp.zeros((b, h, dk, dv), q.dtype)
    xs = tuple(jnp.moveaxis(t, 2, 0) for t in (q_in, k_dec, v, intra, chunk_decay))
    _, o = lax.scan(step, s0, xs)
    return jnp.moveaxis(o, 0, 2)

def mixer_block(hn, w_in, conv_w, a_log, dt_bias, gdn_norm_w, lb, hgrn_norm_w,
                w_branch_a, w_branch_b, w_out):
    b, s, _ = hn.shape
    dt = hn.dtype
    f32 = jnp.float32
    (qkv_a, alpha_pre, beta_pre, og_a, f_pre, q_b, i_b, og_b, gate_a, gate_b) = split_cols(hn @ w_in, IN_SPLITS)

    qkv = jax.nn.silu(causal_depthwise_conv(qkv_a, conv_w))
    q_a = l2norm(qkv[..., :GDN_QK_W].reshape(b, s, GDN_HEADS, GDN_DK))
    k_a = l2norm(qkv[..., GDN_QK_W:2 * GDN_QK_W].reshape(b, s, GDN_HEADS, GDN_DK))
    v_a = qkv[..., 2 * GDN_QK_W:].reshape(b, s, GDN_HEADS, GDN_DV)
    beta = jax.nn.sigmoid(beta_pre.astype(f32))
    log_alpha = -jnp.exp(a_log.astype(f32)) * jax.nn.softplus(alpha_pre.astype(f32) + dt_bias.astype(f32))
    o_a = gated_delta_rule(to_chunks(q_a).astype(f32), to_chunks(k_a).astype(f32), to_chunks(v_a).astype(f32),
                           scalar_chunks(log_alpha), scalar_chunks(beta))
    o_a = from_chunks(o_a).astype(dt)
    y_a = (rmsnorm(o_a, gdn_norm_w) * jax.nn.silu(og_a.reshape(b, s, GDN_HEADS, GDN_DV))).reshape(b, s, GDN_V_W)

    forget = lb + (1.0 - lb) * jax.nn.sigmoid(f_pre.astype(f32))
    log_f = jnp.log(forget)
    k_b = 1.0 - forget
    q_b = q_b.astype(f32) * HGRN_DK ** -0.5
    o_b = hgrn2_chunked(to_chunks(q_b.reshape(b, s, HGRN_HEADS, HGRN_DK)),
                        to_chunks(k_b.reshape(b, s, HGRN_HEADS, HGRN_DK)),
                        to_chunks(i_b.astype(f32).reshape(b, s, HGRN_HEADS, HGRN_DV)),
                        to_chunks(log_f.reshape(b, s, HGRN_HEADS, HGRN_DK)))
    o_b = from_chunks(o_b).astype(dt)
    y_b = (rmsnorm(o_b, hgrn_norm_w) * jax.nn.silu(og_b.reshape(b, s, HGRN_HEADS, HGRN_DV))).reshape(b, s, HGRN_V_W)

    merged = jax.nn.sigmoid(gate_a) * (y_a @ w_branch_a) + jax.nn.sigmoid(gate_b) * (y_b @ w_branch_b)
    return merged @ w_out

def cross_attention(hn, memn, wq, wkv, wo):
    b, s, _ = hn.shape
    m = memn.shape[1]
    q = (hn @ wq).reshape(b, s, XA_HEADS, XA_DH)
    kv = memn @ wkv
    k = kv[..., :D_MODEL].reshape(b, m, XA_HEADS, XA_DH)
    v = kv[..., D_MODEL:].reshape(b, m, XA_HEADS, XA_DH)
    scores = jnp.einsum('bshd,bmhd->bhsm', q, k).astype(jnp.float32) * XA_DH ** -0.5
    p = jax.nn.softmax(scores, axis=-1).astype(v.dtype)
    o = jnp.einsum('bhsm,bmhd->bshd', p, v).reshape(b, s, D_MODEL)
    return o @ wo

def hier_moe(hn, wrg, brg, wre, bre, w_gate, w_up, w_down):
    b, s, d = hn.shape
    t = hn.reshape(-1, d)
    n_tok = t.shape[0]
    g_prob = jax.nn.softmax((t @ wrg + brg).astype(jnp.float32), axis=-1)
    g_p, g_idx = lax.top_k(g_prob, 1)
    e_logits = (t @ wre + bre).astype(jnp.float32).reshape(n_tok, N_GROUPS, EXP_PER_GROUP)
    e_logits = jnp.take_along_axis(e_logits, g_idx[:, :, None], axis=1)[:, 0]
    e_p, e_idx = lax.top_k(jax.nn.softmax(e_logits, axis=-1), TOP_K)
    weights = g_p * e_p / jnp.sum(e_p, axis=-1, keepdims=True)
    expert = g_idx * EXP_PER_GROUP + e_idx

    m = n_tok * TOP_K
    flat_e = expert.reshape(-1).astype(jnp.int32)
    flat_tok = jnp.repeat(jnp.arange(n_tok, dtype=jnp.int32), TOP_K)
    flat_w = weights.reshape(-1)
    order = jnp.argsort(flat_e)
    se, stok, sw = flat_e[order], flat_tok[order], flat_w[order]
    sizes = jnp.bincount(se, length=N_EXPERTS).astype(jnp.int32)
    padded = ((sizes + MOE_BLOCK - 1) // MOE_BLOCK) * MOE_BLOCK
    starts = jnp.cumsum(sizes) - sizes
    pend = jnp.cumsum(padded)
    pstart = pend - padded
    dest = pstart[se] + (jnp.arange(m, dtype=jnp.int32) - starts[se])
    n_rows = ((m + MOE_BLOCK - 1) // MOE_BLOCK) * MOE_BLOCK + N_EXPERTS * MOE_BLOCK
    n_blocks = n_rows // MOE_BLOCK
    x_pad = jnp.zeros((n_rows, d), t.dtype).at[dest].set(t[stok])
    w_pad = jnp.zeros((n_rows,), jnp.float32).at[dest].set(sw)
    tok_pad = jnp.full((n_rows,), n_tok, jnp.int32).at[dest].set(stok)
    blk_start = jnp.arange(n_blocks, dtype=jnp.int32) * MOE_BLOCK
    blk_e = jnp.clip(jnp.searchsorted(pend, blk_start, side='right'), 0, N_EXPERTS - 1)

    def block_mlp(args):
        xb, e = args
        return (jax.nn.silu(xb @ w_gate[e]) * (xb @ w_up[e])) @ w_down[e]

    y_pad = lax.map(block_mlp, (x_pad.reshape(n_blocks, MOE_BLOCK, d), blk_e)).reshape(n_rows, d)
    y_pad = y_pad * w_pad[:, None].astype(y_pad.dtype)
    out = jax.ops.segment_sum(y_pad, tok_pad, num_segments=n_tok)
    return out.reshape(b, s, d)

def second_inputs(seed: int = 0) -> dict:
    key = jax.random.key(seed)
    ks = jax.random.split(key, 32)
    f32 = jnp.float32
    L = DEPTH_2

    def nrm(k, shape, fan_in):
        return jax.random.normal(k, shape, f32) * fan_in ** -0.5

    def gain(k, shape):
        return 1.0 + 0.02 * jax.random.normal(k, shape, f32)

    dt_init = jnp.exp(jax.random.uniform(ks[6], (L, GDN_HEADS), f32, math.log(1e-3), math.log(1e-1)))
    return {
        'x': jax.random.normal(ks[0], (BATCH, SEQ, D_MODEL), f32),
        'mem': jax.random.normal(ks[1], (BATCH, N_MEM, D_MODEL), f32),
        'norm_mix_w': gain(ks[2], (L, D_MODEL)),
        'w_in': nrm(ks[3], (L, D_MODEL, IN_COLS), D_MODEL),
        'conv_w': nrm(ks[4], (L, CONV_K, 2 * GDN_QK_W + GDN_V_W), CONV_K),
        'gdn_a_log': jnp.log(jax.random.uniform(ks[5], (L, GDN_HEADS), f32, 1.0, 16.0)),
        'gdn_dt_bias': jnp.log(jnp.expm1(dt_init)),
        'gdn_out_norm_w': gain(ks[7], (L, GDN_DV)),
        'hgrn_lb': 0.1 * jax.random.normal(ks[8], (L + 1, HGRN_K_W), f32),
        'hgrn_out_norm_w': gain(ks[9], (L, HGRN_DV)),
        'w_branch_a': nrm(ks[10], (L, GDN_V_W, D_MODEL), GDN_V_W),
        'w_branch_b': nrm(ks[11], (L, HGRN_V_W, D_MODEL), HGRN_V_W),
        'w_out': nrm(ks[12], (L, D_MODEL, D_MODEL), D_MODEL),
        'norm_xattn_w': gain(ks[13], (L, D_MODEL)),
        'norm_mem_w': gain(ks[14], (L, D_MODEL)),
        'xattn_wq': nrm(ks[15], (L, D_MODEL, D_MODEL), D_MODEL),
        'xattn_wkv': nrm(ks[16], (L, D_MODEL, 2 * D_MODEL), D_MODEL),
        'xattn_wo': nrm(ks[17], (L, D_MODEL, D_MODEL), D_MODEL),
        'norm_ffn_w': gain(ks[18], (L, D_MODEL)),
        'router_group_w': nrm(ks[19], (L, D_MODEL, N_GROUPS), D_MODEL),
        'router_group_b': 0.01 * jax.random.normal(ks[20], (L, N_GROUPS), f32),
        'router_expert_w': nrm(ks[21], (L, D_MODEL, N_EXPERTS), D_MODEL),
        'router_expert_b': 0.01 * jax.random.normal(ks[22], (L, N_EXPERTS), f32),
        'expert_w_gate': nrm(ks[23], (L, N_EXPERTS, D_MODEL, D_FF_EXPERT), D_MODEL),
        'expert_w_up': nrm(ks[24], (L, N_EXPERTS, D_MODEL, D_FF_EXPERT), D_MODEL),
        'expert_w_down': nrm(ks[25], (L, N_EXPERTS, D_FF_EXPERT, D_MODEL), D_FF_EXPERT),
        'final_norm_w': gain(ks[26], (D_MODEL,)),
    }

def second_block(x, mem, norm_mix_w, w_in, conv_w, gdn_a_log, gdn_dt_bias, gdn_out_norm_w,
              hgrn_lb, hgrn_out_norm_w, w_branch_a, w_branch_b, w_out,
              norm_xattn_w, norm_mem_w, xattn_wq, xattn_wkv, xattn_wo,
              norm_ffn_w, router_group_w, router_group_b, router_expert_w, router_expert_b,
              expert_w_gate, expert_w_up, expert_w_down, final_norm_w):
    lb_all = jnp.cumsum(jax.nn.softmax(hgrn_lb.astype(jnp.float32), axis=0), axis=0)
    h = x
    for layer in range(DEPTH_2):
        hn = rmsnorm(h, norm_mix_w[layer])
        h = h + mixer_block(hn, w_in[layer], conv_w[layer], gdn_a_log[layer], gdn_dt_bias[layer],
                            gdn_out_norm_w[layer], lb_all[layer], hgrn_out_norm_w[layer],
                            w_branch_a[layer], w_branch_b[layer], w_out[layer])
        hn = rmsnorm(h, norm_xattn_w[layer])
        memn = rmsnorm(mem, norm_mem_w[layer])
        h = h + cross_attention(hn, memn, xattn_wq[layer], xattn_wkv[layer], xattn_wo[layer])
        hn = rmsnorm(h, norm_ffn_w[layer])
        h = h + hier_moe(hn, router_group_w[layer], router_group_b[layer], router_expert_w[layer],
                         router_expert_b[layer], expert_w_gate[layer], expert_w_up[layer], expert_w_down[layer])
    return rmsnorm(h, final_norm_w)


def setup_inputs(seed=0):
    out = dict(first_inputs(seed))
    for name, value in second_inputs(seed + 1).items():
        if name != "x":
            out[name + "_2"] = value
    return out


def reference(
    x, even_norm, even_w_in, fourier_w, q_gain, k_gain, even_w_out, odd_norm, odd_w_in, conv_w,
    conv_b, gate_a_w, gate_a_b, gate_x_w, gate_x_b, rglru_lambda, odd_w_out, final_norm, mem_2,
    norm_mix_w_2, w_in_2, conv_w_2, gdn_a_log_2, gdn_dt_bias_2, gdn_out_norm_w_2, hgrn_lb_2,
    hgrn_out_norm_w_2, w_branch_a_2, w_branch_b_2, w_out_2, norm_xattn_w_2, norm_mem_w_2,
    xattn_wq_2, xattn_wkv_2, xattn_wo_2, norm_ffn_w_2, router_group_w_2, router_group_b_2,
    router_expert_w_2, router_expert_b_2, expert_w_gate_2, expert_w_up_2, expert_w_down_2,
    final_norm_w_2,
):
    x = first_block(
        x, even_norm, even_w_in, fourier_w, q_gain, k_gain, even_w_out, odd_norm, odd_w_in,
        conv_w, conv_b, gate_a_w, gate_a_b, gate_x_w, gate_x_b, rglru_lambda, odd_w_out,
        final_norm,
    )
    return second_block(
        x, mem_2, norm_mix_w_2, w_in_2, conv_w_2, gdn_a_log_2, gdn_dt_bias_2, gdn_out_norm_w_2,
        hgrn_lb_2, hgrn_out_norm_w_2, w_branch_a_2, w_branch_b_2, w_out_2, norm_xattn_w_2,
        norm_mem_w_2, xattn_wq_2, xattn_wkv_2, xattn_wo_2, norm_ffn_w_2, router_group_w_2,
        router_group_b_2, router_expert_w_2, router_expert_b_2, expert_w_gate_2, expert_w_up_2,
        expert_w_down_2, final_norm_w_2,
    )


_drawn_inputs = setup_inputs


def setup_inputs(seed=0):
    import zlib

    import numpy as np

    out = dict(_drawn_inputs(seed))
    spreads = {}
    factors = {'q_gain': 8.0,
     'k_gain': 4.675,
     'gate_a_b': 8.0,
     'gate_x_b': 5.785,
     'gdn_out_norm_w_2': 3.96,
     'hgrn_out_norm_w_2': 2.722,
     'norm_xattn_w_2': 5.196,
     'norm_mem_w_2': 5.15,
     'router_group_b_2': 64.0,
     'router_expert_b_2': 30.743,
     'final_norm_w_2': 7.628,
     'norm_ffn_w_2': 8.0}
    for name, (base, spread) in spreads.items():
        noise = np.random.default_rng([zlib.crc32(name.encode()), seed]).standard_normal(out[name].shape)
        drawn = base * np.exp(spread * noise) if base else spread * noise
        out[name] = jnp.asarray(drawn.astype(out[name].dtype))
    for name, factor in factors.items():
        out[name] = (out[name] * factor).astype(out[name].dtype)
    return out
```

```python
from contextlib import ExitStack

import numpy as np

import concourse.bass as bass
from concourse import mybir

F32 = mybir.dt.float32
F32R = mybir.dt.float32r
I32 = mybir.dt.int32
U32 = mybir.dt.uint32
ACT = mybir.ActivationFunctionType
ALU = mybir.AluOpType
AX = mybir.AxisListType

P = 128
SEQ = 512
NT = SEQ // P
D = 1024
KD = D // P
HD = 128
EPS = 1e-6
BIG = 1e30

GROUPS, GROUP = 4, 256
NQ, NKV = 8, 2
RNN = 2048
RB = RNN // P
BATCH = 4
HEADS = 8
QC = 64
MEM = 256
XH, XD = 4, 256
NG, EPG = 4, 8
NE = NG * EPG
FF = 512
BLK = 64
NRB = SEQ // BLK
OVER = 2 * SEQ // BLK - 1
BLOCKS = NE + OVER

RAW = 4
SPL = 2
UNIT = 4 * 512


def constants():
    out = {}
    c = np.arange(GROUP)
    ang = 2.0 * np.pi * ((c[:, None] * c[None, :]) % GROUP) / GROUP
    out["c_dft_c"] = (np.concatenate([np.cos(ang), np.sin(ang)], 1) / np.sqrt(GROUP)).astype(np.float32)
    s = np.arange(SEQ)
    ang = 2.0 * np.pi * ((s[:, None] * s[None, :]) % SEQ) / SEQ
    out["c_dft_s"] = np.stack([np.cos(ang), -np.sin(ang)]).astype(np.float32) / np.float32(np.sqrt(SEQ))
    out["c_dft_s"] = out["c_dft_s"].astype(np.float32)
    grid_w, axis = 64, HD // 2
    inv = (np.float32(10000.0) ** (-np.arange(0, axis, 2, dtype=np.float32) / np.float32(axis))).astype(np.float32)
    row = (s // grid_w).astype(np.float32)[:, None] * inv[None, :]
    col = (s % grid_w).astype(np.float32)[:, None] * inv[None, :]
    cos = np.concatenate([np.cos(row), np.cos(row), np.cos(col), np.cos(col)], 1)
    sin = np.concatenate([-np.sin(row), np.sin(row), -np.sin(col), np.sin(col)], 1)
    out["c_rope"] = np.stack([cos, sin]).astype(np.float32)
    i, j = np.arange(P)[:, None], np.arange(P)[None, :]
    same = lambda w: i // w == j // w
    masks = [
        i == j,
        i <= j,
        i > j,
        np.where(i <= j, 0.0, -BIG),
        np.where(i > j, 0.0, BIG),
        same(16),
        same(32) & ~same(16),
        same(64) & ~same(32),
        ~same(64),
        (i <= j) & same(QC),
        i < j,
        np.ones((P, P)),
        np.broadcast_to(j, (P, P)),
    ]
    out["c_masks"] = np.stack([np.asarray(m, np.float32) for m in masks])
    out["c_tok"] = np.arange(SEQ, dtype=np.float32).reshape(NT, P).T.copy()
    out["c_scan"] = np.broadcast_to((np.arange(SEQ) % QC != 0).astype(np.float32), (P, SEQ)).copy()
    return out


def build(nc, io):
    ctx = ExitStack()
    sems = {}

    REUSED = {
        "h_ln": ("g_EB", 2 * HEADS),
        "h_e": ("g_2", 2 * HEADS),
        "h_dec": ("g_4", 2 * HEADS),
        "h_en": ("g_8", 2 * HEADS),
        "h_ed": ("g_TY0", 2 * HEADS),
        "h_kdev": ("g_TY1", 2 * HEADS),
        "hs_o": ("g_TY2", 2 * HEADS),
        "h_f": ("g_R1", 2 * HEADS),
        "h_cum": ("g_R2", 2 * HEADS),
        "h_q": ("g_R4", 2 * HEADS),
        "h_d": ("g_R8", 2 * HEADS),
        "h_kd": ("g_J0", 2 * HEADS),
        "hs_S": ("g_J1", 2 * HEADS),
        "h_kdT": ("g_row", 2 * HEADS),
        "h_in": ("g_gram", 2 * HEADS),
        "hs_kv": ("g_qk", 2 * HEADS),
        "hs_ope": ("g_NT", 2 * HEADS),
        "xa_sc": ("at_sc", NQ * NT),
        "xa_tr": ("at_tr", NQ * NT),
        "xa_av": ("at_av", NQ),
        "xa_exp": ("at_exp", NQ * NT),
        "xa_pT": ("at_pT", NQ * NT),
        "xa_hi": ("at_hi", NQ),
        "xa_max": ("at_max", NQ * NT),
        "xa_norm": ("at_norm", NQ * NT),
        "xa_lo": ("at_prod", NQ),
        "s_v": ("z_dve", KD),
        "s_new": ("fw_prod", KD),
        "mg_lo": ("rope_done", NT),
        "l2_mul": ("rg_floor", 2 * RB),
        "g_abs": ("lam_abs", 1),
        "g_log": ("lb_diff", 1),
        "l2_var": ("qk_var", 1),
        "s_o": ("z_act", KD),
        "mg_hi": ("fw_hi", KD),
        "l2_sq": ("qkT_act", 3 * NT),
        "l2_std": ("qk_std", 1),
        "g_act": ("lam_exp", 1),
        "g_ecum": ("lb_sig", 1),
        "s_ws": ("z_done", GROUPS * NT),
        "s_ope": ("y_done", KD),
        "s_ds": ("fw_done", KD),
        "l2_ss": ("par_T", 3),
        "l2_bc": ("qkT_done", 3 * NT),
        "g_cum": ("gate_done", 4 * RB),
        "router_in": ("par_in", 192),
        "last_in": ("par_in", 272),
        "h_saved": ("masks_in", 32),
        "picked2": ("masks_in", 48),
        "late_in": ("dft_in", 48),
        "picked3": ("dft_in", 128),
        "final_in": ("rope_in", 16),
        "picked0": ("rope_in", 48),
        "mem_in": ("gain_in", 32),
        "picked1": ("gain_in", 48),
        "hnT_act": ("rg_tanh", 2 * RB),
        "rt_pe": ("ab_done", 1),
        "hnT_pe": ("g_kvT", 2 * HEADS),
        "rt_taken": ("g_ready", 1),
        "rt_exp": ("l2_inv", 1),
        "rt_act": ("ab_act", 1),
        "summed": ("g_kv", 2 * HEADS),
        "e_in0": ("gates_in0", 64),
        "e_in1": ("gates_in1", 64),
        "e_in2": ("gates_in2", 64),
        "e_in3": ("gates_in3", 64),
    }

    def after(name, n):
        return sem(name), (REUSED[name][1] + n if name in REUSED else n)

    def sem(name):
        if name in REUSED:
            name = REUSED[name][0]
        if name not in sems:
            sems[name] = ctx.enter_context(nc.semaphore(name))
        return sems[name]

    BASE = 16512
    cursor = [BASE]

    def place(name, shape, dtype=F32):
        n = int(np.prod(shape[1:])) * 4
        t = nc.alloc_sbuf_tensor_at(name, shape, dtype, offset=cursor[0])
        cursor[0] += (n + 31) // 32 * 32
        return t

    raw = [place(f"raw{s}", [P, 4, 512]) for s in range(RAW)]
    w_hi, w_lo = [], []
    for s in range(SPL):
        w_hi.append(place(f"w_hi{s}", [P, 4, 512], F32R))
        w_lo.append(place(f"w_lo{s}", [P, 4, 512], F32R))
    REG = 16384
    regions = cursor[0]
    cursor[0] += 8 * REG

    def view(name, region, shape, dtype=F32, at=0):
        return nc.alloc_sbuf_tensor_at(name, shape, dtype, offset=regions + region * REG + at)

    masks = place("masks", [P, 13, P])
    ident, m_le, m_gt, m_addT, m_addS = (masks[:, k] for k in range(5))
    m_level = [masks[:, k] for k in (5, 6, 7, 8)]
    m_hgrn, m_before, ones, iota = (masks[:, k] for k in (9, 10, 11, 12))
    rope_at = cursor[0]
    rope = place("rope", [P, 2, NT, HD])
    par = place("par", [P, 104 + 128 + 96])
    PAR1, PAR2 = 104, 104 + 128
    small = place("small", [P, 784])
    mark_a = place("mark_a", [P, 2])
    mark_d = place("mark_d", [P, 2])
    tokid = place("tokid", [P, NT])
    assert cursor[0] <= 229344, cursor[0]

    psum = [ctx.enter_context(nc.psum_tensor(f"bank{b}", [P, 512], F32)) for b in range(8)]

    def dram(name, shape):
        return nc.dram_tensor(name, shape, F32, kind="Internal").ap()

    h_dram = dram("h_dram", [SEQ, D])
    hn_dram = dram("hn_dram", [SEQ, D])
    y_dram = dram("y_dram", [BLOCKS * BLK, D])

    units, panels = [], []
    split_of = []

    def unit(src, split=True):
        u = dict(src=src, split=len(split_of) if split else None, n=len(units))
        if split:
            split_of.append(u["n"])
        units.append(u)
        return u

    done_total = [0]
    evac_total = {"A": 0, "D": 0}
    used_total = [0]

    def panel(srcs, evac, nj=4):
        us = [unit(s) for s in srcs]
        for u in us[:-1]:
            used_total[0] += 1
            u["free"] = ("unit_used", used_total[0])
        p = dict(units=[u["split"] for u in us], evac=evac, nj=nj, done=done_total[0], at=evac_total[evac])
        done_total[0] += nj
        evac_total[evac] += nj
        us[-1]["free"] = ("panel_done", done_total[0])
        panels.append(p)
        return len(panels) - 1

    def wcol(w, c0, k0=0, rows=D):
        return [w[k:k + 512, c0:c0 + 512].rearrange("(k p) n -> p k n", p=P) for k in range(k0, k0 + rows, 512)]

    even_in, even_out = io["even_w_in"][0], io["even_w_out"][0]
    odd_in, odd_out = io["odd_w_in"][0], io["odd_w_out"][0]
    w2 = io["w_in_2"][0]
    AB = 3 * HEADS * HD
    C2 = [AB + 2 * HEADS + D * k for k in range(7)]
    pn = {}
    pn["f_in"] = [panel(wcol(even_in, c), "A") for c in (0, 512)]
    pn["f_gate"] = [panel(wcol(even_in, D + c), "A") for c in (0, 512)]
    pn["qkv"] = [panel(wcol(even_in, 2 * D + c), "A") for c in (0, 512, 1024)]
    pn["a_gate"] = [panel(wcol(even_in, 2 * D + 1536 + c), "A") for c in (0, 512)]
    pn["even_out"] = [panel(wcol(even_out, c, rows=2 * D), "D") for c in (0, 512)]
    pn["xr"] = [panel(wcol(odd_in, c), "D") for c in range(0, RNN, 512)]
    pn["r_gate"] = [panel(wcol(odd_in, RNN + c), "A") for c in range(0, RNN, 512)]
    gate_units = []
    for b in range(RB // 4):
        srcs = [io[w][0][:, 4 * b:4 * b + 4].rearrange("d b c e -> c d b e") for w in ("gate_a_w", "gate_x_w")]
        u = unit(srcs, split=False)
        u["free"] = ("gate_done", 16 * (b + 1))
        gate_units.append(u)
    pn["odd_out"] = [panel(wcol(odd_out, c, rows=RNN), "D") for c in (0, 512)]
    pn["qkv2"] = [panel(wcol(w2, c), "D") for c in range(0, AB, 512)]
    pn["og_a"] = [panel(wcol(w2, C2[0] + c), "A") for c in (0, 512)]
    pn["gate_a"] = [panel(wcol(w2, C2[5] + c), "A") for c in (0, 512)]
    pn["br_a"] = [panel(wcol(io["w_branch_a_2"][0], c), "D") for c in (0, 512)]
    pn["f"] = [panel(wcol(w2, C2[1] + c), "A") for c in (0, 512)]
    pn["q"] = [panel(wcol(w2, C2[2] + c), "A") for c in (0, 512)]
    pn["i"] = [panel(wcol(w2, C2[3] + c), "A") for c in (0, 512)]
    pn["og_b"] = [panel(wcol(w2, C2[4] + c), "A") for c in (0, 512)]
    pn["gate_b"] = [panel(wcol(w2, C2[6] + c), "A") for c in (0, 512)]
    pn["br_b"] = [panel(wcol(io["w_branch_b_2"][0], c), "D") for c in (0, 512)]
    pn["mix_out"] = [panel(wcol(io["w_out_2"][0], c), "D") for c in (0, 512)]
    pn["xq"] = [panel(wcol(io["xattn_wq_2"][0], c), "A") for c in (0, 512)]
    pn["xk"] = [panel(wcol(io["xattn_wkv_2"][0], c), "A") for c in (0, 512)]
    pn["xv"] = [panel(wcol(io["xattn_wkv_2"][0], D + c), "A", nj=MEM // P) for c in (0, 512)]
    pn["xo"] = [panel(wcol(io["xattn_wo_2"][0], c), "D") for c in (0, 512)]

    resid = view("resid", 0, [P, NT, D])
    hT_hi, hT_lo = view("hT_hi", 1, [P, KD, SEQ], F32R), view("hT_lo", 2, [P, KD, SEQ], F32R)
    xs = view("xs", 3, [P, NT, D])
    prow = view("prow", 4, [P, 3, P])
    finT = view("finT", 3, [P, KD, SEQ])
    zz = view("zz", 4, [P, NT, GROUPS, 2 * GROUP])
    dft_s = view("dft_s", 6, [P, 2, NT, SEQ])
    four_w = view("four_w", 7, [P, KD, GROUP])
    dft_c = view("dft_c", 7, [P, 2, 2 * GROUP], at=8192)
    ymixT = view("ymixT", 3, [P, KD, SEQ])
    fgate = view("fgate", 4, [P, KD, SEQ])
    mixf_hi, mixf_lo = view("mixf_hi", 5, [P, KD, SEQ], F32R), view("mixf_lo", 6, [P, KD, SEQ], F32R)
    q_tok, kv_tok = view("q_tok", 3, [P, NT, NQ * HD]), view("kv_tok", 4, [P, NT, 2 * NKV * HD])
    agate = view("agate", 7, [P, NQ, SEQ])
    qkT = view("qkT", 1, [P, NQ + NKV, SEQ])
    rot1 = view("rot1", 4, [P, NQ, HD], at=8192)
    rot2 = view("rot2", 4, [P, NQ, HD], at=12288)
    squares = [view("squares0", 7, [P, 32, HD]), view("squares1", 4, [P, 8, HD], at=8192)]
    pT = [view("pT0", 4, [P, NT, SEQ], at=8192), view("pT1", 2, [P, NT, SEQ], at=4096)]
    probs = [view(f"probs{b}", 2, [P, SEQ], at=12288 + 2048 * b) for b in range(2)]
    probs += [nc.alloc_sbuf_tensor_at(f"probs{2 + b}", [P, SEQ], F32, offset=rope_at + 2048 * b) for b in range(2)]
    mixa_hi, mixa_lo = view("mixa_hi", 3, [P, NQ, SEQ], F32R), view("mixa_lo", 7, [P, NQ, SEQ], F32R)
    xc = view("xc", 3, [P, RB, SEQ])
    rgate = view("rgate", 5, [P, RB, SEQ])
    rr = view("rr", 1, [P, 8, SEQ])
    ri = view("ri", 2, [P, 8, SEQ])
    rt = view("rt", 7, [P, 8, SEQ])
    rp_hi, rp_lo = view("rp_hi", 3, [P, RB, SEQ], F32R), view("rp_lo", 5, [P, RB, SEQ], F32R)

    final_gain = view("final_gain", 1, [P, D])
    qkvT = view("qkvT", 3, [P, 3 * HEADS, SEQ])
    w_ab = view("w_ab", 7, [P, KD, 2 * HEADS])
    wab_hi = view("wab_hi", 7, [P, KD, 2 * HEADS], F32R, at=1024)
    wab_lo = view("wab_lo", 7, [P, KD, 2 * HEADS], F32R, at=2048)
    sq = view("sq", 6, [P, 2 * HEADS, SEQ])
    gs = [[view(f"gs{e}_{k}", 0, [P, 2, P], at=8192 * e + 1024 * k) for k in range(8)] for e in range(2)]
    nm16 = [view(f"nm16_{e}", 0, [P, 2, 2, P], at=8192 * e + 3072) for e in range(2)]
    nm2 = [view(f"nm2_{e}", 0, [P, 2, 2, P], at=8192 * e + 5120) for e in range(2)]
    u_tok = view("u_tok", 6, [P, NT, HEADS, P])
    intraT = view("intraT", 7, [P, HEADS, NT, P])
    gstate = [view(f"gstate{b}", 0, [P, HEADS, P], at=4096 * b) for b in range(2)]
    vnew = view("vnew", 0, [P, HEADS, P], at=8192)
    og = view("og", 3, [P, NT, D])
    y_hi, y_lo = view("y_hi", 4, [P, KD, SEQ], F32R), view("y_lo", 5, [P, KD, SEQ], F32R)
    osq = {"a": view("osq_a", 0, [P, HEADS, P]), "b": view("osq_b", 6, [P, HEADS, P])}
    merged = view("merged", 7, [P, KD, SEQ])
    gate_b = view("gate_b", 6, [P, KD, SEQ])
    mg_hi, mg_lo = view("mg_hi", 3, [P, KD, SEQ], F32R), view("mg_lo", 4, [P, KD, SEQ], F32R)
    forget = view("forget", 0, [P, HEADS, SEQ])
    hqT = view("hqT", 3, [P, HEADS, SEQ])
    hv = view("hv", 4, [P, NT, D])
    hexp = view("hexp", 5, [P, HEADS, SEQ])
    hcum = view("hcum", 6, [P, HEADS, SEQ])
    hkd = view("hkd", 6, [P, HEADS, NT, P])
    hintra = view("hintra", 0, [P, NT, HEADS, P])
    hstate = [view(f"hstate{b}", 5, [P, HEADS, P], at=4096 * b) for b in range(3)]
    mem_tok, mem_xs = view("mem_tok", 5, [P, MEM // P, D]), view("mem_xs", 5, [P, MEM // P, D], at=8192)
    memT_hi, memT_lo = view("memT_hi", 6, [P, KD, MEM], F32R), view("memT_lo", 6, [P, KD, MEM], F32R, at=8192)
    xqT, xkT = view("xqT", 3, [P, KD, SEQ]), view("xkT", 4, [P, KD, MEM])
    xv = view("xv", 4, [P, MEM // P, D], at=8192)
    xpT = [view(f"xpT{b}", 7, [P, MEM // P, SEQ], at=4096 * b) for b in range(2)]
    xprobs = [view(f"xprobs{b}", 7, [P, MEM], at=8192 + 1024 * b) for b in range(2)]
    xo_hi, xo_lo = view("xo_hi", 5, [P, KD, SEQ], F32R), view("xo_lo", 6, [P, KD, SEQ], F32R)
    scan_mask = nc.alloc_sbuf_tensor_at("scan_mask", [P, SEQ], F32, offset=rope_at)
    out_norm = nc.alloc_sbuf_tensor_at("out_norm", [P, 2, HD], F32, offset=rope_at + 2048)
    zeros = nc.alloc_sbuf_tensor_at("zeros", [P, P], F32, offset=rope_at + 3200)
    gdn_par = nc.alloc_sbuf_tensor_at("gdn_par", [P, 2, HEADS], F32, offset=rope_at + 3072)
    hnT = view("hnT", 4, [P, KD, SEQ])
    ffn_gain = view("ffn_gain", 7, [P, D])
    w_router = view("w_router", 7, [P, KD, NG + NE], at=4096)
    b_router = view("b_router", 7, [P, NG + NE], at=8192)
    at6 = [0]

    def scratch(name, shape, dtype=F32):
        t = view(name, 6, shape, dtype, at=8192 + at6[0])
        at6[0] += (int(np.prod(shape[1:])) * 4 + 31) // 32 * 32
        assert at6[0] <= 8192
        return t

    logits = scratch("logits", [P, NT, NG + NE])
    hot_g = scratch("hot_g", [P, NT, NG])
    chosen = scratch("chosen", [P, NT, EPG])
    hot_e = scratch("hot_e", [P, 2, NT, EPG])
    experts = scratch("experts", [P, 2, NT, NE])
    rank = scratch("rank", [P, NT, NE])
    pick = scratch("pick", [P, 2, NT * NE])
    iota_neg = scratch("iota_neg", [P, EPG])
    over_e = scratch("over_e", [P, OVER * NE])
    over_n = scratch("over_n", [P, OVER])
    per_e = [scratch(f"per_e{k}", [P, NE]) for k in range(4)]
    per_t = [scratch(f"per_t{k}", [P, 2 * NT]) for k in range(8)]
    weight = scratch("weight", [P, 2, NT])
    row_of = scratch("row_of", [P, 2 * NT], I32)
    tok_of = scratch("tok_of", [BLK, BLOCKS + 1], I32)
    over = scratch("over", [P, OVER + 1], I32)
    hot_r = view("hot_r", 5, [P, 2 * NT, BLK])
    hot_b = view("hot_b", 5, [P, 2 * NT, BLOCKS + 1], at=4096)
    eraw = [raw[(len(units) + k) % RAW] for k in range(4)] + [view(f"eraw{k}", 2, [P, 4, 512], at=8192 * k) for k in range(2)]
    e_hi, e_lo = [], []
    for k in range(6):
        if k < 2:
            m = (len(split_of) + k) % SPL
            e_hi.append(w_hi[m])
            e_lo.append(w_lo[m])
        else:
            r = (1, 3, 4, 7)[k - 2]
            e_hi.append(view(f"e_hi{k}", r, [P, 4, 512], F32R))
            e_lo.append(view(f"e_lo{k}", r, [P, 4, 512], F32R, at=8192))
    xg = view("xg", 5, [BLK, D])
    bT_hi, bT_lo = view("bT_hi", 5, [P, KD, BLK], F32R, at=4096), view("bT_lo", 5, [P, KD, BLK], F32R, at=8192)
    silu_g, act_h = view("silu_g", 5, [BLK, FF], at=12288), view("act_h", 5, [BLK, FF], at=14336)
    aT_hi, aT_lo = view("aT_hi", 6, [P, FF // P, BLK], F32R), view("aT_lo", 6, [P, FF // P, BLK], F32R, at=2048)
    y_rows = view("y_rows", 6, [BLK, D], at=4096)
    picked = [view(f"picked{t}", 1 + t // 2, [P, 2, D], at=8192 * (t % 2)) for t in range(NT)]
    last_gain = view("last_gain", 4, [P, D])
    G_EVEN, G_ODD, G_MIX, G_X, G_MEM, CONV_B, LB, LAM = 0, 8, 16, 24, 32, 40, 56, 72
    CONV_W, GATE_AB, GATE_XB, CONV2 = PAR1, PAR1 + 64, PAR1 + 96, PAR2
    SS, RS, DECAY, HALF, LBC, OML, ST, SUMS = 0, 4, 8, 40, 72, 80, 96, 136
    T0, T1, T2, T3 = 200, 232, 264, 296
    ABC, GG, BETA, NBETA, CUM, ECUM, EREST, SB, ELAST, L2, DEC8 = 328, 392, 424, 456, 488, 520, 552, 584, 616, 648, 712

    qk_gain = small[:, ABC:ABC + 2 * HD].rearrange("p (k d) -> p k d", d=HD)

    def col(c, n=1):
        return small[:, c:c + n]

    def pcol(c, n=1):
        return par[:, c:c + n]

    def f32(ap):
        return ap.bitcast(F32)

    class Chain:

        def __init__(self, eng, name):
            self.eng, self.sem, self.n = eng, sem(name), 0

        def __call__(self, ins):
            self.n += 1
            ins.then_inc(self.sem, 1)

        def wait(self):
            self.eng.wait_ge(self.sem, self.n)

        def link(self, ins):
            self(ins)
            self.wait()

    unit_free = {u["split"]: u["free"] for u in units if u["split"] is not None}

    rows_at, norm_at, feat_at = {}, {}, {}
    r = n = f = 0
    for name, tiles, features in (("even", NT, KD), ("odd", NT, KD), ("final", NT, 0), ("mix", NT, KD), ("x", NT, KD),
                                  ("mem", MEM // P, KD), ("ffn", NT, 0), ("last", NT, 0)):
        rows_at[name], norm_at[name], feat_at[name] = r, n, f
        r, n, f = r + tiles, n + 1, f + features

    def together(eng, k):
        eng.wait_ge(sem("act_stage"), k)
        eng.wait_ge(sem("dve_stage"), k)

    block = ctx.enter_context(nc.Block())

    @block.sync
    def _(sp):
        x_rows = io["x"][0].rearrange("(t p) d -> p t d", p=P)
        sp.dma_start(resid[:], x_rows).then_inc(sem("x_in"), 16)
        for u in units:
            n, s = u["n"], u["n"] % RAW
            if n >= RAW:
                old = units[n - RAW]
                if old["split"] is not None:
                    sp.wait_ge(sem("lo_done"), old["split"] + 1)
                else:
                    sp.wait_ge(sem(old["free"][0]), old["free"][1])
            if u["split"] is not None:
                sp.dma_start(raw[s][:], u["src"]).then_inc(sem(f"raw_in{s}"), 16)
            else:
                for g, src in enumerate(u["src"]):
                    for d in range(2):
                        sp.dma_start(raw[s][:, 2 * g + d].rearrange("p (b e) -> p b e", e=P), src[:, d]).then_inc(sem(f"gates_in{gate_units.index(u)}"), 16)

        def expert(e, k):
            if k < 4:
                w = io["expert_w_gate_2" if k < 2 else "expert_w_up_2"][0]
                rows = w[bass.ds(e, 1)].rearrange("a (k p) n -> p (a k) n", p=P)
                return rows[:, 4 * (k % 2):4 * (k % 2) + 4]
            w = io["expert_w_down_2"][0]
            return w[bass.ds(e, 1)].rearrange("a (k p) n -> p (a k) n", p=P)[:, :, 512 * (k - 4):512 * (k - 4) + 512]

        def fetch(b, e, ks, first=False):
            for k in ks:
                if not first:
                    if k < 4:
                        sp.wait_ge(sem("gu_lo"), 4 * b + (k - 3))
                    else:
                        sp.wait_ge(sem("d_lo"), 2 * b + (k - 5))
                sp.dma_start(eraw[k][:], expert(e, k)).then_inc(sem(f"e_in{k}"), 16)

        GU, DN = range(4), (4, 5)
        for k in GU:
            u = units[len(units) - RAW + k]
            sp.wait_ge(sem("lo_done"), u["split"] + 1)
            fetch(0, 0, [k], True)
        together(sp, 20)
        fetch(0, 0, DN, True)
        fetch(1, 1, GU)
        with sp.Fori(1, NE - 1) as e:
            fetch(e + 1, e + 1, GU)
            fetch(e, e, DN)
        fetch(NE - 1, NE - 1, DN)
        together(sp, 23)
        n_over = sp.value_load(over[0:1, OVER:OVER + 1], min_val=0, max_val=OVER)
        with sp.If(n_over > 0):
            with sp.Fori(NE, BLOCKS) as b:
                e = sp.value_load(over[0:1, bass.ds(b - NE, 1)], min_val=0, max_val=NE - 1)
                fetch(b, e, GU)
                fetch(b, e, DN)

    def raw_arrived(eng, n):
        k = sum(1 for u in units[:n + 1] if u["n"] % RAW == n % RAW and u["split"] is not None)
        eng.wait_ge(sem(f"raw_in{n % RAW}"), 16 * k)

    @block.gpsimd
    def _(pool):
        def load(dst, src, name):
            pool.dma_start(dst, src).then_inc(sem(name), 16)

        def rows(r, k, src):
            n = src.shape[0]
            load(prow[r:r + n, k], src, "par_in")

        def vec(a):
            return a.rearrange("(r p) -> r p", p=P)

        rows(G_EVEN, 0, vec(io["even_norm"][0]))
        rows(G_ODD, 0, vec(io["odd_norm"][0]))
        rows(G_MIX, 0, vec(io["norm_mix_w_2"][0]))
        rows(G_X, 0, vec(io["norm_xattn_w_2"][0]))
        rows(G_MEM, 0, vec(io["norm_mem_w_2"][0]))
        rows(CONV_B, 0, vec(io["conv_b"][0]))
        rows(LB, 0, io["hgrn_lb_2"].rearrange("l (r p) -> (l r) p", p=P))
        rows(LAM, 0, io["rglru_lambda"][0].rearrange("l (r p) -> (l r) p", p=P))
        rows(0, 1, io["conv_w"][0].rearrange("l (r p) -> (l r) p", p=P))
        rows(64, 1, io["gate_a_b"][0].rearrange("l r p -> (l r) p"))
        rows(96, 1, io["gate_x_b"][0].rearrange("l r p -> (l r) p"))
        rows(0, 2, io["conv_w_2"][0].rearrange("l (r p) -> (l r) p", p=P))
        load(masks[:], io["c_masks"].rearrange("k p n -> p k n"), "masks_in")
        load(tokid[:], io["c_tok"], "masks_in")
        load(dft_c[:], io["c_dft_c"].rearrange("(k p) n -> p k n", p=P), "dft_in")
        load(dft_s[:], io["c_dft_s"].rearrange("r (t p) n -> p r t n", p=P), "dft_in")
        load(four_w[:], io["fourier_w"][0].rearrange("g (k p) e -> p (g k) e", p=P), "dft_in")
        load(rope[:], io["c_rope"].rearrange("r (t p) n -> p r t n", p=P), "rope_in")
        together(pool, 1)
        load(qk_gain[:, 0], io["q_gain"].to_broadcast([P, HD]), "gain_in")
        load(qk_gain[:, 1], io["k_gain"].to_broadcast([P, HD]), "gain_in")
        together(pool, 7)
        pool.memset(zeros[:], 0.0).then_inc(sem("zeros_set"), 1)
        pool.wait_ge(sem("zeros_set"), 1)
        rows = OVER * BLK // 10
        load(y_dram[NE * BLK:].rearrange("(p r) (k d) -> p (r k) d", r=10, d=P), zeros[0:rows].unsqueeze(1).to_broadcast([rows, 10 * KD, P]), "y_zeroed")
        load(scan_mask[:], io["c_scan"], "late_in")
        load(out_norm[:, 0], io["gdn_out_norm_w_2"].to_broadcast([P, HD]), "late_in")
        load(out_norm[:, 1], io["hgrn_out_norm_w_2"].to_broadcast([P, HD]), "late_in")
        load(gdn_par[:, 0], io["gdn_a_log_2"].to_broadcast([P, HEADS]), "late_in")
        load(gdn_par[:, 1], io["gdn_dt_bias_2"].to_broadcast([P, HEADS]), "late_in")
        together(pool, 9)
        for it in range(2 * RB):
            pool.wait_ge(sem("gate_sig"), 2 * it + 2)
            pool.tensor_tensor(ri[:, it % 8], ri[:, it % 8], xc[:, it // 2], ALU.mult).then_inc(sem("ix"), 1)
        together(pool, 10)
        load(final_gain[:], io["final_norm"].rearrange("(a d) -> a d", a=1).to_broadcast([P, D]), "final_in")
        load(w_ab[:], w2[:, AB:AB + 2 * HEADS].rearrange("(k p) n -> p k n", p=P), "final_in")
        pool.wait_ge(sem("norm_rows"), rows_at["final"] + NT)
        load(h_dram.rearrange("(t p) d -> p t d", p=P), resid[:], "h_saved")
        def part(e, dst, level):
            return pool.tensor_tensor(dst, gs[e][2][:], m_level[level].unsqueeze(1).to_broadcast([P, 2, P]), ALU.mult)

        for h in range(HEADS):
            for e in range(2):
                pool.wait_ge(sem("g_M"), 2 * (2 * h + e) + 2)
                part(e, nm16[e][:, 1], 0).then_inc(sem("g_M16"), 1)
            for e in range(2):
                pool.wait_ge(sem("g_qdec"), 2 * h + e + 1)
                part(e, gs[e][0][:], 1).then_inc(sem("g_M32"), 1)
                part(e, gs[e][1][:], 2).then_inc(sem("g_M64"), 1)
            for e in range(2):
                pool.wait_ge(sem("g_R4pe"), 2 * h + e + 1)
                part(e, nm16[e][:, 0], 3).then_inc(sem("g_M128"), 1)
        together(pool, 18)
        load(resid[:], h_dram.rearrange("(t p) d -> p t d", p=P), "h_back")
        load(mem_tok[:], io["mem_2"][0].rearrange("(t p) d -> p t d", p=P), "mem_in")
        together(pool, 21)
        load(ffn_gain[:], io["norm_ffn_w_2"].to_broadcast([P, D]), "router_in")
        load(w_router[:, :, 0:NG], io["router_group_w_2"][0].rearrange("(k p) n -> p k n", p=P), "router_in")
        load(w_router[:, :, NG:], io["router_expert_w_2"][0].rearrange("(k p) n -> p k n", p=P), "router_in")
        load(b_router[:, 0:NG], io["router_group_b_2"].to_broadcast([P, NG]), "router_in")
        load(b_router[:, NG:], io["router_expert_b_2"].to_broadcast([P, NE]), "router_in")
        pool.wait_ge(sem("norm_rows"), rows_at["ffn"] + NT)
        load(hn_dram.rearrange("(t p) d -> p t d", p=P), xs[:], "hn_saved")

        def gather(b):
            if b:
                pool.wait_ge(sem("x_T"), b)
            pool.indirect_dma_start(out=xg[:], out_offset=None, in_=hn_dram,
                                    in_offset=bass.IndirectOffsetOnAxis(ap=tok_of[:, b:b + 1], axis=0)).then_inc(sem("x_rows"), 16)
        together(pool, 23)
        pool.wait_ge(sem("y_zeroed"), 16)
        pool.wait_ge(sem("hn_saved"), 16)
        for b in range(NE):
            gather(b)
        n_over = pool.value_load(over[0:1, OVER:OVER + 1], min_val=0, max_val=OVER)
        with pool.If(n_over > 0):
            for b in range(NE, BLOCKS):
                gather(b)
            pool.wait_ge(sem("y_saved"), 16 * BLOCKS)
        together(pool, 24)
        pool.wait_ge(sem("y_saved"), 16 * NE)
        load(last_gain[:], io["final_norm_w_2"].rearrange("(a d) -> a d", a=1).to_broadcast([P, D]), "last_in")
        for t in range(NT):
            for a in range(2):
                pool.indirect_dma_start(out=picked[t][:, a], out_offset=None, in_=y_dram,
                                        in_offset=bass.IndirectOffsetOnAxis(ap=row_of[:, a * NT + t:a * NT + t + 1], axis=0)).then_inc(sem(f"picked{t}"), 16)
        out = io["out"][0].rearrange("(t p) d -> p t d", p=P)
        for t in range(NT):
            pool.wait_ge(sem("norm_rows"), rows_at["last"] + t + 1)
            load(out[:, t], resid[:, t], "out_saved")
        pool.wait_ge(sem("out_saved"), 16 * NT)

    @block.tensor
    def _(pe):
        stage_n = [0]

        def stage(wait=True):
            stage_n[0] += 1
            if wait:
                together(pe, stage_n[0])

        def gemm(ps, act_in, feature, ntok=SEQ):
            for p in ps:
                pan = panels[p]
                if p >= 2:
                    old = panels[p - 2]
                    pe.wait_ge(sem("evac_act" if old["evac"] == "A" else "evac_dve"), old["at"] + old["nj"])
                for ui, m in enumerate(pan["units"]):
                    pe.wait_ge(sem("lo_done"), m + 1)
                    last_unit = ui == len(pan["units"]) - 1
                    wh, wl = w_hi[m % SPL], w_lo[m % SPL]
                    for j in range(pan["nj"]):
                        for k in range(4):
                            kk = 4 * ui + k
                            ah, al = act_in(kk)
                            first, last = kk == 0, last_unit and k == 3
                            if feature:
                                js = slice(j * P, j * P + P)
                                pairs = [(wh[:, k, js], ah), (wl[:, k, js], ah), (wh[:, k, js], al)]
                                out = psum[4 * (p % 2) + j][:, 0:ntok]
                            else:
                                js = slice(j * P, j * P + P)
                                pairs = [(ah[:, js], wh[:, k]), (ah[:, js], wl[:, k]), (al[:, js], wh[:, k])]
                                out = psum[4 * (p % 2) + j][:]
                            for x, (st, mv) in enumerate(pairs):
                                mm = pe.matmul(out, st, mv, start=first and x == 0, stop=last and x == 2)
                        if last_unit:
                            mm.then_inc(sem("panel_done"), 1)
                    if not last_unit:
                        mm.then_inc(sem("unit_used"), 1)

        def norm(name, nt=NT):
            for t in range(nt):
                pe.wait_ge(sem("norm_rows"), rows_at[name] + t + 1)
                for f in range(KD):
                    src = mem_xs if name == "mem" else xs
                    tr = pe.transpose(psum[f][:, t * P:t * P + P], src[:, t, f * P:f * P + P], ident)
                    if t == nt - 1:
                        tr.then_inc(sem("norm_T"), 1)

        def hT(k):
            return hT_hi[:, k], hT_lo[:, k]

        pe.wait_ge(sem("masks_in"), 32)
        pe.wait_ge(sem("par_in"), 16 * 12)
        for k, n in enumerate((104, 128, 96)):
            pe.transpose(psum[k][:, 0:n], prow[0:n, k], ident[0:n, 0:n]).then_inc(sem("par_T"), 1)
        stage()
        norm("even")
        pe.wait_ge(sem("norm_lo"), feat_at["even"] + KD)
        gemm(pn["f_in"], hT, True)
        stage()
        pe.wait_ge(sem("dft_in"), 48)
        for i in range(GROUPS * NT):
            g, t = i // NT, i % NT
            if i >= 8:
                pe.wait_ge(sem("z_dve" if i % 2 else "z_act"), (i - 8) // 2 + 1)
            for k in range(2):
                mm = pe.matmul(psum[i % 8][:], finT[:, 2 * g + k, t * P:t * P + P], dft_c[:, k],
                               start=k == 0, stop=k == 1)
            mm.then_inc(sem("z_done"), 1)
        pe.wait_ge(sem("z_act"), 8)
        pe.wait_ge(sem("z_dve"), 8)
        for i in range(KD):
            g, h = i // 2, i % 2
            for t in range(NT):
                for r in range(2):
                    c = r * GROUP + h * P
                    mm = pe.matmul(psum[i][:], zz[:, t, g, c:c + P], dft_s[:, r, t],
                                   start=t == 0 and r == 0, stop=t == NT - 1 and r == 1)
            mm.then_inc(sem("y_done"), 1)
        stage()
        gemm(pn["f_gate"], hT, True)
        old = panels[pn["f_gate"][-1]]
        pe.wait_ge(sem("evac_act"), old["at"] + old["nj"])
        for i in range(KD):
            g, h = i // 2, i % 2
            for k in range(2):
                mm = pe.matmul(psum[i][:], four_w[:, 2 * g + k, h * P:h * P + P], ymixT[:, 2 * g + k],
                               start=k == 0, stop=k == 1)
            mm.then_inc(sem("fw_done"), 1)
        stage()
        gemm(pn["qkv"], hT, False)
        gemm(pn["a_gate"], hT, True)
        stage(wait=False)
        pe.wait_ge(sem("act_stage"), stage_n[0])
        for t in range(NT):
            pe.wait_ge(sem("rope_done"), t + 1)
            for hg in range(3):
                i = 3 * t + hg
                if i >= 8:
                    pe.wait_ge(sem("qkT_act"), i - 7)
                for h in range(4 * hg, min(4 * hg + 4, NQ + NKV)):
                    src = q_tok[:, t, h * HD:h * HD + HD] if h < NQ else kv_tok[:, t, (h - NQ) * HD:(h - NQ + 1) * HD]
                    tr = pe.transpose(psum[i % 8][:, (h % 4) * P:(h % 4) * P + P], src, ident)
                tr.then_inc(sem("qkT_done"), 1)
        stage()
        n_i = NQ * NT

        def scores(i):
            h, t = i // NT, i % NT
            if i >= 4:
                pe.wait_ge(sem("at_exp"), i - 3)
            pe.matmul(psum[i % 4][:], qkT[:, h, t * P:t * P + P], qkT[:, NQ + h // (NQ // NKV)],
                      start=True, stop=True).then_inc(sem("at_sc"), 1)

        def attend(h):
            pe.wait_ge(sem("at_pT"), NT * (h + 1))
            if h >= 2:
                pe.wait_ge(sem("at_prod"), h - 1)
            for t in range(NT):
                c = (NKV + h // (NQ // NKV)) * HD
                mm = pe.matmul(psum[6 + h % 2][:], kv_tok[:, t, c:c + HD], pT[h % 2][:, t],
                               start=t == 0, stop=t == NT - 1)
            mm.then_inc(sem("at_av"), 1)

        for i in range(3):
            scores(i)
        for i in range(n_i):
            if i + 3 < n_i:
                scores(i + 3)
            pe.wait_ge(sem("at_norm"), i + 1)
            if i >= 2:
                pe.wait_ge(sem("at_pT"), i - 1)
            for k in range(NT):
                tr = pe.transpose(psum[4 + i % 2][:, k * P:k * P + P], probs[i % 4][:, k * P:k * P + P], ident)
            tr.then_inc(sem("at_tr"), 1)
            if i % NT == 1 and i >= NT:
                attend(i // NT - 1)
        attend(NQ - 1)
        stage()
        def mix(k):
            if k < KD:
                return mixf_hi[:, k], mixf_lo[:, k]
            return mixa_hi[:, k - KD], mixa_lo[:, k - KD]
        gemm(pn["even_out"], mix, False)
        stage()
        norm("odd")
        pe.wait_ge(sem("norm_lo"), feat_at["odd"] + KD)
        gemm(pn["xr"], hT, True)
        gemm(pn["r_gate"], hT, True)
        stage()
        for it in range(2 * RB):
            blk, d = it // 2, it % 2
            u = gate_units[blk // 4]
            if it % 8 == 0:
                pe.wait_ge(sem(f"gates_in{blk // 4}"), 16 * 4)
            for g in range(2):
                n = 2 * it + g
                if n >= 8:
                    pe.wait_ge(sem("gate_sig"), n - 7)
                pe.matmul(psum[n % 8][:], raw[u["n"] % RAW][:, 2 * g + d, (blk % 4) * P:(blk % 4) * P + P],
                          xc[:, blk], start=True, stop=True).then_inc(sem("gate_done"), 1)
        stage(wait=False)
        pe.wait_ge(sem("gate_sig"), 4 * RB)

        def rnn_out(k):
            pe.wait_ge(sem("rp_lo"), k // 4 + 1)
            return rp_hi[:, k], rp_lo[:, k]
        gemm(pn["odd_out"], rnn_out, False)
        stage()
        norm("mix")
        pe.wait_ge(sem("norm_lo"), feat_at["mix"] + KD)
        gemm(pn["qkv2"], hT, True)
        pe.wait_ge(sem("ab_lo"), 1)
        last = panels[pn["qkv2"][-1]]
        pe.wait_ge(sem("evac_dve"), last["at"] + last["nj"])
        for t in range(NT):
            for k in range(KD):
                ah, al = hT(k)
                ts = slice(t * P, t * P + P)
                for x, (st, mv) in enumerate(((ah[:, ts], wab_hi[:, k]), (ah[:, ts], wab_lo[:, k]), (al[:, ts], wab_hi[:, k]))):
                    mm = pe.matmul(psum[0][:, t * 16:t * 16 + 16], st, mv, start=k == 0 and x == 0, stop=k == KD - 1 and x == 2)
        mm.then_inc(sem("ab_done"), 1)
        stage()
        for f in range(2 * HEADS):
            pe.wait_ge(*after("l2_sq", f // 4 + 1))
            for t in range(NT):
                mm = pe.matmul(psum[2][:, f * NT + t:f * NT + t + 1], sq[:, f, t * P:t * P + P], ones[:, 0:1], start=True, stop=True)
        mm.then_inc(sem("l2_ss"), 1)
        pe.wait_ge(*after("g_log", 1))
        pe.matmul(psum[0][:, 0:32], m_le, col(GG, 32), start=True, stop=True).then_inc(sem("g_cum"), 1)
        pe.matmul(psum[1][:, 0:32], m_gt, col(GG, 32), start=True, stop=True).then_inc(sem("g_cum"), 1)
        pe.wait_ge(sem("l2_inv"), 1)
        for f in range(2 * HEADS):
            if f >= 4:
                pe.wait_ge(*after("l2_mul", f - 3))
            for t in range(NT):
                c = L2 + f * NT + t
                tr = pe.transpose(psum[4 + f % 4][:, t * P:t * P + P], col(c).to_broadcast([P, P]), ident)
            tr.then_inc(sem("l2_bc"), 1)
        pe.wait_ge(*after("l2_mul", 2 * HEADS))
        pe.wait_ge(sem("g_ready"), 1)
        EE = (0, 1)

        def bank(e, b):
            return psum[4 * e + b]

        def two(e, b, at, f, inc=None):
            for c in range(2):
                mm = pe.matmul(bank(e, b)[:, at + c * P:at + c * P + P], *f(c), start=True, stop=True)
            if inc:
                mm.then_inc(sem(inc), 1)

        def two_T(e, b, at, f, inc=None):
            for c in range(2):
                mm = pe.transpose(bank(e, b)[:, at + c * P:at + c * P + P], f(c), ident)
            if inc:
                mm.then_inc(sem(inc), 1)

        for h in range(HEADS):
            def g(e):
                return 2 * h + e
            def tile(f, e, c):
                t = 2 * e + c
                return qkvT[:, f * HEADS + h, t * P:t * P + P]
            for e in EE:
                if h:
                    pe.wait_ge(sem("g_uw"), 2 * (g(e) - 2) + 2)
                two(e, 0, 0, lambda c: (col(GG + (2 * e + c) * HEADS + h).to_broadcast([P, P]), m_le), "g_row")
                two(e, 1, 0, lambda c: (tile(1, e, c), tile(1, e, c)), "g_gram")
                two(e, 2, 0, lambda c: (tile(1, e, c), tile(0, e, c)), "g_qk")
            for e in EE:
                pe.wait_ge(sem("g_M"), 2 * g(e) + 2)
                two_T(e, 3, 0, lambda c: gs[e][2][:, c], "g_NT")
            for e in EE:
                pe.wait_ge(sem("g_N16"), g(e) + 1)
                pe.wait_ge(sem("g_M16"), g(e) + 1)
                two(e, 0, 0, lambda c: (nm16[e][:, 1, c], nm16[e][:, 0, c]))
                two(e, 0, 256, lambda c: (nm16[e][:, 0, c], nm16[e][:, 1, c]), "g_2pe")
            for e in EE:
                pe.wait_ge(sem("g_2"), g(e) + 1)
                two(e, 2, 0, lambda c: (nm2[e][:, 1, c], nm2[e][:, 0, c]))
                two(e, 2, 256, lambda c: (nm2[e][:, 0, c], nm2[e][:, 1, c]), "g_4pe")
                pe.wait_ge(sem("g_R1"), g(e) + 1)
                two(e, 1, 0, lambda c: (nm2[e][:, 1, c], gs[e][7][:, c]), "g_R2pe")
            for e in EE:
                pe.wait_ge(sem("g_4"), g(e) + 1)
                pe.wait_ge(sem("g_R2"), g(e) + 1)
                two(e, 3, 256, lambda c: (nm16[e][:, 0, c], nm16[e][:, 1, c]))
                two(e, 3, 0, lambda c: (nm16[e][:, 1, c], gs[e][7][:, c]), "g_R4pe")
            for e in EE:
                pe.wait_ge(sem("g_8"), g(e) + 1)
                pe.wait_ge(sem("g_R4"), g(e) + 1)
                two(e, 0, 0, lambda c: (nm2[e][:, 0, c], gs[e][7][:, c]), "g_R8pe")
            for lv in range(3):
                off = (gs, gs, nm16)[lv]
                b1, b2 = ((1, 2), (3, 0), (1, 2))[lv]
                for e in EE:
                    o = (gs[e][0], gs[e][1], nm16[e][:, 0])[lv]
                    pe.wait_ge(sem(("g_R8", "g_J0", "g_J1")[lv]), g(e) + 1)
                    pe.wait_ge(sem(("g_M32", "g_M64", "g_M128")[lv]), g(e) + 1)
                    two_T(e, b1, 0, lambda c: gs[e][7][:, c])
                    two(e, b1, 256, lambda c: (o[:, c], gs[e][7][:, c]), f"g_TYpe{lv}")
                for e in EE:
                    pe.wait_ge(sem(f"g_TY{lv}"), g(e) + 1)
                    two(e, b2, 0, lambda c: (nm2[e][:, 0, c], nm2[e][:, 1, c]), f"g_Jpe{lv}")
            for e in EE:
                two_T(e, 3, 0, lambda c: tile(1, e, c))
                two_T(e, 3, 256, lambda c: tile(2, e, c), "g_kvT")
            for e in EE:
                pe.wait_ge(sem("g_J2"), g(e) + 1)
                pe.wait_ge(sem("g_kv"), g(e) + 1)
                two(e, 0, 0, lambda c: (gs[e][7][:, c], nm2[e][:, 1, c]))
                two(e, 0, 256, lambda c: (nm2[e][:, 0, c], gs[e][7][:, c]), "g_uwpe")
        stage()
        for t in range(NT):
            s_in = gstate[t % 2]
            ts = slice(t * P, t * P + P)
            if t:
                for h in range(HEADS):
                    if h % 4 == 0:
                        pe.wait_ge(*after("s_new", 2 * (t - 1) + h // 4 + 1))
                    mm = pe.matmul(psum[h // 4][:, (h % 4) * P:(h % 4) * P + P], qkvT[:, HEADS + h, ts], s_in[:, h],
                                   start=True, stop=True)
                    if h % 4 == 3:
                        mm.then_inc(sem("s_ws"), 1)
            for h in range(HEADS):
                if h % 4 == 0:
                    pe.wait_ge(*after("s_v", 2 * t + h // 4 + 1))
                    if t:
                        pe.wait_ge(*after("s_o", 2 * (t - 1) + h // 4 + 1))
                out = psum[2 + h // 4][:, (h % 4) * P:(h % 4) * P + P]
                if t:
                    pe.matmul(out, qkvT[:, h, ts], s_in[:, h], start=True, stop=False)
                mm = pe.matmul(out, intraT[:, h, t], vnew[:, h], start=t == 0, stop=True)
                if h % 4 == 3:
                    mm.then_inc(sem("s_ope"), 1)
            if t < NT - 1:
                for h in range(HEADS):
                    mm = pe.matmul(psum[4 + h // 4][:, (h % 4) * P:(h % 4) * P + P], qkvT[:, 2 * HEADS + h, ts], vnew[:, h],
                                   start=True, stop=True)
                    if h % 4 == 3:
                        mm.then_inc(sem("s_ds"), 1)

        def branch(b, w_panels):
            last = panels[pn["gate_" + b][-1]]
            pe.wait_ge(sem("evac_act"), last["at"] + last["nj"])
            o = u_tok[:].rearrange("p t h d -> p t (h d)") if b == "a" else hintra[:].rearrange("p t h d -> p t (h d)")
            for t in range(NT):
                pe.wait_ge(sem("y_rows"), t + 1 + (NT if b == "b" else 0))
                for f in range(KD):
                    tr = pe.transpose(psum[f][:, t * P:t * P + P], o[:, t, f * P:f * P + P], ident)
                    if t == NT - 1:
                        tr.then_inc(sem("y_T"), 1)
            pe.wait_ge(sem("y_lo"), KD + (KD if b == "b" else 0))
            gemm(w_panels, lambda k: (y_hi[:, k], y_lo[:, k]), True)

        stage()
        gemm(pn["og_a"], hT, False)
        gemm(pn["gate_a"], hT, True)
        branch("a", pn["br_a"])
        stage()
        gemm(pn["f"], hT, True)
        gemm(pn["q"], hT, True)
        gemm(pn["i"], hT, False)
        last = panels[pn["i"][-1]]
        pe.wait_ge(sem("evac_act"), last["at"] + last["nj"])
        for h in range(HEADS):
            pe.wait_ge(*after("h_kd", h + 1))
            for t in range(NT):
                tr = pe.transpose(psum[h][:, t * P:t * P + P], forget[:, h, t * P:t * P + P], ident)
            tr.then_inc(sem("h_kdT"), 1)
        for h in range(HEADS):
            pe.wait_ge(*after("h_kdev", h + 1))
            for t in range(NT):
                ts = slice(t * P, t * P + P)
                mm = pe.matmul(psum[h][:, ts], hexp[:, h, ts], hqT[:, h, ts], start=True, stop=True)
            mm.then_inc(sem("h_in"), 1)
        stage()
        for t in range(NT):
            for s in range(2):
                for h in range(HEADS):
                    if h % 4 == 0 and t:
                        pe.wait_ge(*after("hs_S", HEADS * (2 * (t - 1) + s) + 4 * (h // 4) + 4))
                    r = slice(s * QC, s * QC + QC)
                    mm = pe.matmul(psum[2 * s + h // 4][:, (h % 4) * P:(h % 4) * P + P], hkd[r, h, t], hv[r, t, h * P:h * P + P],
                                   start=True, stop=True)
                    if h % 4 == 3:
                        mm.then_inc(sem("hs_kv"), 1)
            for h in range(HEADS):
                bk = psum[4 + 2 * (t % 2) + h // 4]
                cs = slice((h % 4) * P, (h % 4) * P + P)
                if h % 4 == 0 and t >= 2:
                    pe.wait_ge(*after("hs_o", 2 * (t - 2) + h // 4 + 1))
                pe.wait_ge(*after("hs_S", HEADS * 2 * t + h + 1))
                for s in range(2):
                    r = slice(s * QC, s * QC + QC)
                    pe.matmul(bk[r, cs], hqT[:, h, t * P + s * QC:t * P + s * QC + QC], hstate[(2 * t + s) % 3][:, h],
                              start=True, stop=False, skip_group_check=True)
                mm = pe.matmul(bk[:, cs], hintra[:, t, h], hv[:, t, h * P:h * P + P], start=False, stop=True,
                               skip_group_check=True)
                if h % 4 == 3:
                    mm.then_inc(sem("hs_ope"), 1)
        stage()
        gemm(pn["og_b"], hT, False)
        gemm(pn["gate_b"], hT, True)
        branch("b", pn["br_b"])
        stage()
        pe.wait_ge(*after("mg_lo", 2))
        gemm(pn["mix_out"], lambda k: (mg_hi[:, k], mg_lo[:, k]), False)
        stage()
        norm("x")
        pe.wait_ge(sem("norm_lo"), feat_at["x"] + KD)
        norm("mem", MEM // P)
        pe.wait_ge(sem("norm_lo"), feat_at["mem"] + KD)
        def memT(k):
            return memT_hi[:, k], memT_lo[:, k]
        gemm(pn["xq"], hT, True)
        gemm(pn["xk"], memT, True, MEM)
        gemm(pn["xv"], memT, False)
        stage()
        n_x = XH * NT

        def xscores(i):
            h, t = i // NT, i % NT
            if i >= 2:
                pe.wait_ge(*after("xa_exp", i - 1))
            for c in range(2):
                mm = pe.matmul(psum[i % 2][:, 0:MEM], xqT[:, 2 * h + c, t * P:t * P + P], xkT[:, 2 * h + c],
                               start=c == 0, stop=c == 1)
            mm.then_inc(sem("xa_sc"), 1)

        def xattend(h):
            pe.wait_ge(*after("xa_pT", NT * (h + 1)))
            if h >= 2:
                pe.wait_ge(*after("xa_lo", 2 * (h - 2) + 2))
            for c in range(2):
                for m in range(MEM // P):
                    mm = pe.matmul(psum[4 + 2 * (h % 2) + c][:], xv[:, m, h * XD + c * P:h * XD + c * P + P], xpT[h % 2][:, m],
                                   start=m == 0, stop=m == MEM // P - 1)
                mm.then_inc(sem("xa_av"), 1)

        xscores(0)
        for i in range(n_x):
            if i + 1 < n_x:
                xscores(i + 1)
            pe.wait_ge(*after("xa_norm", i + 1))
            if i >= 2:
                pe.wait_ge(*after("xa_pT", i - 1))
            for m in range(MEM // P):
                tr = pe.transpose(psum[2 + i % 2][:, m * P:m * P + P], xprobs[i % 2][:, m * P:m * P + P], ident)
            tr.then_inc(sem("xa_tr"), 1)
            if i % NT == 1 and i >= NT:
                xattend(i // NT - 1)
        xattend(XH - 1)
        stage()
        gemm(pn["xo"], lambda k: (xo_hi[:, k], xo_lo[:, k]), False)
        stage()
        for t in range(NT):
            pe.wait_ge(sem("norm_rows"), rows_at["ffn"] + t + 1)
            for f in range(KD):
                tr = pe.transpose(psum[f][:, t * P:t * P + P], xs[:, t, f * P:f * P + P], ident)
                if t == NT - 1:
                    tr.then_inc(sem("hnT_pe"), 1)
        pe.wait_ge(*after("hnT_act", KD))
        pe.wait_ge(*after("router_in", 16 * 5))
        R = NG + NE
        for t in range(NT):
            for k in range(KD):
                mm = pe.matmul(psum[0][:, t * R:t * R + R], hnT[:, k, t * P:t * P + P], w_router[:, k], start=k == 0, stop=k == KD - 1)
        mm.then_inc(sem("rt_pe"), 1)
        pe.wait_ge(*after("rt_taken", 1))
        for t in range(NT):
            n = 0
            for a in range(2):
                for s in range(t + 1):
                    pe.matmul(psum[1][:, t * NE:t * NE + NE], m_before if s == t else ones, experts[:, a, s],
                              start=n == 0, stop=n == 2 * t + 1)
                    n += 1
        for n in range(2 * NT):
            mm = pe.matmul(psum[2][:, 0:NE], ones, experts[:, n // NT, n % NT], start=n == 0, stop=n == 2 * NT - 1)
        mm.then_inc(sem("rt_pe"), 1)
        pe.wait_ge(*after("rt_taken", 2))
        for n in range(2 * NT):
            mm = pe.matmul(psum[3][0:BLK, 0:BLOCKS + 1], hot_r[:, n], hot_b[:, n], start=n == 0, stop=n == 2 * NT - 1)
        mm.then_inc(sem("rt_pe"), 1)
        stage()

        def rows_T(b, first=False):
            pe.wait_ge(sem("x_rows"), 16 * b + 16)
            if not first:
                pe.wait_ge(sem("x_lo"), b)
            for f in range(KD):
                tr = pe.matmul(psum[2][:, f * BLK:f * BLK + BLK], xg[:, f * P:f * P + P], ident[0:BLK, 0:BLK], start=True, stop=True)
            tr.then_inc(sem("x_T"), 1)

        def three(out, ah, al, k_slot, k, first, last):
            pe.matmul(out, ah, e_hi[k_slot][:, k], start=first, stop=False)
            pe.matmul(out, ah, e_lo[k_slot][:, k], start=False, stop=False)
            return pe.matmul(out, al, e_hi[k_slot][:, k], start=False, stop=last)

        def gate_up(b, first=False):
            if not first:
                pe.wait_ge(sem("e_prod"), b)
            for u in range(4):
                if u == 0:
                    pe.wait_ge(sem("x_lo"), b + 1)
                pe.wait_ge(sem("gu_lo"), 4 * b + u + 1)
                for k in range(4):
                    f = 4 * (u % 2) + k
                    mm = three(psum[u // 2][0:BLK], bT_hi[:, f], bT_lo[:, f], u, k, f == 0, f == KD - 1)
                mm.then_inc(sem("gu_used"), 1)

        def acts_T(b, first=False):
            pe.wait_ge(sem("e_prod"), b + 1)
            if not first:
                pe.wait_ge(sem("h_lo"), b)
            for k in range(FF // P):
                tr = pe.matmul(psum[4][:, k * BLK:k * BLK + BLK], act_h[:, k * P:k * P + P], ident[0:BLK, 0:BLK], start=True, stop=True)
            tr.then_inc(sem("h_T"), 1)

        def down(b, first=False):
            pe.wait_ge(sem("h_lo"), b + 1)
            if not first:
                pe.wait_ge(sem("y_out"), 2 * b)
            for u in range(2):
                pe.wait_ge(sem("d_lo"), 2 * b + u + 1)
                for k in range(4):
                    mm = three(psum[5 + u][0:BLK], aT_hi[:, k], aT_lo[:, k], 4 + u, k, k == 0, k == 3)
                mm.then_inc(sem("d_used"), 1)

        rows_T(0, True)
        gate_up(0, True)
        rows_T(1)
        acts_T(0, True)
        gate_up(1)
        rows_T(2)
        down(0, True)
        acts_T(1)
        with pe.Fori(2, NE - 1) as e:
            gate_up(e)
            rows_T(e + 1)
            down(e - 1)
            acts_T(e)
        gate_up(NE - 1)
        down(NE - 2)
        acts_T(NE - 1)
        down(NE - 1)
        n_over = pe.value_load(over[0:1, OVER:OVER + 1], min_val=0, max_val=OVER)
        with pe.If(n_over > 0):
            with pe.Fori(NE, BLOCKS) as b:
                rows_T(b)
                gate_up(b)
                acts_T(b)
                down(b)

    @block.scalar
    def _(act):
        stage_n = [0]
        next_hi = [0]

        def stage(wait=True):
            stage_n[0] += 1
            act.activation(mark_a[0:1, 0:1], mark_a[0:1, 1:2], ACT.Copy).then_inc(sem("act_stage"), 1)
            if wait:
                together(act, stage_n[0])

        def hi_to(m_end):
            while next_hi[0] < min(m_end, len(split_of)):
                m = next_hi[0]
                n = split_of[m]
                raw_arrived(act, n)
                if m >= SPL:
                    act.wait_ge(sem(unit_free[m - SPL][0]), unit_free[m - SPL][1])
                act.activation(w_hi[m % SPL][:], raw[n % RAW][:], ACT.Copy).then_inc(sem("hi_done"), 1)
                next_hi[0] += 1

        def gemm(ps, evac, ahead=SPL):
            for x, p in enumerate(ps):
                m0 = panels[p]["units"][0]
                hi_to(m0 + 2)
                if x and evac:
                    read(ps[x - 1], x - 1, evac)
                hi_to(m0 + len(panels[p]["units"]))
            if ahead:
                hi_to(next_hi[0] + 1)
            if evac:
                read(ps[-1], len(ps) - 1, evac)
            hi_to(panels[ps[-1]]["units"][-1] + 1 + ahead)

        def read(p, x, evac):
            for j in range(panels[p]["nj"]):
                act.wait_ge(sem("panel_done"), panels[p]["done"] + j + 1)
                ins = evac(x, j, psum[4 * (p % 2) + j])
                if panels[p]["evac"] == "A":
                    ins.then_inc(sem("evac_act"), 1)

        def to(dst, func=ACT.Copy, **kw):
            return lambda x, j, bank: act.activation(dst(x, j), bank[:], func, **kw)

        def norm(name, src, g, hi, nt=NT):
            for t in range(nt):
                act.activation((mem_xs if name == "mem" else xs)[:, t], src[:, t], ACT.Square,
                               accum_out=col(SS + t)).then_inc(sem("norm_ss"), 1)
            act.wait_ge(sem("norm_var"), norm_at[name] + 1)
            act.activation(col(RS, nt), col(SS, nt), ACT.Sqrt).then_inc(sem("norm_std"), 1)
            if hi is not None:
                for f in range(KD):
                    act.wait_ge(sem("norm_T"), feat_at[name] + f + 1)
                    act.activation(hi[:, f], psum[f][:, 0:nt * P], ACT.Copy, scale=pcol(g + f)).then_inc(sem("norm_hi"), 1)

        hi_to(2)
        for k, (n, c) in enumerate(((104, 0), (128, PAR1), (96, PAR2))):
            act.wait_ge(sem("par_T"), k + 1)
            act.activation(pcol(c, n), psum[k][:, 0:n], ACT.Copy).then_inc(sem("par_done"), 1)
        act.wait_ge(sem("lam_abs"), 1)
        act.activation(col(T1, 32), col(T0, 32), ACT.Exp, scale=-1.0).then_inc(sem("lam_exp"), 1)
        act.wait_ge(sem("lb_diff"), 1)
        act.activation(col(T3, 8), col(T2, 8), ACT.Sigmoid).then_inc(sem("lb_sig"), 1)
        act.wait_ge(sem("x_in"), 16)
        stage()
        norm("even", resid, G_EVEN, hT_hi)
        gemm(pn["f_in"], to(lambda x, j: finT[:, 4 * x + j]))
        stage()
        for i in range(0, GROUPS * NT, 2):
            act.wait_ge(sem("z_done"), i + 1)
            act.activation(zz[:, i % NT, i // NT], psum[i % 8][:], ACT.Copy).then_inc(sem("z_act"), 1)
        for i in range(0, KD, 2):
            act.wait_ge(sem("y_done"), i + 1)
            act.activation(ymixT[:, i], psum[i][:], ACT.Copy)
        stage()
        gemm(pn["f_gate"], to(lambda x, j: fgate[:, 4 * x + j], ACT.Silu))
        for i in range(KD):
            act.wait_ge(sem("fw_prod"), i + 1)
            act.activation(mixf_hi[:, i], fgate[:, i], ACT.Copy).then_inc(sem("fw_hi"), 1)
        stage()

        def qkv_out(x, j, bank):
            for h in range(4 if x < 2 else NKV):
                n = j * (NQ + NKV) + 4 * x + h
                act.activation(squares[n // 32][:, n % 32], bank[:, h * HD:h * HD + HD], ACT.Square, accum_out=col(ST + n))
            return act.activation(q_tok[:, j, x * 512:x * 512 + 512] if x < 2 else kv_tok[:, j], bank[:], ACT.Copy)
        gemm(pn["qkv"], qkv_out)
        act.wait_ge(sem("qk_var"), 1)
        act.activation(col(ST, 40), col(ST, 40), ACT.Sqrt).then_inc(sem("qk_std"), 1)
        gemm(pn["a_gate"], to(lambda x, j: agate[:, 4 * x + j], ACT.Silu))
        stage(wait=False)
        for i in range(3 * NT):
            act.wait_ge(sem("qkT_done"), i + 1)
            t, hg = i // 3, i % 3
            n = min(4, NQ + NKV - 4 * hg)
            act.activation(qkT[:, 4 * hg:4 * hg + n, t * P:t * P + P],
                           psum[i % 8][:, 0:n * P].rearrange("p (h s) -> p h s", s=P), ACT.Copy).then_inc(sem("qkT_act"), 1)
        stage()
        n_i = NQ * NT

        def evac(i):
            h, t = i // NT, i % NT
            act.wait_ge(sem("at_tr"), i + 1)
            if h >= 2:
                act.wait_ge(sem("at_av"), h - 1)
            act.activation(pT[h % 2][:, :, t * P:t * P + P], psum[4 + i % 2][:].rearrange("p (k s) -> p k s", s=P),
                           ACT.Copy).then_inc(sem("at_pT"), 1)

        def head_hi(h):
            act.wait_ge(sem("at_prod"), h + 1)
            act.activation(mixa_hi[:, h], agate[:, h], ACT.Copy).then_inc(sem("at_hi"), 1)

        for i in range(n_i):
            act.wait_ge(sem("at_max"), i + 1)
            if i >= 4:
                act.wait_ge(sem("at_tr"), i - 3)
            act.activation(probs[i % 4][:], psum[i % 4][:], ACT.Exp, bias=col(T0 + i % 32), scale=HD ** -0.5,
                           accum_out=col(SUMS + i)).then_inc(sem("at_exp"), 1)
            if i >= 2:
                evac(i - 2)
            if i % NT == 0 and i >= 2 * NT:
                head_hi(i // NT - 2)
        evac(n_i - 2)
        evac(n_i - 1)
        head_hi(NQ - 2)
        head_hi(NQ - 1)
        stage()
        gemm(pn["even_out"], None)
        stage()
        norm("odd", resid, G_ODD, hT_hi)

        def conv_base(x, j, bank):
            f = 4 * x + j
            return act.activation(xc[:, f], bank[:], ACT.Identity, scale=pcol(CONV_W + 2 * RB + f),
                                  bias=pcol(CONV_B + f)).then_inc(sem("conv_base"), 1)
        gemm(pn["xr"], conv_base)
        gemm(pn["r_gate"], to(lambda x, j: rgate[:, 4 * x + j], ACT.Silu), ahead=0)
        stage()

        def rnn_hi(k):
            act.wait_ge(sem("rg_prod"), 4 * k + 4)
            act.activation(rp_hi[:, 4 * k:4 * k + 4], rgate[:, 4 * k:4 * k + 4], ACT.Copy).then_inc(sem("rp_hi"), 1)

        for b in range(2 * RB // BATCH):
            its = range(BATCH * b, BATCH * b + BATCH)
            for it in its:
                blk, d = it // 2, it % 2
                for g, dst in enumerate((rr, ri)):
                    act.wait_ge(sem("gate_done"), 2 * it + g + 1)
                    if b >= 2:
                        act.wait_ge(sem("rg_prod"), blk - BATCH + 1)
                    act.activation(dst[:, it % 8], psum[(2 * it + g) % 8][:], ACT.Sigmoid,
                                   bias=pcol((GATE_AB, GATE_XB)[g] + d * RB + blk)).then_inc(sem("gate_sig"), 1)
            for it in its:
                blk, d = it // 2, it % 2
                act.wait_ge(sem("gate_sig"), 2 * it + 1)
                act.activation(rt[:, it % 8], rr[:, it % 8], ACT.Tanh, scale=col(HALF + d * RB + blk)).then_inc(sem("rg_tanh"), 1)
                act.wait_ge(sem("rg_tanh"), it + 1)
                act.activation(rr[:, it % 8], rr[:, it % 8], ACT.Exp, scale=col(DECAY + d * RB + blk)).then_inc(sem("rg_a"), 1)
            if b >= 2 and b % 2 == 0:
                rnn_hi(b // 2 - 1)
            if b == 6:
                hi_to(next_hi[0] + SPL)
            for it in its:
                act.wait_ge(sem("rg_floor"), it + 1)
                act.activation(rt[:, it % 8], rt[:, it % 8], ACT.Sqrt).then_inc(sem("rg_sqrt"), 1)
        rnn_hi(RB // 4 - 1)
        stage(wait=False)
        gemm(pn["odd_out"], None)
        stage()
        norm("final", resid, None, None)
        act.wait_ge(sem("norm_rows"), rows_at["final"] + NT)
        norm("mix", resid, G_MIX, hT_hi)
        act.wait_ge(*after("final_in", 32))
        act.activation(wab_hi[:], w_ab[:], ACT.Copy).then_inc(sem("ab_hi"), 1)

        def silu2(x):
            last = panels[pn["qkv2"][x]]
            act.wait_ge(sem("evac_dve"), last["at"] + last["nj"])
            qs = qkvT[:, 4 * x:4 * x + 4]
            act.activation(qs, qs, ACT.Silu).then_inc(sem("silu2"), 1)

        def conv2_base(x, j, bank):
            if j == 0 and x:
                silu2(x - 1)
            f = 4 * x + j
            return act.activation(qkvT[:, f], bank[:], ACT.Copy, scale=pcol(CONV2 + 72 + f)).then_inc(sem("conv2_base"), 1)
        gemm(pn["qkv2"], conv2_base)
        silu2(5)
        act.wait_ge(sem("ab_done"), 1)
        act.activation(col(ABC, 64), psum[0][:, 0:64], ACT.Copy).then_inc(sem("ab_act"), 1)
        stage()
        act.wait_ge(sem("silu2"), 6)
        for k in range(4):
            act.activation(sq[:, 4 * k:4 * k + 4], qkvT[:, 4 * k:4 * k + 4], ACT.Square).then_inc(sem("l2_sq"), 1)
        ab = col(ABC, 64).rearrange("p (t x) -> p t x", x=2 * HEADS)
        act.wait_ge(*after("late_in", 80))
        act.activation(col(BETA, 32).rearrange("p (t h) -> p t h", h=HEADS), ab[:, :, HEADS:], ACT.Sigmoid).then_inc(sem("g_act"), 1)
        act.activation(col(T3, 8), gdn_par[:, 0], ACT.Exp).then_inc(sem("g_act"), 1)
        act.wait_ge(*after("g_abs", 1))
        act.activation(col(T1, 32), col(T1, 32), ACT.Exp, scale=-1.0).then_inc(sem("g_act"), 1)
        act.wait_ge(*after("l2_var", 1))
        act.activation(col(L2, 64), col(L2, 64), ACT.Sqrt).then_inc(sem("l2_std"), 1)
        act.wait_ge(*after("g_cum", 2))
        act.activation(col(ECUM, 32), psum[0][:, 0:32], ACT.Exp).then_inc(sem("g_ecum"), 1)
        act.activation(col(EREST, 32), psum[1][:, 0:32], ACT.Exp).then_inc(sem("g_ecum"), 1)
        EE = (0, 1)

        def gbank(e, b, at=0, n=256):
            return psum[4 * e + b][:, at:at + n].rearrange("p (x c j) -> p x c j", c=2, j=P) if n == 512 \
                else psum[4 * e + b][:, at:at + n].rearrange("p (c j) -> p c j", j=P)

        for h in range(HEADS):
            def g(e):
                return 2 * h + e
            for e in EE:
                act.wait_ge(sem("g_row"), g(e) + 1)
                act.activation(gs[e][0][:], gbank(e, 0), ACT.Exp).then_inc(sem("g_EB"), 1)
            for e in EE:
                act.wait_ge(sem("g_D"), 2 * g(e) + 2)
                act.activation(gs[e][2][:], gs[e][2][:], ACT.Exp, scale=-1.0).then_inc(sem("g_dec"), 1)
                act.activation(gs[e][1][:], gs[e][1][:], ACT.Exp).then_inc(sem("g_dec"), 1)
            for e in EE:
                act.wait_ge(sem("g_2pe"), g(e) + 1)
                act.activation(nm2[e][:], gbank(e, 0, 0, 512), ACT.Copy).then_inc(sem("g_2"), 1)
            for e in EE:
                act.wait_ge(sem("g_4pe"), g(e) + 1)
                act.wait_ge(sem("g_R1"), g(e) + 1)
                act.activation(nm16[e][:], gbank(e, 2, 0, 512), ACT.Copy).then_inc(sem("g_4"), 1)
            for e in EE:
                act.wait_ge(sem("g_R4"), g(e) + 1)
                act.activation(nm2[e][:, 0], gbank(e, 3, 256), ACT.Copy).then_inc(sem("g_8"), 1)
            for lv in range(3):
                for e in EE:
                    act.wait_ge(sem(f"g_TYpe{lv}"), g(e) + 1)
                    act.activation(nm2[e][:], gbank(e, (1, 3, 1)[lv], 0, 512), ACT.Copy).then_inc(sem(f"g_TY{lv}"), 1)
            for e in EE:
                act.wait_ge(sem("g_uwpe"), g(e) + 1)
                act.activation(u_tok[:, 2 * e:2 * e + 2, h], gbank(e, 0), ACT.Copy).then_inc(sem("g_uw"), 1)
                act.activation(qkvT[:, HEADS + h, 256 * e:256 * e + 256], psum[4 * e][:, 256:512], ACT.Copy).then_inc(sem("g_uw"), 1)
        stage()
        for t in range(NT):
            for hg in range(2):
                act.wait_ge(*after("s_ope", 2 * t + hg + 1))
                act.activation(u_tok[:, t, 4 * hg:4 * hg + 4], psum[2 + hg][:].rearrange("p (h d) -> p h d", d=P),
                               ACT.Copy).then_inc(sem("s_o"), 1)

        def branch(b, w_panels):
            act.wait_ge(sem("o_var"), 1 + (1 if b == "b" else 0))
            act.activation(col(ST, 32), col(ST, 32), ACT.Sqrt).then_inc(sem("o_std"), 1)
            gemm(pn["og_" + b], to(lambda x, j: og[:, j, x * 512:x * 512 + 512], ACT.Silu))
            dst = merged if b == "a" else gate_b
            gemm(pn["gate_" + b], to(lambda x, j: dst[:, 4 * x + j], ACT.Sigmoid))
            for f in range(KD):
                act.wait_ge(sem("y_T"), f + 1 + (KD if b == "b" else 0))
                act.activation(y_hi[:, f], psum[f][:], ACT.Copy).then_inc(sem("y_hi"), 1)
            gemm(w_panels, None)

        stage()
        branch("a", pn["br_a"])
        stage()
        gemm(pn["f"], to(lambda x, j: forget[:, 4 * x + j], ACT.Sigmoid))
        gemm(pn["q"], to(lambda x, j: hqT[:, 4 * x + j], ACT.Copy, scale=HD ** -0.5))
        gemm(pn["i"], to(lambda x, j: hv[:, j, x * 512:x * 512 + 512]))
        H8 = range(HEADS)
        for h in H8:
            act.wait_ge(*after("h_f", h + 1))
            act.activation(hexp[:, h], forget[:, h], ACT.Ln).then_inc(sem("h_ln"), 1)
        for h in H8:
            act.wait_ge(*after("h_cum", h + 1))
            act.activation(hexp[:, h], hcum[:, h], ACT.Exp).then_inc(sem("h_e"), 1)
            act.activation(col(DEC8 + 8 * h, 8), hcum[:, h, QC - 1::QC], ACT.Exp).then_inc(sem("h_dec"), 1)
        for h in H8:
            act.wait_ge(*after("h_q", h + 1))
            act.activation(hexp[:, h], hcum[:, h], ACT.Exp, scale=-1.0).then_inc(sem("h_en"), 1)
        for h in H8:
            act.wait_ge(*after("h_d", h + 1))
            act.activation(hcum[:, h], hcum[:, h], ACT.Exp).then_inc(sem("h_ed"), 1)
        for h in H8:
            act.wait_ge(*after("h_kdT", h + 1))
            act.activation(hkd[:, h], psum[h][:].rearrange("p (t d) -> p t d", d=P), ACT.Copy).then_inc(sem("h_kdev"), 1)
        stage()
        for t in range(NT):
            for hg in range(2):
                act.wait_ge(*after("hs_ope", 2 * t + hg + 1))
                act.activation(hintra[:, t, 4 * hg:4 * hg + 4], psum[4 + 2 * (t % 2) + hg][:].rearrange("p (h d) -> p h d", d=P),
                               ACT.Copy).then_inc(sem("hs_o"), 1)
        stage()
        branch("b", pn["br_b"])
        stage()
        for k in range(2):
            act.activation(mg_hi[:, 4 * k:4 * k + 4], merged[:, 4 * k:4 * k + 4], ACT.Copy).then_inc(sem("mg_hi"), 1)
        gemm(pn["mix_out"], None)
        stage()
        norm("x", resid, G_X, hT_hi)
        act.wait_ge(*after("mem_in", 16))
        norm("mem", mem_tok, G_MEM, memT_hi, MEM // P)
        gemm(pn["xq"], to(lambda x, j: xqT[:, 4 * x + j]))
        gemm(pn["xk"], lambda x, j, bank: act.activation(xkT[:, 4 * x + j], bank[:, 0:MEM], ACT.Copy))
        gemm(pn["xv"], to(lambda x, j: xv[:, j, x * 512:x * 512 + 512]))
        stage()
        n_x = XH * NT

        def xevac(i):
            h, t = i // NT, i % NT
            act.wait_ge(*after("xa_tr", i + 1))
            if h >= 2:
                act.wait_ge(*after("xa_av", 2 * (h - 2) + 2))
            act.activation(xpT[h % 2][:, :, t * P:t * P + P], psum[2 + i % 2][:, 0:MEM].rearrange("p (k s) -> p k s", s=P),
                           ACT.Copy).then_inc(sem("xa_pT"), 1)

        def xhead_hi(h):
            for c in range(2):
                act.wait_ge(*after("xa_av", 2 * h + c + 1))
                act.activation(xo_hi[:, 2 * h + c], psum[4 + 2 * (h % 2) + c][:], ACT.Copy).then_inc(sem("xa_hi"), 1)

        for i in range(n_x):
            act.wait_ge(*after("xa_max", i + 1))
            if i >= 2:
                act.wait_ge(*after("xa_tr", i - 1))
            act.activation(xprobs[i % 2][:], psum[i % 2][:, 0:MEM], ACT.Exp, bias=col(T0 + i), scale=XD ** -0.5,
                           accum_out=col(SUMS + i)).then_inc(sem("xa_exp"), 1)
            if i:
                xevac(i - 1)
            if i % NT == 3 and i >= NT:
                xhead_hi(i // NT - 1)
        xevac(n_x - 1)
        xhead_hi(XH - 1)
        stage()
        gemm(pn["xo"], None)
        def gu_hi(b, us, first=False):
            for u in us:
                act.wait_ge(*after(f"e_in{u}", 16 * b + 16))
                if not first:
                    act.wait_ge(sem("gu_used"), 4 * b + (u - 3))
                act.activation(e_hi[u][:], eraw[u][:], ACT.Copy).then_inc(sem("gu_hi"), 1)

        stage()
        norm("ffn", resid, None, None)
        gu_hi(0, range(3), True)
        for f in range(KD):
            act.wait_ge(*after("hnT_pe", f + 1))
            act.activation(hnT[:, f], psum[f][:], ACT.Copy).then_inc(sem("hnT_act"), 1)
        act.wait_ge(*after("rt_exp", 1))
        act.activation(logits[:, :, 0:NG], logits[:, :, 0:NG], ACT.Exp).then_inc(sem("rt_act"), 1)
        act.wait_ge(*after("rt_exp", 2))
        act.activation(weight[:, 1], weight[:, 1], ACT.Exp).then_inc(sem("rt_act"), 1)
        stage()

        def d_hi(b, u, first=False):
            act.wait_ge(*after(f"e_in{4 + u}", 16 * b + 16))
            if not first:
                act.wait_ge(sem("d_used"), 2 * b + (u - 1))
            act.activation(e_hi[4 + u][:], eraw[4 + u][:], ACT.Copy).then_inc(sem("d_hi"), 1)

        def silu_of_gate(b, first=False):
            act.wait_ge(sem("gu_used"), 4 * b + 2)
            if not first:
                act.wait_ge(sem("e_prod"), b)
            act.activation(silu_g[:], psum[0][0:BLK], ACT.Silu).then_inc(sem("e_silu"), 1)

        def x_hi(b, first=False):
            act.wait_ge(sem("x_T"), b + 1)
            if not first:
                act.wait_ge(sem("gu_used"), 4 * b)
            act.activation(bT_hi[:], psum[2][:].rearrange("p (k r) -> p k r", r=BLK), ACT.Copy).then_inc(sem("x_hi"), 1)

        def h_hi(b, first=False):
            act.wait_ge(sem("h_T"), b + 1)
            if not first:
                act.wait_ge(sem("d_used"), 2 * b)
            act.activation(aT_hi[:], psum[4][:, 0:FF // P * BLK].rearrange("p (k r) -> p k r", r=BLK), ACT.Copy).then_inc(sem("h_hi"), 1)

        def y_half(b, u, first=False):
            act.wait_ge(sem("d_used"), 2 * b + u + 1)
            if not first:
                act.wait_ge(sem("y_saved"), 16 * b)
            act.activation(y_rows[:, 512 * u:512 * u + 512], psum[5 + u][0:BLK], ACT.Copy).then_inc(sem("y_out"), 1)

        def y_save(b):
            act.wait_ge(sem("y_out"), 2 * b + 2)
            act.dma_start(y_dram[bass.ds(b * BLK, BLK)], y_rows[:]).then_inc(sem("y_saved"), 16)

        def step(e, y=True, first=False, ahead=True, last_first=False):
            if ahead:
                gu_hi(e + 1, (0, 1))
            silu_of_gate(e, first)
            if ahead:
                gu_hi(e + 1, (2, 3))
                x_hi(e + 1)
            d_hi(e, 0, first)
            if y:
                y_half(e - 1, 0, last_first)
            d_hi(e, 1, first)
            if y:
                y_half(e - 1, 1, last_first)
            h_hi(e, first)
            if y:
                y_save(e - 1)

        act.wait_ge(sem("hn_saved"), 16)
        gu_hi(0, (3,), True)
        x_hi(0, True)
        step(0, y=False, first=True)
        step(1, last_first=True)
        with act.Fori(2, NE - 1) as e:
            step(e)
        step(NE - 1, ahead=False)
        for u in range(2):
            y_half(NE - 1, u)
        y_save(NE - 1)
        n_over = act.value_load(over[0:1, OVER:OVER + 1], min_val=0, max_val=OVER)
        with act.If(n_over > 0):
            with act.Fori(NE, BLOCKS) as b:
                gu_hi(b, range(4))
                x_hi(b)
                silu_of_gate(b)
                for u in range(2):
                    d_hi(b, u)
                h_hi(b)
                for u in range(2):
                    y_half(b, u)
                y_save(b)
        stage()
        act.wait_ge(*after("summed", NT))
        norm("last", resid, None, None)

    @block.vector
    def _(dve):
        own = Chain(dve, "dve_own")
        stage_n = [0]
        next_lo = [0]

        def stage(wait=True):
            stage_n[0] += 1
            dve.memset(mark_d[0:1, 0:1], 0.0).then_inc(sem("dve_stage"), 1)
            if wait:
                together(dve, stage_n[0])

        def lo_to(m_end):
            while next_lo[0] < min(m_end, len(split_of)):
                m = next_lo[0]
                dve.wait_ge(sem("hi_done"), m + 1)
                dve.tensor_tensor(w_lo[m % SPL][:], raw[split_of[m] % RAW][:], f32(w_hi[m % SPL][:]),
                                  ALU.subtract).then_inc(sem("lo_done"), 1)
                next_lo[0] += 1

        def gemm(ps, evac, ahead=SPL):
            for x, p in enumerate(ps):
                m0 = panels[p]["units"][0]
                lo_to(m0 + 2)
                if x and evac:
                    read(ps[x - 1], x - 1, evac)
                lo_to(m0 + len(panels[p]["units"]))
            if ahead:
                lo_to(next_lo[0] + 1)
            if evac:
                read(ps[-1], len(ps) - 1, evac)
            lo_to(panels[ps[-1]]["units"][-1] + 1 + ahead)

        def read(p, x, evac):
            for j in range(panels[p]["nj"]):
                dve.wait_ge(sem("panel_done"), panels[p]["done"] + j + 1)
                evac(x, j, psum[4 * (p % 2) + j]).then_inc(sem("evac_dve"), 1)

        def add_to(dst):
            def evac(x, j, bank):
                d = dst[:, j, x * 512:x * 512 + 512]
                return dve.tensor_tensor(d, bank[:], d, ALU.add)
            return evac

        def norm(name, src, g, hi, lo, nt=NT, rows=None, gain=None):
            out = rows if rows is not None else (mem_xs if name == "mem" else xs)
            dve.wait_ge(sem("norm_ss"), rows_at[name] + nt)
            dve.tensor_scalar(col(SS, nt), col(SS, nt), 1.0 / D, EPS, ALU.mult, ALU.add).then_inc(sem("norm_var"), 1)
            dve.wait_ge(sem("norm_std"), norm_at[name] + 1)
            own.link(dve.reciprocal(col(RS, nt), col(RS, nt)))
            for t in range(nt):
                if gain is None:
                    ins = dve.tensor_scalar(out[:, t], src[:, t], col(RS + t), None, ALU.mult)
                else:
                    ins = dve.scalar_tensor_tensor(out[:, t], src[:, t], col(RS + t), gain[:], ALU.mult, ALU.mult)
                ins.then_inc(sem("norm_rows"), 1)
            if hi is not None:
                for f in range(KD):
                    dve.wait_ge(sem("norm_hi"), feat_at[name] + f + 1)
                    dve.scalar_tensor_tensor(lo[:, f], psum[f][:, 0:nt * P], pcol(g + f), f32(hi[:, f]),
                                             ALU.mult, ALU.subtract).then_inc(sem("norm_lo"), 1)

        def softplus(z, e, out, tmp, n):
            own.link(dve.tensor_scalar(tmp, e, 2.0, None, ALU.add))
            own.link(dve.reciprocal(tmp, tmp))
            own.link(dve.tensor_tensor(e, e, tmp, ALU.mult))
            own.link(dve.tensor_tensor(tmp, e, e, ALU.mult))
            own.link(dve.tensor_scalar(out, tmp, 1.0 / 17, None, ALU.mult))
            for k in (15, 13, 11, 9, 7, 5, 3):
                own.link(dve.scalar_tensor_tensor(out, out, 1.0 / k, tmp, ALU.add, ALU.mult))
            own.link(dve.scalar_tensor_tensor(out, out, 1.0, e, ALU.add, ALU.mult))
            own.link(dve.tensor_scalar(tmp, z, 0.0, None, ALU.max))
            own.link(dve.scalar_tensor_tensor(out, out, 2.0, tmp, ALU.mult, ALU.add))

        lo_to(2)
        own(dve.memset(mark_d[:], 0.0))
        own(dve.memset(mark_a[:], 0.0))
        own(dve.memset(small[:], 0.0))
        own.wait()
        dve.wait_ge(sem("par_done"), 3)
        dve.scalar_tensor_tensor(col(T0, 32), pcol(LAM, 32), -1.0, pcol(LAM, 32), ALU.mult, ALU.max).then_inc(sem("lam_abs"), 1)
        dve.tensor_tensor(col(T2, 8), pcol(LB, 8), pcol(LB + 8, 8), ALU.subtract).then_inc(sem("lb_diff"), 1)
        dve.wait_ge(sem("lam_exp"), 1)
        own.link(dve.tensor_scalar(col(T0, 32), pcol(LAM, 32), -1.0, None, ALU.mult))
        softplus(col(T0, 32), col(T1, 32), col(DECAY, 32), col(HALF, 32), 32)
        own.link(dve.tensor_scalar(col(HALF, 32), col(DECAY, 32), 4.0, None, ALU.mult))
        own.link(dve.tensor_scalar(col(DECAY, 32), col(DECAY, 32), -8.0, None, ALU.mult))
        dve.wait_ge(sem("lb_sig"), 1)
        own.link(dve.tensor_copy(col(LBC, 8), col(T3, 8)))
        own.link(dve.tensor_scalar(col(OML, 8), col(T3, 8), -1.0, 1.0, ALU.mult, ALU.add))
        dve.wait_ge(sem("x_in"), 16)
        stage()
        norm("even", resid, G_EVEN, hT_hi, hT_lo)
        gemm(pn["f_in"], None)
        stage()
        for i in range(1, GROUPS * NT, 2):
            dve.wait_ge(sem("z_done"), i + 1)
            dve.tensor_copy(zz[:, i % NT, i // NT], psum[i % 8][:]).then_inc(sem("z_dve"), 1)
        for i in range(1, KD, 2):
            dve.wait_ge(sem("y_done"), i + 1)
            dve.tensor_copy(ymixT[:, i], psum[i][:])
        stage()
        gemm(pn["f_gate"], None)
        for i in range(KD):
            dve.wait_ge(sem("fw_done"), i + 1)
            dve.tensor_tensor(fgate[:, i], psum[i][:], fgate[:, i], ALU.mult).then_inc(sem("fw_prod"), 1)
        for i in range(KD):
            dve.wait_ge(sem("fw_hi"), i + 1)
            dve.tensor_tensor(mixf_lo[:, i], fgate[:, i], f32(mixf_hi[:, i]), ALU.subtract)
        stage()
        gemm(pn["qkv"], None)
        last = panels[pn["qkv"][-1]]
        dve.wait_ge(sem("evac_act"), last["at"] + last["nj"])
        dve.tensor_scalar(col(ST, 40), col(ST, 40), 1.0 / HD, EPS, ALU.mult, ALU.add).then_inc(sem("qk_var"), 1)
        parts = [(q_tok, 0, NQ, 0), (kv_tok, NQ, NKV, 1)]
        dve.wait_ge(sem("qk_std"), 1)
        own.link(dve.reciprocal(col(ST, 40), col(ST, 40)))
        dve.wait_ge(sem("gain_in"), 32)
        dve.wait_ge(sem("rope_in"), 16)
        for t in range(NT):
            if t == 2:
                lo_to(next_lo[0] + 2)
            for buf, h0, n, gi in parts:
                x = buf[:, t, 0:n * HD].rearrange("p (h d) -> p h d", d=HD)
                rs = col(ST + t * 10 + h0, n).unsqueeze(2).to_broadcast([P, n, HD])
                own.link(dve.tensor_tensor(x, x, rs, ALU.mult))
                own.link(dve.tensor_tensor(x, x, qk_gain[:, gi:gi + 1].to_broadcast([P, n, HD]), ALU.mult))
                own(dve.tensor_tensor(rot1[:, 0:n], x, rope[:, 0, t:t + 1].to_broadcast([P, n, HD]), ALU.mult))
                for ax in range(4):
                    a, o = ax * 32, (ax ^ 1) * 32
                    own(dve.tensor_tensor(rot2[:, 0:n, a:a + 32], x[:, :, o:o + 32],
                                          rope[:, 1, t:t + 1, a:a + 32].to_broadcast([P, n, 32]), ALU.mult))
                own.wait()
                last = dve.tensor_tensor(x, rot1[:, 0:n], rot2[:, 0:n], ALU.add)
                if gi == 0:
                    own(last)
            last.then_inc(sem("rope_done"), 1)
        gemm(pn["a_gate"], None)
        stage()
        stage()
        n_i = NQ * NT

        def row_max(i):
            dve.wait_ge(sem("at_sc"), i + 1)
            own.link(dve.tensor_reduce(col(T0 + i % 32), psum[i % 4][:], AX.X, ALU.max))
            dve.tensor_scalar(col(T0 + i % 32), col(T0 + i % 32), -HD ** -0.5, None, ALU.mult).then_inc(sem("at_max"), 1)

        def head_product(h):
            dve.wait_ge(sem("at_av"), h + 1)
            dve.tensor_tensor(agate[:, h], psum[6 + h % 2][:], agate[:, h], ALU.mult).then_inc(sem("at_prod"), 1)

        def head_lo(h):
            dve.wait_ge(sem("at_hi"), h + 1)
            dve.tensor_tensor(mixa_lo[:, h], agate[:, h], f32(mixa_hi[:, h]), ALU.subtract)

        row_max(0)
        row_max(1)
        for i in range(n_i):
            if i + 2 < n_i:
                row_max(i + 2)
            dve.wait_ge(sem("at_exp"), i + 1)
            own.link(dve.reciprocal(col(SUMS + i), col(SUMS + i)))
            dve.tensor_scalar(probs[i % 4][:], probs[i % 4][:], col(SUMS + i), None, ALU.mult).then_inc(sem("at_norm"), 1)
            if i % NT == 3 and i >= NT:
                head_product(i // NT - 1)
            if i % NT == 1 and i >= 2 * NT:
                head_lo(i // NT - 2)
        head_product(NQ - 1)
        head_lo(NQ - 2)
        head_lo(NQ - 1)
        stage()
        gemm(pn["even_out"], add_to(resid))
        stage()
        norm("odd", resid, G_ODD, hT_hi, hT_lo)

        def conv(x, j, bank):
            f = 4 * x + j
            dve.wait_ge(sem("conv_base"), f + 1)
            def tap(n, dst, src):
                return dve.scalar_tensor_tensor(xc[:, f, dst], bank[:, src], pcol(CONV_W + n * RB + f), xc[:, f, dst],
                                                ALU.mult, ALU.add)
            own.link(tap(0, slice(2, SEQ), slice(0, SEQ - 2)))
            own.link(tap(1, slice(1, SEQ), slice(0, SEQ - 1)))
            return tap(3, slice(0, SEQ - 1), slice(1, SEQ))
        gemm(pn["xr"], conv)
        gemm(pn["r_gate"], None, ahead=0)
        stage()

        def rnn_lo(k):
            dve.wait_ge(sem("rp_hi"), k + 1)
            dve.tensor_tensor(rp_lo[:, 4 * k:4 * k + 4], rgate[:, 4 * k:4 * k + 4], f32(rp_hi[:, 4 * k:4 * k + 4]),
                              ALU.subtract).then_inc(sem("rp_lo"), 1)

        for b in range(2 * RB // BATCH):
            its = range(BATCH * b, BATCH * b + BATCH)
            for it in its:
                dve.wait_ge(sem("rg_a"), it + 1)
                dve.tensor_scalar(rt[:, it % 8], rt[:, it % 8], 1e-34, None, ALU.max).then_inc(sem("rg_floor"), 1)
            if b >= 2 and b % 2 == 0:
                rnn_lo(b // 2 - 1)
            if b == 6:
                lo_to(next_lo[0] + SPL)
            for it in its:
                a, u, h = rr[:, it % 8], rt[:, it % 8], ri[:, it % 8]
                dve.wait_ge(sem("rg_sqrt"), it + 1)
                own(dve.scalar_tensor_tensor(u, a, 1.0, u, ALU.add, ALU.mult))
                own.wait()
                dve.wait_ge(sem("ix"), it + 1)
                own.link(dve.tensor_tensor(u, u, h, ALU.mult))
                back = slice(None, None, -1) if it % 2 else slice(None)
                own(dve.tensor_tensor_scan(h[:, back], a[:, back], u[:, back], 0.0, ALU.mult, ALU.add))
                if it % 2:
                    own.wait()
                    own.link(dve.tensor_tensor(h, h, ri[:, it % 8 - 1], ALU.add))
                    dve.tensor_tensor(rgate[:, it // 2], rgate[:, it // 2], h, ALU.mult).then_inc(sem("rg_prod"), 1)
        rnn_lo(RB // 4 - 1)
        stage(wait=False)
        gemm(pn["odd_out"], add_to(resid))
        stage()
        dve.wait_ge(*after("final_in", 32))
        norm("final", resid, None, None, None, rows=resid, gain=final_gain)
        dve.wait_ge(sem("norm_rows"), rows_at["final"] + NT)
        norm("mix", resid, G_MIX, hT_hi, hT_lo)
        dve.wait_ge(sem("ab_hi"), 1)
        dve.tensor_tensor(wab_lo[:], w_ab[:], f32(wab_hi[:]), ALU.subtract).then_inc(sem("ab_lo"), 1)

        def conv2(x, j, bank):
            f = 4 * x + j
            dve.wait_ge(sem("conv2_base"), f + 1)
            for back in (1, 2, 3):
                ins = dve.scalar_tensor_tensor(qkvT[:, f, back:SEQ], bank[:, 0:SEQ - back], pcol(CONV2 + (3 - back) * 24 + f),
                                               qkvT[:, f, back:SEQ], ALU.mult, ALU.add)
                if back < 3:
                    own.link(ins)
            return ins
        gemm(pn["qkv2"], conv2)
        dve.wait_ge(*after("h_saved", 16))
        stage()
        dve.wait_ge(*after("late_in", 80))
        dve.wait_ge(sem("ab_act"), 1)
        ab = col(ABC, 64).rearrange("p (t x) -> p t x", x=2 * HEADS)

        def th(c):
            return col(c, 32).rearrange("p (t h) -> p t h", h=HEADS)

        own.link(dve.tensor_tensor(th(T0), ab[:, :, 0:HEADS], gdn_par[:, 1:2].to_broadcast([P, NT, HEADS]), ALU.add))
        dve.scalar_tensor_tensor(col(T1, 32), col(T0, 32), -1.0, col(T0, 32), ALU.mult, ALU.max).then_inc(sem("g_abs"), 1)
        dve.wait_ge(*after("g_act", 3))
        softplus(col(T0, 32), col(T1, 32), col(GG, 32), col(T2, 32), 32)
        own.link(dve.scalar_tensor_tensor(th(GG), th(GG), -1.0, col(T3, 8).unsqueeze(1).to_broadcast([P, NT, HEADS]),
                                          ALU.mult, ALU.mult))
        own(dve.tensor_scalar(col(NBETA, 32), col(BETA, 32), -1.0, None, ALU.mult))
        dve.tensor_copy(col(T0, 1), col(GG, 1)).then_inc(sem("g_log"), 1)
        dve.wait_ge(*after("l2_ss", 1))
        dve.tensor_scalar(col(L2, 64), psum[2][:, 0:64], EPS, None, ALU.add).then_inc(sem("l2_var"), 1)
        dve.wait_ge(*after("l2_std", 1))
        own.link(dve.reciprocal(col(L2, 64), col(L2, 64)))
        dve.tensor_scalar(col(L2, 32), col(L2, 32), HD ** -0.5, None, ALU.mult).then_inc(sem("l2_inv"), 1)
        dve.wait_ge(*after("g_ecum", 2))
        own(dve.tensor_copy(col(CUM, 32), psum[0][:, 0:32]))
        own(dve.tensor_tensor(col(SB, 32), col(BETA, 32), col(ECUM, 32), ALU.mult))
        own.wait()
        for f in range(2 * HEADS):
            dve.wait_ge(*after("l2_bc", f + 1))
            dve.tensor_tensor(qkvT[:, f], psum[4 + f % 4][:], qkvT[:, f], ALU.mult).then_inc(sem("l2_mul"), 1)
        dve.wait_ge(*after("l2_mul", 2 * HEADS))
        dve.tensor_copy(col(T0, 1), col(CUM, 1)).then_inc(sem("g_ready"), 1)
        EE = (0, 1)

        def gbank(e, b, at=0):
            return psum[4 * e + b][:, at:at + 256].rearrange("p (c j) -> p c j", j=P)

        def mask2(m):
            return m.unsqueeze(1).to_broadcast([P, 2, P])

        for h in range(HEADS):
            def g(e):
                return 2 * h + e
            def per_tok(c, e):
                return col(c, 32).rearrange("p (t h) -> p t h", h=HEADS)[:, 2 * e:2 * e + 2, h:h + 1].to_broadcast([P, 2, P])
            def cs(e):
                return slice(256 * e, 256 * e + 256)
            for e in EE:
                dve.wait_ge(sem("g_EB"), g(e) + 1)
                own.link(dve.tensor_tensor(gs[e][7][:], gbank(e, 0), per_tok(CUM, e), ALU.subtract))
                dve.tensor_tensor(gs[e][2][:], gs[e][7][:], mask2(m_addS), ALU.add).then_inc(sem("g_D"), 1)
                dve.tensor_tensor(gs[e][1][:], gs[e][7][:], mask2(m_addT), ALU.add).then_inc(sem("g_D"), 1)
                own(dve.tensor_copy(th(ELAST)[:, 2 * e:2 * e + 2, h:h + 1], gs[e][0][:, :, P - 1:P]))
            for e in EE:
                dve.wait_ge(sem("g_dec"), 2 * g(e) + 2)
                dve.wait_ge(sem("g_gram"), g(e) + 1)
                for c in range(2):
                    dve.scalar_tensor_tensor(gs[e][2][:, c], gbank(e, 1)[:, c], col(NBETA + (2 * e + c) * HEADS + h),
                                             gs[e][2][:, c], ALU.mult, ALU.mult).then_inc(sem("g_M"), 1)
            for e in EE:
                dve.wait_ge(sem("g_qk"), g(e) + 1)
                own(dve.tensor_tensor(intraT[:, h, 2 * e:2 * e + 2], gbank(e, 2), gs[e][1][:], ALU.mult))
                q = qkvT[:, h, cs(e)].rearrange("p (c j) -> p c j", j=P)
                dve.tensor_tensor(q, q, gs[e][0][:], ALU.mult).then_inc(sem("g_qdec"), 1)
            for e in EE:
                dve.wait_ge(sem("g_NT"), g(e) + 1)
                dve.tensor_tensor(nm16[e][:, 0], gbank(e, 3), mask2(m_level[0]), ALU.mult).then_inc(sem("g_N16"), 1)
            for e in EE:
                dve.wait_ge(sem("g_N16"), g(e) + 1)
                dve.tensor_tensor(gs[e][7][:], nm16[e][:, 0], mask2(ident), ALU.add).then_inc(sem("g_R1"), 1)

            def grow(pe_sem, b, name):
                for e in EE:
                    dve.wait_ge(sem(pe_sem), g(e) + 1)
                    dve.tensor_tensor(gs[e][7][:], gbank(e, b), gs[e][7][:], ALU.add).then_inc(sem(name), 1)
            grow("g_R2pe", 1, "g_R2")
            grow("g_R4pe", 3, "g_R4")
            grow("g_R8pe", 0, "g_R8")
            grow("g_Jpe0", 2, "g_J0")
            grow("g_Jpe1", 0, "g_J1")
            grow("g_Jpe2", 2, "g_J2")
            for e in EE:
                dve.wait_ge(sem("g_kvT"), g(e) + 1)
                own(dve.tensor_tensor(nm2[e][:, 0], gbank(e, 3), per_tok(SB, e), ALU.mult))
                vs = qkvT[:, 2 * HEADS + h, cs(e)].rearrange("p (c j) -> p c j", j=P)
                own(dve.tensor_tensor(vs, gbank(e, 3), per_tok(EREST, e), ALU.mult))
                dve.tensor_tensor(nm2[e][:, 1], gbank(e, 3, 256), per_tok(BETA, e), ALU.mult).then_inc(sem("g_kv"), 1)
        stage()
        for t in range(NT):
            s_in, s_out = gstate[t % 2], gstate[(t + 1) % 2]
            for hg in range(2):
                hs = slice(4 * hg, 4 * hg + 4)
                if t:
                    dve.wait_ge(*after("s_ws", 2 * (t - 1) + hg + 1))
                    dve.wait_ge(*after("s_ds", 2 * (t - 1) + hg + 1))
                    dve.tensor_tensor(vnew[:, hs], u_tok[:, t, hs], psum[hg][:].rearrange("p (h d) -> p h d", d=P),
                                      ALU.subtract).then_inc(sem("s_v"), 1)
                else:
                    dve.tensor_copy(vnew[:, hs], u_tok[:, t, hs]).then_inc(sem("s_v"), 1)
            if t < NT - 1:
                if t:
                    own(dve.tensor_tensor(s_out[:], s_in[:], th(ELAST)[:, t].unsqueeze(2).to_broadcast([P, HEADS, P]), ALU.mult))
                    own.wait()
                for hg in range(2):
                    hs = slice(4 * hg, 4 * hg + 4)
                    dve.wait_ge(*after("s_ds", 2 * t + hg + 1))
                    ds = psum[4 + hg][:].rearrange("p (h d) -> p h d", d=P)
                    if t:
                        dve.tensor_tensor(s_out[:, hs], ds, s_out[:, hs], ALU.add).then_inc(sem("s_new"), 1)
                    else:
                        dve.tensor_copy(s_out[:, hs], ds).then_inc(sem("s_new"), 1)

        def branch(b, w_panels):
            o = u_tok if b == "a" else hintra
            for t in range(NT):
                own.link(dve.tensor_tensor(osq[b][:], o[:, t], o[:, t], ALU.mult))
                own.link(dve.tensor_reduce(col(ST + HEADS * t, HEADS), osq[b][:], AX.X, ALU.add))
            dve.tensor_scalar(col(ST, 32), col(ST, 32), 1.0 / HD, EPS, ALU.mult, ALU.add).then_inc(sem("o_var"), 1)
            dve.wait_ge(sem("o_std"), 1 + (1 if b == "b" else 0))
            own.link(dve.reciprocal(col(ST, 32), col(ST, 32)))
            w = out_norm[:, 0 if b == "a" else 1].unsqueeze(1).to_broadcast([P, HEADS, HD])
            for t in range(NT):
                own(dve.tensor_tensor(o[:, t], o[:, t], col(ST + HEADS * t, HEADS).unsqueeze(2).to_broadcast([P, HEADS, HD]), ALU.mult))
            own.wait()
            for t in range(NT):
                own(dve.tensor_tensor(o[:, t], o[:, t], w, ALU.mult))
            own.wait()
            gemm(pn["og_" + b], None)
            gemm(pn["gate_" + b], None)
            last = panels[pn["og_" + b][-1]]
            dve.wait_ge(sem("evac_act"), last["at"] + last["nj"])
            for t in range(NT):
                dve.tensor_tensor(o[:, t], o[:, t], og[:, t].rearrange("p (h d) -> p h d", d=HD), ALU.mult).then_inc(sem("y_rows"), 1)
            for f in range(KD):
                dve.wait_ge(sem("y_hi"), f + 1 + (KD if b == "b" else 0))
                dve.tensor_tensor(y_lo[:, f], psum[f][:], f32(y_hi[:, f]), ALU.subtract).then_inc(sem("y_lo"), 1)
            if b == "a":
                gemm(w_panels, lambda x, j, bank: dve.tensor_tensor(merged[:, 4 * x + j], bank[:], merged[:, 4 * x + j], ALU.mult))
            else:
                def evac(x, j, bank):
                    f = 4 * x + j
                    own.link(dve.tensor_tensor(gate_b[:, f], bank[:], gate_b[:, f], ALU.mult))
                    return dve.tensor_tensor(merged[:, f], merged[:, f], gate_b[:, f], ALU.add)
                gemm(w_panels, evac)

        stage()
        branch("a", pn["br_a"])
        stage()
        gemm(pn["f"], None)
        gemm(pn["q"], None)
        gemm(pn["i"], None)
        H8 = range(HEADS)
        last = panels[pn["q"][-1]]
        dve.wait_ge(sem("evac_act"), last["at"] + last["nj"])
        for h in H8:
            dve.tensor_scalar(forget[:, h], forget[:, h], col(OML + h), col(LBC + h), ALU.mult, ALU.add).then_inc(sem("h_f"), 1)
        for h in H8:
            dve.wait_ge(*after("h_ln", h + 1))
            dve.tensor_tensor_scan(hcum[:, h], scan_mask[:], hexp[:, h], 0.0, ALU.mult, ALU.add).then_inc(sem("h_cum"), 1)
            own(dve.tensor_scalar(forget[:, h], forget[:, h], -1.0, 1.0, ALU.mult, ALU.add))
        for h in H8:
            dve.wait_ge(*after("h_e", h + 1))
            dve.tensor_tensor(hqT[:, h], hqT[:, h], hexp[:, h], ALU.mult).then_inc(sem("h_q"), 1)
        own.wait()
        for h in H8:
            dve.wait_ge(*after("h_en", h + 1))
            dve.wait_ge(*after("h_dec", h + 1))
            own(dve.tensor_tensor(hexp[:, h], forget[:, h], hexp[:, h], ALU.mult))
            cum = hcum[:, h].rearrange("p (c s) -> p c s", s=QC)
            own(dve.tensor_copy(col(T0 + 8 * h, 8), cum[:, :, QC - 1]))
            own.wait()
            dve.tensor_tensor(cum, col(T0 + 8 * h, 8).unsqueeze(2).to_broadcast([P, SEQ // QC, QC]), cum, ALU.subtract).then_inc(sem("h_d"), 1)
        for h in H8:
            dve.wait_ge(*after("h_ed", h + 1))
            dve.tensor_tensor(forget[:, h], forget[:, h], hcum[:, h], ALU.mult).then_inc(sem("h_kd"), 1)
        dve.wait_ge(*after("h_kdT", HEADS))
        for h in H8:
            dve.wait_ge(*after("h_in", h + 1))
            dve.tensor_tensor(hintra[:, :, h], psum[h][:].rearrange("p (t j) -> p t j", j=P),
                              m_hgrn.unsqueeze(1).to_broadcast([P, NT, P]), ALU.mult)
        stage()
        own.link(dve.memset(hstate[0][:], 0.0))
        for t in range(NT):
            for s in range(2):
                n = 2 * t + s
                s_in, s_out = hstate[n % 3], hstate[(n + 1) % 3]
                for h in H8:
                    if h % 4 == 0:
                        dve.wait_ge(*after("hs_kv", 2 * n + h // 4 + 1))
                        if n:
                            dve.wait_ge(*after("hs_S", HEADS * n))
                        if n >= 2:
                            dve.wait_ge(*after("hs_ope", 2 * ((n - 2) // 2) + 2))
                    kv = psum[2 * s + h // 4][:, (h % 4) * P:(h % 4) * P + P]
                    dve.scalar_tensor_tensor(s_out[:, h], s_in[:, h], col(DEC8 + 8 * h + n), kv, ALU.mult, ALU.add).then_inc(sem("hs_S"), 1)
        stage()
        branch("b", pn["br_b"])
        stage()
        for k in range(2):
            dve.wait_ge(*after("mg_hi", k + 1))
            dve.tensor_tensor(mg_lo[:, 4 * k:4 * k + 4], merged[:, 4 * k:4 * k + 4], f32(mg_hi[:, 4 * k:4 * k + 4]),
                              ALU.subtract).then_inc(sem("mg_lo"), 1)
        dve.wait_ge(sem("h_back"), 16)
        gemm(pn["mix_out"], add_to(resid))
        stage()
        norm("x", resid, G_X, hT_hi, hT_lo)
        dve.wait_ge(*after("mem_in", 16))
        norm("mem", mem_tok, G_MEM, memT_hi, memT_lo, MEM // P)
        gemm(pn["xq"], None)
        gemm(pn["xk"], None)
        gemm(pn["xv"], None)
        stage()
        n_x = XH * NT

        def xrow_max(i):
            dve.wait_ge(*after("xa_sc", i + 1))
            own.link(dve.tensor_reduce(col(T0 + i), psum[i % 2][:, 0:MEM], AX.X, ALU.max))
            dve.tensor_scalar(col(T0 + i), col(T0 + i), -XD ** -0.5, None, ALU.mult).then_inc(sem("xa_max"), 1)

        def xhead_lo(h):
            for c in range(2):
                dve.wait_ge(*after("xa_hi", 2 * h + c + 1))
                dve.tensor_tensor(xo_lo[:, 2 * h + c], psum[4 + 2 * (h % 2) + c][:], f32(xo_hi[:, 2 * h + c]),
                                  ALU.subtract).then_inc(sem("xa_lo"), 1)

        xrow_max(0)
        for i in range(n_x):
            if i + 1 < n_x:
                xrow_max(i + 1)
            dve.wait_ge(*after("xa_exp", i + 1))
            own.link(dve.reciprocal(col(SUMS + i), col(SUMS + i)))
            dve.tensor_scalar(xprobs[i % 2][:], xprobs[i % 2][:], col(SUMS + i), None, ALU.mult).then_inc(sem("xa_norm"), 1)
            if i % NT == 3 and i >= NT:
                xhead_lo(i // NT - 1)
        xhead_lo(XH - 1)
        stage()
        gemm(pn["xo"], add_to(resid))
        def gu_lo(b, us):
            for u in us:
                dve.wait_ge(sem("gu_hi"), 4 * b + u + 1)
                dve.tensor_tensor(e_lo[u][:], eraw[u][:], f32(e_hi[u][:]), ALU.subtract).then_inc(sem("gu_lo"), 1)

        stage()
        dve.wait_ge(*after("router_in", 16 * 5))
        norm("ffn", resid, None, None, None, gain=ffn_gain)
        gu_lo(0, range(3))
        own.link(dve.tensor_scalar(iota_neg[:], iota[:, 0:EPG], float(-P), None, ALU.add))
        dve.wait_ge(*after("rt_pe", 1))
        R = NG + NE
        own.link(dve.tensor_tensor(logits[:], psum[0][:, 0:NT * R].rearrange("p (t n) -> p t n", n=R),
                                   b_router[:].unsqueeze(1).to_broadcast([P, NT, R]), ALU.add))

        def bc(ap, n):
            return ap.unsqueeze(2).to_broadcast([P, NT, n])

        def first_max(hot, vals, n, top):
            idx, eq = per_t[7][:, 0:NT], over_e[:, 0:NT * n].rearrange("p (t n) -> p t n", n=n)
            own.link(dve.tensor_reduce(top, vals, AX.X, ALU.max))
            own.link(dve.tensor_tensor(eq, vals, bc(top, n), ALU.is_equal))
            own.link(dve.tensor_tensor(eq, eq, iota_neg[:, 0:n].unsqueeze(1).to_broadcast([P, NT, n]), ALU.mult))
            own.link(dve.tensor_reduce(idx, eq, AX.X, ALU.min))
            own.link(dve.tensor_tensor(hot, iota_neg[:, 0:n].unsqueeze(1).to_broadcast([P, NT, n]), bc(idx, n), ALU.is_equal))

        g_max, v1, v2, g_p = (per_t[k][:, 0:NT] for k in range(4))
        first_max(hot_g[:], logits[:, :, 0:NG], NG, g_max)
        for t in range(NT):
            tmp = over_e[:, 0:NE]
            own.link(dve.tensor_tensor(tmp.rearrange("p (g e) -> p g e", e=EPG), logits[:, t, NG:].rearrange("p (g e) -> p g e", e=EPG),
                                       hot_g[:, t].unsqueeze(2).to_broadcast([P, NG, EPG]), ALU.mult))
            own.link(dve.tensor_reduce(chosen[:, t], tmp.rearrange("p (g e) -> p e g", e=EPG), AX.X, ALU.add))
        dve.tensor_tensor(logits[:, :, 0:NG], logits[:, :, 0:NG], bc(g_max, NG), ALU.subtract).then_inc(sem("rt_exp"), 1)
        first_max(hot_e[:, 0], chosen[:], EPG, v1)
        own.link(dve.scalar_tensor_tensor(chosen[:], hot_e[:, 0], -BIG, chosen[:], ALU.mult, ALU.add))
        first_max(hot_e[:, 1], chosen[:], EPG, v2)
        dve.tensor_tensor(weight[:, 1], v2, v1, ALU.subtract).then_inc(sem("rt_exp"), 1)
        for a in range(2):
            for t in range(NT):
                own(dve.tensor_tensor(experts[:, a, t].rearrange("p (g e) -> p g e", e=EPG),
                                      hot_g[:, t].unsqueeze(2).to_broadcast([P, NG, EPG]),
                                      hot_e[:, a, t].unsqueeze(1).to_broadcast([P, NG, EPG]), ALU.mult))
        own.wait()
        dve.tensor_copy(per_t[6][:, 0:1], experts[:, 1, NT - 1, 0:1]).then_inc(sem("rt_taken"), 1)
        dve.wait_ge(*after("rt_act", 1))
        own.link(dve.tensor_reduce(g_p, logits[:, :, 0:NG], AX.X, ALU.add))
        dve.wait_ge(*after("rt_act", 2))
        own.link(dve.tensor_scalar(v1, weight[:, 1], 1.0, None, ALU.add))
        own.link(dve.tensor_tensor(g_p, g_p, v1, ALU.mult))
        own.link(dve.reciprocal(weight[:, 0], g_p))
        own(dve.tensor_tensor(weight[:, 1], weight[:, 1], weight[:, 0], ALU.mult))
        dve.wait_ge(*after("rt_pe", 2))
        extra, total, start, _ = per_e
        own.link(dve.tensor_scalar(extra[:], psum[2][:, 0:NE], BLK + 0.5, None, ALU.is_gt))
        for k in range(2, NRB):
            own.link(dve.scalar_tensor_tensor(extra[:], psum[2][:, 0:NE], k * BLK + 0.5, extra[:], ALU.is_gt, ALU.add))
        own.link(dve.tensor_tensor_scan(total[:], ones[:, 0:NE], extra[:], 0.0, ALU.mult, ALU.add))
        own(dve.tensor_tensor(start[:], total[:], extra[:], ALU.subtract))
        own(dve.tensor_copy(over[:, OVER:OVER + 1], total[:, NE - 1:NE]))
        tmp = over_e[:, 0:OVER * NE].rearrange("p (i e) -> p i e", e=NE)
        own.link(dve.tensor_tensor(tmp, total[:].unsqueeze(1).to_broadcast([P, OVER, NE]),
                                   iota[:, 0:OVER].unsqueeze(2).to_broadcast([P, OVER, NE]), ALU.is_le))
        own.link(dve.tensor_reduce(over_n[:], tmp, AX.X, ALU.add))
        own.link(dve.tensor_scalar(over[:, 0:OVER], over_n[:], float(NE - 1), None, ALU.min))
        pos, eid, first, further, r = per_t[0:5]
        picks = pick[:].rearrange("p a n -> p (a n)").rearrange("p (n e) -> p n e", e=NE)
        taken = experts[:].rearrange("p a t e -> p (a t) e")
        own.link(dve.tensor_copy(rank[:].rearrange("p t e -> p (t e)"), psum[1][:, 0:NT * NE]))
        own.link(dve.tensor_tensor(pick[:], experts[:].rearrange("p a t e -> p a (t e)"),
                                   rank[:].rearrange("p t e -> p (t e)").unsqueeze(1).to_broadcast([P, 2, NT * NE]), ALU.mult))
        own.link(dve.tensor_reduce(pos[:], picks, AX.X, ALU.add))
        for dst, of in ((eid, iota[:, 0:NE]), (first, start[:])):
            own.link(dve.tensor_tensor(picks, taken, of.unsqueeze(1).to_broadcast([P, 2 * NT, NE]), ALU.mult))
            own.link(dve.tensor_reduce(dst[:], picks, AX.X, ALU.add))
        own.link(dve.tensor_scalar(further[:], pos[:], BLK - 0.5, None, ALU.is_gt))
        for k in range(2, NRB):
            own.link(dve.scalar_tensor_tensor(further[:], pos[:], k * BLK - 0.5, further[:], ALU.is_gt, ALU.add))
        own(dve.scalar_tensor_tensor(r[:], further[:], float(-BLK), pos[:], ALU.mult, ALU.add))
        own.link(dve.tensor_tensor(first[:], first[:], further[:], ALU.add))
        own.link(dve.scalar_tensor_tensor(first[:], first[:], NE - 1.0, eid[:], ALU.add, ALU.subtract))
        own.link(dve.scalar_tensor_tensor(first[:], further[:], 0.5, first[:], ALU.is_gt, ALU.mult))
        own.link(dve.tensor_tensor(first[:], first[:], eid[:], ALU.add))
        own(dve.scalar_tensor_tensor(row_of[:], first[:], float(BLK), r[:], ALU.mult, ALU.add))
        for n in range(2 * NT):
            own(dve.tensor_scalar(hot_r[:, n], iota[:, 0:BLK], r[:, n:n + 1], None, ALU.is_equal))
            own(dve.tensor_scalar(hot_b[:, n], iota[:, 0:BLOCKS + 1], first[:, n:n + 1], tokid[:, n % NT:n % NT + 1], ALU.is_equal, ALU.mult))
        own.wait()
        dve.tensor_copy(per_t[6][:, 0:1], hot_b[:, 0, 0:1]).then_inc(sem("rt_taken"), 1)
        dve.wait_ge(*after("rt_pe", 3))
        own.link(dve.tensor_copy(tok_of[:], psum[3][0:BLK, 0:BLOCKS + 1]))
        stage()

        def d_lo(b):
            for u in range(2):
                dve.wait_ge(sem("d_hi"), 2 * b + u + 1)
                dve.tensor_tensor(e_lo[4 + u][:], eraw[4 + u][:], f32(e_hi[4 + u][:]), ALU.subtract).then_inc(sem("d_lo"), 1)

        def product(b, first=False):
            dve.wait_ge(sem("e_silu"), b + 1)
            dve.wait_ge(sem("gu_used"), 4 * b + 4)
            if not first:
                dve.wait_ge(sem("h_T"), b)
            dve.tensor_tensor(act_h[:], psum[1][0:BLK], silu_g[:], ALU.mult).then_inc(sem("e_prod"), 1)

        def x_lo(b):
            dve.wait_ge(sem("x_hi"), b + 1)
            dve.tensor_tensor(bT_lo[:], psum[2][:].rearrange("p (k r) -> p k r", r=BLK), f32(bT_hi[:]),
                              ALU.subtract).then_inc(sem("x_lo"), 1)

        def h_lo(b):
            dve.wait_ge(sem("h_hi"), b + 1)
            dve.tensor_tensor(aT_lo[:], psum[4][:, 0:FF // P * BLK].rearrange("p (k r) -> p k r", r=BLK), f32(aT_hi[:]),
                              ALU.subtract).then_inc(sem("h_lo"), 1)

        gu_lo(0, (3,))
        x_lo(0)
        gu_lo(1, (0, 1, 2))
        product(0, True)
        gu_lo(1, (3,))
        x_lo(1)
        d_lo(0)
        h_lo(0)
        with dve.Fori(1, NE - 1) as e:
            gu_lo(e + 1, (0, 1, 2))
            product(e)
            gu_lo(e + 1, (3,))
            x_lo(e + 1)
            d_lo(e)
            h_lo(e)
        product(NE - 1)
        d_lo(NE - 1)
        h_lo(NE - 1)
        n_over = dve.value_load(over[0:1, OVER:OVER + 1], min_val=0, max_val=OVER)
        with dve.If(n_over > 0):
            with dve.Fori(NE, BLOCKS) as b:
                gu_lo(b, range(4))
                x_lo(b)
                product(b)
                d_lo(b)
                h_lo(b)
        stage()
        for t in range(NT):
            dve.wait_ge(*after(f"picked{t}", 32))
            own(dve.scalar_tensor_tensor(resid[:, t], picked[t][:, 0], weight[:, 0, t:t + 1], resid[:, t], ALU.mult, ALU.add))
            own.wait()
            dve.scalar_tensor_tensor(resid[:, t], picked[t][:, 1], weight[:, 1, t:t + 1], resid[:, t], ALU.mult, ALU.add).then_inc(sem("summed"), 1)
        dve.wait_ge(*after("last_in", 16))
        norm("last", resid, None, None, None, rows=resid, gain=last_gain)
    ctx.close()


INPUTS = ["x", "even_norm", "even_w_in", "fourier_w", "q_gain", "k_gain", "even_w_out", "odd_norm", "odd_w_in",
          "conv_w", "conv_b", "gate_a_w", "gate_a_b", "gate_x_w", "gate_x_b", "rglru_lambda", "odd_w_out", "final_norm",
          "mem_2", "norm_mix_w_2", "w_in_2", "conv_w_2", "gdn_a_log_2", "gdn_dt_bias_2", "gdn_out_norm_w_2",
          "hgrn_lb_2", "hgrn_out_norm_w_2", "w_branch_a_2", "w_branch_b_2", "w_out_2", "norm_xattn_w_2",
          "norm_mem_w_2", "xattn_wq_2", "xattn_wkv_2", "xattn_wo_2", "norm_ffn_w_2", "router_group_w_2",
          "router_group_b_2", "router_expert_w_2", "router_expert_b_2", "expert_w_gate_2", "expert_w_up_2",
          "expert_w_down_2", "final_norm_w_2"]


def kernel(**inputs):
    from concourse import bacc
    from concourse.bass_utils import run_bass_kernel_spmd

    nc = bacc.Bacc("TRN2", target_bir_lowering=False, num_devices=1)
    arrays = {name: np.ascontiguousarray(inputs[name]) for name in INPUTS}
    arrays.update(constants())
    io = {name: nc.dram_tensor(name, a.shape, mybir.dt.from_np(a.dtype), kind="ExternalInput").ap()
          for name, a in arrays.items()}
    io["out"] = nc.dram_tensor("out", (1, SEQ, D), F32, kind="ExternalOutput").ap()
    build(nc, io)
    result = run_bass_kernel_spmd(nc, [arrays], core_ids=[0])
    return result.results[0]["out"]
```

```python
from contextlib import ExitStack

import numpy as np

import concourse.bass as bass
from concourse import mybir

F32 = mybir.dt.float32
F32R = mybir.dt.float32r
I32 = mybir.dt.int32
U32 = mybir.dt.uint32
ACT = mybir.ActivationFunctionType
ALU = mybir.AluOpType
AX = mybir.AxisListType

P = 128
SEQ = 512
NT = SEQ // P
D = 1024
KD = D // P
HD = 128
EPS = 1e-6
BIG = 1e30

GROUPS, GROUP = 4, 256
NQ, NKV = 8, 2
RNN = 2048
RB = RNN // P
BATCH = 4
HEADS = 8
QC = 64
MEM = 256
XH, XD = 4, 256
NG, EPG = 4, 8
NE = NG * EPG
FF = 512
BLK = 64
NRB = SEQ // BLK
OVER = 2 * SEQ // BLK - 1
BLOCKS = NE + OVER

RAW = 4
SPL = 2
UNIT = 4 * 512


def constants():
    out = {}
    c = np.arange(GROUP)
    ang = 2.0 * np.pi * ((c[:, None] * c[None, :]) % GROUP) / GROUP
    half = GROUP // 2
    out["c_dft_c"] = (np.concatenate([np.cos(ang)[:, :half + 1], np.sin(ang)[:, 1:half]], 1) / np.sqrt(GROUP)).astype(np.float32)
    s = np.arange(SEQ)
    ang = 2.0 * np.pi * ((s[:, None] * s[None, :]) % SEQ) / SEQ
    half = SEQ // 2
    out["c_dft_s"] = (np.concatenate([np.cos(ang)[:, :half + 1], -np.sin(ang)[:, 1:half]], 1) / np.sqrt(SEQ)).astype(np.float32)
    grid_w, axis = 64, HD // 2
    inv = (np.float32(10000.0) ** (-np.arange(0, axis, 2, dtype=np.float32) / np.float32(axis))).astype(np.float32)
    row = (s // grid_w).astype(np.float32)[:, None] * inv[None, :]
    col = (s % grid_w).astype(np.float32)[:, None] * inv[None, :]
    cos = np.concatenate([np.cos(row), np.cos(row), np.cos(col), np.cos(col)], 1)
    sin = np.concatenate([-np.sin(row), np.sin(row), -np.sin(col), np.sin(col)], 1)
    out["c_rope"] = np.stack([cos, sin]).astype(np.float32)
    i, j = np.arange(P)[:, None], np.arange(P)[None, :]
    same = lambda w: i // w == j // w
    masks = [
        i == j,
        i <= j,
        i > j,
        np.where(i <= j, 0.0, -BIG),
        np.where(i > j, 0.0, BIG),
        same(16),
        same(32) & ~same(16),
        same(64) & ~same(32),
        ~same(64),
        (i <= j) & same(QC),
        i < j,
        np.ones((P, P)),
        np.broadcast_to(j, (P, P)),
    ]
    out["c_masks"] = np.stack([np.asarray(m, np.float32) for m in masks])
    out["c_tok"] = np.arange(SEQ, dtype=np.float32).reshape(NT, P).T.copy()
    out["c_scan"] = np.broadcast_to((np.arange(SEQ) % QC != 0).astype(np.float32), (P, SEQ)).copy()
    return out


def build(nc, io):
    ctx = ExitStack()
    sems = {}

    REUSED = {
        "h_ln": ("g_EB", 2 * HEADS),
        "h_e": ("g_2", 2 * HEADS),
        "h_dec": ("g_4", 2 * HEADS),
        "h_en": ("g_8", 2 * HEADS),
        "h_ed": ("g_TY0", 2 * HEADS),
        "h_kdev": ("g_TY1", 2 * HEADS),
        "hs_o": ("g_TY2", 2 * HEADS),
        "h_f": ("g_R1", 2 * HEADS),
        "h_cum": ("g_R2", 2 * HEADS),
        "h_q": ("g_R4", 2 * HEADS),
        "h_d": ("g_R8", 2 * HEADS),
        "h_kd": ("g_J0", 2 * HEADS),
        "hs_S": ("g_J1", 2 * HEADS),
        "h_in": ("g_gram", 2 * HEADS),
        "hs_kv": ("g_qk", 2 * HEADS),
        "hs_ope": ("g_NT", 2 * HEADS),
        "xa_sc": ("at_sc", NQ * NT),
        "xa_tr": ("at_tr", NQ * NT),
        "xa_av": ("at_av", NQ),
        "xa_exp": ("at_exp", NQ * NT),
        "xa_pT": ("at_pT", NQ * NT),
        "xa_hi": ("at_hi", NQ),
        "xa_max": ("at_max", NQ * NT),
        "xa_norm": ("at_norm", NQ * NT),
        "xa_lo": ("at_prod", NQ),
        "s_v": ("z_dve", 2 * KD),
        "s_new": ("fw_prod", KD),
        "mg_lo": ("rope_done", NT),
        "l2_mul": ("rg_floor", 2 * RB // BATCH),
        "g_abs": ("lam_abs", 1),
        "g_log": ("lb_diff", 1),
        "l2_var": ("qk_var", 1),
        "s_o": ("z_act", 2 * KD),
        "mg_hi": ("fw_hi", KD),
        "l2_sq": ("ix", 2 * RB),
        "l2_std": ("qk_std", 1),
        "g_act": ("lam_exp", 1),
        "g_ecum": ("lb_sig", 1),
        "s_ws": ("z_done", GROUPS * NT // 2),
        "s_ope": ("y_done", KD),
        "s_ds": ("fw_done", KD),
        "l2_ss": ("par_T", 4),
        "l2_bc": ("qkT_done", 3 * NT),
        "g_cum": ("gate_done", 4 * RB),
        "router_in": ("h_saved", 16),
        "last_in": ("y_zeroed", 16),
        "picked2": ("h_back", 16),
        "late_in": ("dft_in", 80),
        "picked3": ("dft_in", 160),
        "final_in": ("rope_in", 16),
        "picked0": ("rope_in", 32),
        "mem_in": ("gain_in", 32),
        "picked1": ("gain_in", 48),
        "hnT_act": ("rg_tanh", 2 * RB),
        "rt_pe": ("ab_done", 2),
        "hnT_pe": ("g_kvT", 2 * HEADS),
        "rt_taken": ("g_ready", 1),
        "rt_exp": ("l2_inv", 1),
        "rt_act": ("ab_act", 2),
        "summed": ("g_kv", 2 * HEADS),
        "e_in0": ("gates_in0", 64),
        "e_in1": ("gates_in1", 64),
        "e_in2": ("gates_in2", 64),
        "e_in3": ("gates_in3", 64),
    }

    def after(name, n):
        return sem(name), (REUSED[name][1] + n if name in REUSED else n)

    def sem(name):
        if name in REUSED:
            name = REUSED[name][0]
        if name not in sems:
            sems[name] = ctx.enter_context(nc.semaphore(name))
        return sems[name]

    BASE = 16512
    cursor = [BASE]

    def place(name, shape, dtype=F32):
        n = int(np.prod(shape[1:])) * 4
        t = nc.alloc_sbuf_tensor_at(name, shape, dtype, offset=cursor[0])
        cursor[0] += (n + 31) // 32 * 32
        return t

    raw = [place(f"raw{s}", [P, 4, 512]) for s in range(RAW)]
    w_hi, w_lo = [], []
    for s in range(SPL):
        w_hi.append(place(f"w_hi{s}", [P, 4, 512], F32R))
        w_lo.append(place(f"w_lo{s}", [P, 4, 512], F32R))
    REG = 16384
    regions = cursor[0]
    cursor[0] += 8 * REG

    def view(name, region, shape, dtype=F32, at=0):
        return nc.alloc_sbuf_tensor_at(name, shape, dtype, offset=regions + region * REG + at)

    masks = place("masks", [P, 13, P])
    ident, m_le, m_gt, m_addT, m_addS = (masks[:, k] for k in range(5))
    m_level = [masks[:, k] for k in (5, 6, 7, 8)]
    m_hgrn, m_before, ones, iota = (masks[:, k] for k in (9, 10, 11, 12))
    rope_at = cursor[0]
    rope = place("rope", [P, 2, NT, HD])
    par = place("par", [P, 104 + 128 + 96])
    PAR1, PAR2 = 104, 104 + 128
    small = place("small", [P, 784])
    mark_a = place("mark_a", [P, 2])
    mark_d = place("mark_d", [P, 2])
    tokid = place("tokid", [P, NT])
    assert cursor[0] <= 229344, cursor[0]

    psum = [ctx.enter_context(nc.psum_tensor(f"bank{b}", [P, 512], F32)) for b in range(8)]

    def dram(name, shape):
        return nc.dram_tensor(name, shape, F32, kind="Internal").ap()

    h_dram = dram("h_dram", [SEQ, D])
    hT_dram = nc.dram_tensor("hT_dram", [P, KD, SEQ], F32R, kind="Internal").ap()
    hn_dram = dram("hn_dram", [SEQ, D])
    y_dram = dram("y_dram", [BLOCKS * BLK, D])

    units, panels = [], []
    split_of = []

    def unit(src, split=True):
        u = dict(src=src, split=len(split_of) if split else None, n=len(units))
        if split:
            split_of.append(u["n"])
        units.append(u)
        return u

    done_total = [0]
    evac_total = {"A": 0, "D": 0}
    used_total = [0]

    def panel(srcs, evac, nj=4):
        us = [unit(s) for s in srcs]
        for u in us[:-1]:
            used_total[0] += 1
            u["free"] = ("unit_used", used_total[0])
        p = dict(units=[u["split"] for u in us], evac=evac, nj=nj, done=done_total[0], at=evac_total[evac])
        done_total[0] += nj
        evac_total[evac] += nj
        us[-1]["free"] = ("panel_done", done_total[0])
        panels.append(p)
        return len(panels) - 1

    def wcol(w, c0, k0=0, rows=D):
        return [w[k:k + 512, c0:c0 + 512].rearrange("(k p) n -> p k n", p=P) for k in range(k0, k0 + rows, 512)]

    even_in, even_out = io["even_w_in"][0], io["even_w_out"][0]
    odd_in, odd_out = io["odd_w_in"][0], io["odd_w_out"][0]
    w2 = io["w_in_2"][0]
    AB = 3 * HEADS * HD
    C2 = [AB + 2 * HEADS + D * k for k in range(7)]
    pn = {}
    pn["f_in"] = [panel(wcol(even_in, c), "A") for c in (0, 512)]
    pn["f_gate"] = [panel(wcol(even_in, D + c), "A") for c in (0, 512)]
    pn["qkv"] = [panel(wcol(even_in, 2 * D + c), "A") for c in (0, 512, 1024)]
    pn["a_gate"] = [panel(wcol(even_in, 2 * D + 1536 + c), "A") for c in (0, 512)]
    pn["even_out"] = [panel(wcol(even_out, c, rows=2 * D), "D") for c in (0, 512)]
    pn["xr"] = [panel(wcol(odd_in, c), "D") for c in range(0, RNN, 512)]
    pn["r_gate"] = [panel(wcol(odd_in, RNN + c), "A") for c in range(0, RNN, 512)]
    gate_units = []
    for b in range(RB // 4):
        srcs = [io[w][0][:, 4 * b:4 * b + 4].rearrange("d b c e -> c d b e") for w in ("gate_a_w", "gate_x_w")]
        u = unit(srcs, split=False)
        u["free"] = ("gate_done", 16 * (b + 1))
        gate_units.append(u)
    pn["odd_out"] = [panel(wcol(odd_out, c, rows=RNN), "D") for c in (0, 512)]
    pn["qkv2"] = [panel(wcol(w2, c), "D") for c in range(0, AB, 512)]
    pn["og_a"] = [panel(wcol(w2, C2[0] + c), "A") for c in (0, 512)]
    pn["gate_a"] = [panel(wcol(w2, C2[5] + c), "A") for c in (0, 512)]
    pn["br_a"] = [panel(wcol(io["w_branch_a_2"][0], c), "D") for c in (0, 512)]
    pn["f"] = [panel(wcol(w2, C2[1] + c), "A") for c in (0, 512)]
    pn["q"] = [panel(wcol(w2, C2[2] + c), "A") for c in (0, 512)]
    pn["i"] = [panel(wcol(w2, C2[3] + c), "A") for c in (0, 512)]
    pn["og_b"] = [panel(wcol(w2, C2[4] + c), "A") for c in (0, 512)]
    pn["gate_b"] = [panel(wcol(w2, C2[6] + c), "A") for c in (0, 512)]
    pn["br_b"] = [panel(wcol(io["w_branch_b_2"][0], c), "D") for c in (0, 512)]
    pn["mix_out"] = [panel(wcol(io["w_out_2"][0], c), "D") for c in (0, 512)]
    pn["xk"] = [panel(wcol(io["xattn_wkv_2"][0], c), "A") for c in (0, 512)]
    pn["xv"] = [panel(wcol(io["xattn_wkv_2"][0], D + c), "A", nj=MEM // P) for c in (0, 512)]
    pn["xq"] = [panel(wcol(io["xattn_wq_2"][0], c), "A") for c in (0, 512)]
    pn["xo"] = [panel(wcol(io["xattn_wo_2"][0], c), "D") for c in (0, 512)]

    resid = view("resid", 0, [P, NT, D])
    hT_hi, hT_lo = view("hT_hi", 1, [P, KD, SEQ], F32R), view("hT_lo", 2, [P, KD, SEQ], F32R)
    xs = view("xs", 3, [P, NT, D])
    prow = view("prow", 7, [P, 3, P], at=12288)
    normed = {"even": xs, "odd": view("xs_odd", 4, [P, NT, D]), "final": view("xs_final", 7, [P, NT, D]), "x": xs, "ffn": xs, "last": xs}
    normed["mix"] = normed["final"]
    finT = view("finT", 3, [P, KD, SEQ])
    zz = view("zz", 4, [P, NT, GROUPS, 2, 2, P])
    dft_s = view("dft_s", 6, [P, NT, SEQ])
    four_w = view("four_w", 7, [P, KD, GROUP])
    y_odd = view("y_odd", 6, [P, KD, SEQ // 2 - 1], at=8192)
    dft_c = view("dft_c", 7, [P, 2, GROUP], at=8192)
    HC, HS = GROUP // 2, SEQ // 2
    ymixT = view("ymixT", 3, [P, KD, SEQ])
    fgate = view("fgate", 4, [P, KD, SEQ])
    mixf_hi, mixf_lo = view("mixf_hi", 5, [P, KD, SEQ], F32R), view("mixf_lo", 6, [P, KD, SEQ], F32R)
    q_tok, kv_tok = view("q_tok", 3, [P, NT, NQ * HD]), view("kv_tok", 4, [P, NT, 2 * NKV * HD])
    agate = view("agate", 7, [P, NQ, SEQ])
    qkT = view("qkT", 1, [P, NQ + NKV, SEQ])
    rot1 = view("rot1", 4, [P, NQ, HD], at=8192)
    rot2 = view("rot2", 4, [P, NQ, HD], at=12288)
    squares = [view("squares0", 7, [P, 32, HD]), view("squares1", 4, [P, 8, HD], at=8192)]
    pT = [view("pT0", 4, [P, NT, SEQ], at=8192), view("pT1", 2, [P, NT, SEQ], at=4096)]
    probs = [view(f"probs{b}", 2, [P, SEQ], at=12288 + 2048 * b) for b in range(2)]
    probs += [nc.alloc_sbuf_tensor_at(f"probs{2 + b}", [P, SEQ], F32, offset=rope_at + 2048 * b) for b in range(2)]
    mixa_hi, mixa_lo = view("mixa_hi", 3, [P, NQ, SEQ], F32R), view("mixa_lo", 7, [P, NQ, SEQ], F32R)
    xc = view("xc", 3, [P, RB, SEQ])
    rgate = view("rgate", 5, [P, RB, SEQ])
    rr = view("rr", 1, [P, 8, SEQ])
    ri = view("ri", 2, [P, 8, SEQ])
    rt = view("rt", 7, [P, 8, SEQ])
    rp_hi, rp_lo = view("rp_hi", 3, [P, RB, SEQ], F32R), view("rp_lo", 5, [P, RB, SEQ], F32R)

    final_gain = view("final_gain", 1, [P, D])
    qkvT = view("qkvT", 3, [P, 3 * HEADS, SEQ])
    w_ab = view("w_ab", 0, [P, KD, 2 * HEADS])
    wab_hi = view("wab_hi", 0, [P, KD, 2 * HEADS], F32R, at=1024)
    wab_lo = view("wab_lo", 0, [P, KD, 2 * HEADS], F32R, at=2048)
    ab_rows = view("ab_rows", 0, [2 * HEADS, SEQ], at=4096)
    ab_base, l2_base = (4 * (pn["qkv2"][k] % 2) for k in (-2, -1))
    sq = view("sq", 6, [P, 2 * HEADS, SEQ])
    g_at = [(0, 0), (0, 8192), (2, 0), (2, 8192)]
    gs = [[view(f"gs{e}_{k}", r, [P, 2, P], at=at + 1024 * k) for k in range(8)] for e, (r, at) in enumerate(g_at)]
    nm16 = [view(f"nm16_{e}", r, [P, 2, 2, P], at=at + 3072) for e, (r, at) in enumerate(g_at)]
    nm2 = [view(f"nm2_{e}", r, [P, 2, 2, P], at=at + 5120) for e, (r, at) in enumerate(g_at)]
    u_tok = view("u_tok", 6, [P, NT, HEADS, P])
    intraT = view("intraT", 7, [P, HEADS, NT, P])
    gstate = [view(f"gstate{b}", 0, [P, HEADS, P], at=4096 * b) for b in range(2)]
    vnew = view("vnew", 0, [P, HEADS, P], at=8192)
    og = view("og", 3, [P, NT, D])
    y_hi, y_lo = view("y_hi", 4, [P, KD, SEQ], F32R), view("y_lo", 5, [P, KD, SEQ], F32R)
    osq = {"a": view("osq_a", 0, [P, HEADS, P]), "b": view("osq_b", 6, [P, HEADS, P])}
    merged = view("merged", 7, [P, KD, SEQ])
    gate_b = view("gate_b", 6, [P, KD, SEQ])
    mg_hi, mg_lo = view("mg_hi", 3, [P, KD, SEQ], F32R), view("mg_lo", 1, [P, KD, SEQ], F32R)
    forget = view("forget", 0, [P, HEADS, SEQ])
    hqT = view("hqT", 3, [P, HEADS, SEQ])
    hv = view("hv", 4, [P, NT, D])
    hexp = view("hexp", 5, [P, HEADS, SEQ])
    hcum = view("hcum", 6, [P, HEADS, SEQ])
    hkd = view("hkd", 6, [P, HEADS, NT, P])
    hintra = view("hintra", 0, [P, NT, HEADS, P])
    hstate = [view(f"hstate{b}", 5, [P, HEADS, P], at=4096 * b) for b in range(3)]
    mem_tok, mem_xs = view("mem_tok", 5, [P, MEM // P, D]), view("mem_xs", 5, [P, MEM // P, D], at=8192)
    memT_hi, memT_lo = view("memT_hi", 6, [P, KD, MEM], F32R), view("memT_lo", 6, [P, KD, MEM], F32R, at=8192)
    xqT, xkT = view("xqT", 3, [P, KD, SEQ]), view("xkT", 4, [P, KD, MEM])
    xv = view("xv", 4, [P, MEM // P, D], at=8192)
    xpT = [view(f"xpT{b}", 7, [P, MEM // P, SEQ], at=4096 * b) for b in range(2)]
    xprobs = [view(f"xprobs{b}", 7, [P, MEM], at=8192 + 1024 * b) for b in range(4)]
    xo_hi, xo_lo = view("xo_hi", 5, [P, KD, SEQ], F32R), view("xo_lo", 6, [P, KD, SEQ], F32R)
    scan_mask = nc.alloc_sbuf_tensor_at("scan_mask", [P, SEQ], F32, offset=rope_at)
    out_norm = nc.alloc_sbuf_tensor_at("out_norm", [P, 2, HD], F32, offset=rope_at + 2048)
    zeros = nc.alloc_sbuf_tensor_at("zeros", [P, P], F32, offset=rope_at + 3200)
    gdn_par = nc.alloc_sbuf_tensor_at("gdn_par", [P, 2, HEADS], F32, offset=rope_at + 3072)
    hnT = view("hnT", 4, [P, KD, SEQ])
    ffn_gain = view("ffn_gain", 7, [P, D])
    w_router = view("w_router", 7, [P, KD, NG + NE], at=4096)
    b_router = view("b_router", 7, [P, NG + NE], at=8192)
    at6 = [0]

    def scratch(name, shape, dtype=F32):
        t = view(name, 6, shape, dtype, at=8192 + at6[0])
        at6[0] += (int(np.prod(shape[1:])) * 4 + 31) // 32 * 32
        assert at6[0] <= 8192
        return t

    logits = scratch("logits", [P, NT, NG + NE])
    hot_g = scratch("hot_g", [P, NT, NG])
    chosen = scratch("chosen", [P, NT, EPG])
    hot_e = scratch("hot_e", [P, 2, NT, EPG])
    experts = scratch("experts", [P, 2, NT, NE])
    rank = scratch("rank", [P, NT, NE])
    pick = scratch("pick", [P, 2, NT * NE])
    iota_neg = scratch("iota_neg", [P, EPG])
    over_e = scratch("over_e", [P, OVER * NE])
    over_n = scratch("over_n", [P, OVER])
    per_e = [scratch(f"per_e{k}", [P, NE]) for k in range(4)]
    per_t = [scratch(f"per_t{k}", [P, 2 * NT]) for k in range(8)]
    weight = scratch("weight", [P, 2, NT])
    row_of = scratch("row_of", [P, 2 * NT], I32)
    tok_of = scratch("tok_of", [BLK, BLOCKS + 1], I32)
    over = scratch("over", [P, OVER + 1], I32)
    hot_r = view("hot_r", 5, [P, 2 * NT, BLK])
    hot_b = view("hot_b", 5, [P, 2 * NT, BLOCKS + 1], at=4096)
    eraw = [raw[(len(units) + k) % RAW] for k in range(4)] + [view(f"eraw{k}", 2, [P, 4, 512], at=8192 * k) for k in range(2)]
    e_hi, e_lo = [], []
    for k in range(6):
        if k < 2:
            m = (len(split_of) + k) % SPL
            e_hi.append(w_hi[m])
            e_lo.append(w_lo[m])
        else:
            r = (1, 3, 4, 7)[k - 2]
            e_hi.append(view(f"e_hi{k}", r, [P, 4, 512], F32R))
            e_lo.append(view(f"e_lo{k}", r, [P, 4, 512], F32R, at=8192))
    xg = view("xg", 5, [BLK, D])
    bT_hi, bT_lo = view("bT_hi", 5, [P, KD, BLK], F32R, at=4096), view("bT_lo", 5, [P, KD, BLK], F32R, at=8192)
    silu_g, act_h = view("silu_g", 5, [BLK, FF], at=12288), view("act_h", 5, [BLK, FF], at=14336)
    aT_hi, aT_lo = view("aT_hi", 6, [P, FF // P, BLK], F32R), view("aT_lo", 6, [P, FF // P, BLK], F32R, at=2048)
    y_rows = view("y_rows", 6, [BLK, D], at=4096)
    picked = [view(f"picked{t}", 1 + t // 2, [P, 2, D], at=8192 * (t % 2)) for t in range(NT)]
    last_gain = view("last_gain", 4, [P, D])
    G_EVEN, G_ODD, G_MIX, G_X, G_MEM, CONV_B, LB, LAM = 0, 8, 16, 24, 32, 40, 56, 72
    CONV_W, GATE_AB, GATE_XB, CONV2 = PAR1, PAR1 + 64, PAR1 + 96, PAR2
    SS, RS, DECAY, HALF, LBC, OML, ST, SUMS = 0, 4, 8, 40, 72, 80, 96, 136
    T0, T1, T2, T3 = 200, 232, 264, 296
    ABC, GG, BETA, NBETA, CUM, ECUM, EREST, SB, ELAST, L2, DEC8 = 328, 392, 424, 456, 488, 520, 552, 584, 616, 648, 712

    qk_gain = small[:, ABC:ABC + 2 * HD].rearrange("p (k d) -> p k d", d=HD)

    def col(c, n=1):
        return small[:, c:c + n]

    def pcol(c, n=1):
        return par[:, c:c + n]

    def f32(ap):
        return ap.bitcast(F32)

    class Chain:

        def __init__(self, eng, name):
            self.eng, self.sem, self.n = eng, sem(name), 0

        def __call__(self, ins):
            self.n += 1
            ins.then_inc(self.sem, 1)

        def wait(self):
            self.eng.wait_ge(self.sem, self.n)

        def link(self, ins):
            self(ins)
            self.wait()

    def z_parts(i):
        g, t = i // (NT // 2), 2 * (i % (NT // 2))
        bank, z = psum[i][:].rearrange("p (t c) -> p t c", c=GROUP), zz[:, t:t + 2, g]
        return ((z[:, :, 0, 0], bank[:, :, 0:HC]), (z[:, :, 0, 1, 1:], bank[:, :, HC + 1:]),
                (z[:, :, 1, 0], bank[:, :, HC:0:-1]), (z[:, :, 1, 1, 1:], bank[:, :, GROUP - 1:HC:-1]))

    def qkT_bank(i):
        return psum[(4 * (pn["a_gate"][0] % 2) + i) % 8]

    unit_free = {u["split"]: u["free"] for u in units if u["split"] is not None}

    rows_at, norm_at, feat_at = {}, {}, {}
    r = n = f = 0
    for name, tiles, features in (("even", NT, KD), ("odd", NT, KD), ("final", NT, 0), ("mix", NT, KD), ("mem", MEM // P, KD),
                                  ("x", NT, KD), ("ffn", NT, 0), ("last", NT, 0)):
        rows_at[name], norm_at[name], feat_at[name] = r, n, f
        r, n, f = r + tiles, n + 1, f + features

    def norm_bank(name, f):
        base = 4 * (pn[{"even": "f_in", "odd": "xr", "mix": "qkv2", "mem": "xk", "x": "xq"}[name]][0] % 2)
        if name == "mem":
            return psum[base + f // 2][:, (f % 2) * MEM:(f % 2) * MEM + MEM]
        return psum[(base + f) % 8][:]

    def together(eng, k):
        eng.wait_ge(sem("act_stage"), k)
        eng.wait_ge(sem("dve_stage"), k)

    block = ctx.enter_context(nc.Block())

    @block.sync
    def _(sp):
        x_rows = io["x"][0].rearrange("(t p) d -> p t d", p=P)
        sp.dma_start(resid[:], x_rows).then_inc(sem("x_in"), 16)
        sp.dma_start(ident, io["c_masks"][0]).then_inc(sem("first_in"), 16)
        sp.dma_start(prow[G_EVEN:G_EVEN + KD, 0], io["even_norm"][0].rearrange("(r p) -> r p", p=P)).then_inc(sem("first_in"), 16)
        for u in units:
            n, s = u["n"], u["n"] % RAW
            if n == 1:
                sp.wait_ge(sem("x_in"), 16)
            if n >= RAW:
                old = units[n - RAW]
                if old["split"] is not None:
                    sp.wait_ge(sem("lo_done"), old["split"] + 1)
                else:
                    sp.wait_ge(sem(old["free"][0]), old["free"][1])
            if u["split"] is not None:
                sp.dma_start(raw[s][:], u["src"]).then_inc(sem(f"raw_in{s}"), 16)
            else:
                for g, src in enumerate(u["src"]):
                    for d in range(2):
                        sp.dma_start(raw[s][:, 2 * g + d].rearrange("p (b e) -> p b e", e=P), src[:, d]).then_inc(sem(f"gates_in{gate_units.index(u)}"), 16)

        def expert(e, k):
            if k < 4:
                w = io["expert_w_gate_2" if k < 2 else "expert_w_up_2"][0]
                rows = w[bass.ds(e, 1)].rearrange("a (k p) n -> p (a k) n", p=P)
                return rows[:, 4 * (k % 2):4 * (k % 2) + 4]
            w = io["expert_w_down_2"][0]
            return w[bass.ds(e, 1)].rearrange("a (k p) n -> p (a k) n", p=P)[:, :, 512 * (k - 4):512 * (k - 4) + 512]

        def fetch(b, e, ks, first=False):
            for k in ks:
                if not first:
                    if k < 4:
                        sp.wait_ge(sem("gu_lo"), 4 * b + (k - 3))
                    else:
                        sp.wait_ge(sem("d_lo"), 2 * b + (k - 5))
                sp.dma_start(eraw[k][:], expert(e, k)).then_inc(sem(f"e_in{k}"), 16)

        GU, DN = range(4), (4, 5)
        for k in GU:
            u = units[len(units) - RAW + k]
            sp.wait_ge(sem("lo_done"), u["split"] + 1)
            fetch(0, 0, [k], True)
        together(sp, 20)
        fetch(0, 0, DN, True)
        fetch(1, 1, GU)
        with sp.Fori(1, NE - 1) as e:
            fetch(e + 1, e + 1, GU)
            fetch(e, e, DN)
        fetch(NE - 1, NE - 1, DN)
        together(sp, 23)
        n_over = sp.value_load(over[0:1, OVER:OVER + 1], min_val=0, max_val=OVER)
        with sp.If(n_over > 0):
            with sp.Fori(NE, BLOCKS) as b:
                e = sp.value_load(over[0:1, bass.ds(b - NE, 1)], min_val=0, max_val=NE - 1)
                fetch(b, e, GU)
                fetch(b, e, DN)
        out = io["out"][0].rearrange("(t p) d -> p t d", p=P)
        for t in range(NT):
            sp.wait_ge(sem("norm_rows"), rows_at["last"] + t + 1)
            sp.dma_start(out[:, t], resid[:, t]).then_inc(sem("out_saved"), 16)
        sp.wait_ge(sem("out_saved"), 16 * NT)

    def raw_arrived(eng, n):
        k = sum(1 for u in units[:n + 1] if u["n"] % RAW == n % RAW and u["split"] is not None)
        eng.wait_ge(sem(f"raw_in{n % RAW}"), 16 * k)

    @block.gpsimd
    def _(pool):
        def load(dst, src, name):
            pool.dma_start(dst, src).then_inc(sem(name), 16)

        def rows(r, k, src):
            n = src.shape[0]
            load(prow[r:r + n, k], src, "par_in")

        def vec(a):
            return a.rearrange("(r p) -> r p", p=P)

        rows(G_ODD, 0, vec(io["odd_norm"][0]))
        rows(G_MIX, 0, vec(io["norm_mix_w_2"][0]))
        rows(G_X, 0, vec(io["norm_xattn_w_2"][0]))
        rows(G_MEM, 0, vec(io["norm_mem_w_2"][0]))
        rows(CONV_B, 0, vec(io["conv_b"][0]))
        rows(LB, 0, io["hgrn_lb_2"].rearrange("l (r p) -> (l r) p", p=P))
        rows(LAM, 0, io["rglru_lambda"][0].rearrange("l (r p) -> (l r) p", p=P))
        rows(0, 1, io["conv_w"][0].rearrange("l (r p) -> (l r) p", p=P))
        rows(64, 1, io["gate_a_b"][0].rearrange("l r p -> (l r) p"))
        rows(96, 1, io["gate_x_b"][0].rearrange("l r p -> (l r) p"))
        rows(0, 2, io["conv_w_2"][0].rearrange("l (r p) -> (l r) p", p=P))
        pool.wait_ge(sem("x_in"), 16)
        pool.wait_ge(sem("raw_in1"), 16)
        load(masks[:, 1:], io["c_masks"][1:].rearrange("k p n -> p k n"), "dft_in")
        load(tokid[:], io["c_tok"], "dft_in")
        load(dft_c[:], io["c_dft_c"].rearrange("(k p) n -> p k n", p=P), "dft_in")
        load(dft_s[:], io["c_dft_s"].rearrange("(t p) n -> p t n", p=P), "dft_in")
        load(four_w[:], io["fourier_w"][0].rearrange("g (k p) e -> p (g k) e", p=P), "dft_in")
        load(rope[:], io["c_rope"].rearrange("r (t p) n -> p r t n", p=P), "rope_in")
        together(pool, 1)
        load(qk_gain[:, 0], io["q_gain"].to_broadcast([P, HD]), "gain_in")
        load(qk_gain[:, 1], io["k_gain"].to_broadcast([P, HD]), "gain_in")
        together(pool, 7)
        pool.memset(zeros[:], 0.0).then_inc(sem("zeros_set"), 1)
        pool.wait_ge(sem("zeros_set"), 1)
        rows = OVER * BLK // 10
        load(y_dram[NE * BLK:].rearrange("(p r) (k d) -> p (r k) d", r=10, d=P), zeros[0:rows].unsqueeze(1).to_broadcast([rows, 10 * KD, P]), "y_zeroed")
        load(scan_mask[:], io["c_scan"], "late_in")
        load(out_norm[:, 0], io["gdn_out_norm_w_2"].to_broadcast([P, HD]), "late_in")
        load(out_norm[:, 1], io["hgrn_out_norm_w_2"].to_broadcast([P, HD]), "late_in")
        load(gdn_par[:, 0], io["gdn_a_log_2"].to_broadcast([P, HEADS]), "late_in")
        load(gdn_par[:, 1], io["gdn_dt_bias_2"].to_broadcast([P, HEADS]), "late_in")
        together(pool, 9)
        for it in range(2 * RB):
            pool.wait_ge(sem("gate_sig"), 2 * it + 2)
            pool.tensor_tensor(ri[:, it % 8], ri[:, it % 8], xc[:, it // 2], ALU.mult).then_inc(sem("ix"), 1)
        together(pool, 10)
        load(final_gain[:], io["final_norm"].rearrange("(a d) -> a d", a=1).to_broadcast([P, D]), "final_in")
        pool.wait_ge(sem("norm_rows"), rows_at["final"] + NT)
        load(h_dram.rearrange("(t p) d -> p t d", p=P), resid[:], "h_saved")
        pool.wait_ge(sem("norm_lo"), feat_at["mix"] + KD)
        load(hT_dram, hT_lo[:], "hT_saved")
        pool.wait_ge(*after("h_saved", 16))
        load(w_ab[:], w2[:, AB:AB + 2 * HEADS].rearrange("(k p) n -> p k n", p=P), "w_ab_in")
        for f in range(2 * HEADS):
            if f % 4 == 0:
                pool.wait_ge(sem("silu2"), f // 4 + 1)
            pool.tensor_tensor(sq[:, f], qkvT[:, f], qkvT[:, f], ALU.mult).then_inc(sem("l2_sq"), 1)
        def part(e, dst, level):
            return pool.tensor_tensor(dst, gs[e][2][:], m_level[level].unsqueeze(1).to_broadcast([P, 2, P]), ALU.mult)

        for n in range(0, 2 * HEADS, 4):
            for e in range(4):
                pool.wait_ge(sem("g_M"), 2 * (n + e) + 2)
                part(e, nm16[e][:, 1], 0).then_inc(sem("g_M16"), 1)
            for e in range(4):
                pool.wait_ge(sem("g_qdec"), n + e + 1)
                part(e, gs[e][0][:], 1).then_inc(sem("g_M32"), 1)
                part(e, gs[e][1][:], 2).then_inc(sem("g_M64"), 1)
            for e in range(4):
                pool.wait_ge(sem("g_R4pe"), n + e + 1)
                part(e, nm16[e][:, 0], 3).then_inc(sem("g_M128"), 1)
        together(pool, 13)
        load(hT_lo[:], hT_dram, "hT_back")
        pool.wait_ge(sem("y_T"), 2 * KD)
        load(resid[:], h_dram.rearrange("(t p) d -> p t d", p=P), "h_back")
        last = panels[pn["br_b"][-1]]
        pool.wait_ge(sem("panel_done"), last["done"] + last["nj"])
        load(mem_tok[:], io["mem_2"][0].rearrange("(t p) d -> p t d", p=P), "mem_in")
        together(pool, 21)
        load(ffn_gain[:], io["norm_ffn_w_2"].to_broadcast([P, D]), "router_in")
        load(w_router[:, :, 0:NG], io["router_group_w_2"][0].rearrange("(k p) n -> p k n", p=P), "router_in")
        load(w_router[:, :, NG:], io["router_expert_w_2"][0].rearrange("(k p) n -> p k n", p=P), "router_in")
        load(b_router[:, 0:NG], io["router_group_b_2"].to_broadcast([P, NG]), "router_in")
        load(b_router[:, NG:], io["router_expert_b_2"].to_broadcast([P, NE]), "router_in")
        pool.wait_ge(sem("norm_rows"), rows_at["ffn"] + NT)
        load(hn_dram.rearrange("(t p) d -> p t d", p=P), xs[:], "hn_saved")

        def gather(b):
            if b:
                pool.wait_ge(sem("x_T"), b)
            pool.indirect_dma_start(out=xg[:], out_offset=None, in_=hn_dram,
                                    in_offset=bass.IndirectOffsetOnAxis(ap=tok_of[:, b:b + 1], axis=0)).then_inc(sem("x_rows"), 16)
        together(pool, 23)
        pool.wait_ge(sem("y_zeroed"), 16)
        pool.wait_ge(sem("hn_saved"), 16)
        for b in range(NE):
            gather(b)
        n_over = pool.value_load(over[0:1, OVER:OVER + 1], min_val=0, max_val=OVER)
        with pool.If(n_over > 0):
            for b in range(NE, BLOCKS):
                gather(b)
            pool.wait_ge(sem("y_saved"), 16 * BLOCKS)
        together(pool, 24)
        pool.wait_ge(sem("y_saved"), 16 * NE)
        for t in range(NT):
            for a in range(2):
                pool.indirect_dma_start(out=picked[t][:, a], out_offset=None, in_=y_dram,
                                        in_offset=bass.IndirectOffsetOnAxis(ap=row_of[:, a * NT + t:a * NT + t + 1], axis=0)).then_inc(sem(f"picked{t}"), 16)
        load(last_gain[:], io["final_norm_w_2"].rearrange("(a d) -> a d", a=1).to_broadcast([P, D]), "last_in")

    @block.tensor
    def _(pe):
        stage_n = [0]

        def stage(wait=True):
            stage_n[0] += 1
            if wait:
                together(pe, stage_n[0])

        def gemm(ps, act_in, feature, ntok=SEQ):
            for p in ps:
                pan = panels[p]
                if p >= 2:
                    old = panels[p - 2]
                    pe.wait_ge(sem("evac_act" if old["evac"] == "A" else "evac_dve"), old["at"] + old["nj"])
                for ui, m in enumerate(pan["units"]):
                    pe.wait_ge(sem("lo_done"), m + 1)
                    last_unit = ui == len(pan["units"]) - 1
                    wh, wl = w_hi[m % SPL], w_lo[m % SPL]
                    for j in range(pan["nj"]):
                        for k in range(4):
                            kk = 4 * ui + k
                            ah, al = act_in(kk)
                            first, last = kk == 0, last_unit and k == 3
                            if feature:
                                js = slice(j * P, j * P + P)
                                pairs = [(wh[:, k, js], ah), (wl[:, k, js], ah), (wh[:, k, js], al)]
                                out = psum[4 * (p % 2) + j][:, 0:ntok]
                            else:
                                js = slice(j * P, j * P + P)
                                pairs = [(ah[:, js], wh[:, k]), (ah[:, js], wl[:, k]), (al[:, js], wh[:, k])]
                                out = psum[4 * (p % 2) + j][:]
                            for x, (st, mv) in enumerate(pairs):
                                mm = pe.matmul(out, st, mv, start=first and x == 0, stop=last and x == 2)
                        if last_unit:
                            mm.then_inc(sem("panel_done"), 1)
                    if not last_unit:
                        mm.then_inc(sem("unit_used"), 1)

        def norm(name):
            rows = normed[name]
            for t in range(NT):
                pe.wait_ge(sem("norm_rows"), rows_at[name] + t + 1)
                for f in range(KD):
                    tr = pe.transpose(norm_bank(name, f)[:, t * P:t * P + P], rows[:, t, f * P:f * P + P], ident)
                    if t == NT - 1:
                        tr.then_inc(sem("norm_T"), 1)

        def hT(k):
            return hT_hi[:, k], hT_lo[:, k]

        def hT_as_it_comes(name):
            there = set()

            def f(k):
                if k not in there:
                    there.add(k)
                    pe.wait_ge(sem("norm_lo"), feat_at[name] + k + 1)
                return hT(k)
            return f

        stage()
        pe.wait_ge(sem("first_in"), 32)
        pe.transpose(psum[0][:, 0:KD], prow[0:KD, 0], ident[0:KD, 0:KD]).then_inc(sem("par_T"), 1)
        pe.wait_ge(sem("par_done"), 1)
        norm("even")
        gemm(pn["f_in"], hT_as_it_comes("even"), True)
        stage(wait=False)
        pe.wait_ge(sem("dft_in"), 16 * 5)
        for i in range(GROUPS * NT // 2):
            g = i // (NT // 2)
            if i % 4 == 0:
                done = panels[pn["f_in"][i // 4]]
                pe.wait_ge(sem("evac_act"), done["at"] + done["nj"])
            for tt in range(2):
                t = 2 * (i % (NT // 2)) + tt
                for k in range(2):
                    mm = pe.matmul(psum[i][:, tt * GROUP:tt * GROUP + GROUP], finT[:, 2 * g + k, t * P:t * P + P], dft_c[:, k],
                                   start=k == 0, stop=k == 1)
            mm.then_inc(sem("z_done"), 1)
        pe.wait_ge(sem("z_act"), 2 * KD)
        pe.wait_ge(sem("z_dve"), 2 * KD)
        pe.wait_ge(sem("par_in"), 16 * 11)
        for k, n in enumerate((104, 128, 96)):
            pe.transpose(psum[5 + k][:, 0:n], prow[0:n, k], ident[0:n, 0:n]).then_inc(sem("par_T"), 1)
        for i in range(KD):
            g, h = i // 2, i % 2
            if i >= 5:
                pe.wait_ge(sem("par_done"), i - 3)
            for r, c in ((0, slice(0, HS + 1)), (1, slice(HS + 1, SEQ))):
                for t in range(NT):
                    mm = pe.matmul(psum[i][:, c], zz[:, t, g, h, r], dft_s[:, t, c], start=t == 0, stop=t == NT - 1)
            mm.then_inc(sem("y_done"), 1)
        stage()
        gemm(pn["f_gate"], hT, True)
        old = panels[pn["f_gate"][-1]]
        pe.wait_ge(sem("evac_act"), old["at"] + old["nj"])
        for i in range(KD):
            g, h = i // 2, i % 2
            for k in range(2):
                mm = pe.matmul(psum[i][:], four_w[:, 2 * g + k, h * P:h * P + P], ymixT[:, 2 * g + k],
                               start=k == 0, stop=k == 1)
            mm.then_inc(sem("fw_done"), 1)
        stage(wait=False)
        pe.wait_ge(sem("fw_prod"), KD)
        gemm(pn["qkv"], hT, False)
        gemm(pn["a_gate"], hT, True)
        stage(wait=False)
        for t in range(NT):
            pe.wait_ge(sem("rope_done"), t + 1)
            for hg in range(3):
                i = 3 * t + hg
                if i in (0, 4):
                    done = panels[pn["a_gate"][i // 4]]
                    pe.wait_ge(sem("evac_act"), done["at"] + done["nj"])
                if i >= 8:
                    pe.wait_ge(sem("qkT_act"), i - 7)
                for h in range(4 * hg, min(4 * hg + 4, NQ + NKV)):
                    src = q_tok[:, t, h * HD:h * HD + HD] if h < NQ else kv_tok[:, t, (h - NQ) * HD:(h - NQ + 1) * HD]
                    tr = pe.transpose(qkT_bank(i)[:, (h % 4) * P:(h % 4) * P + P], src, ident)
                tr.then_inc(sem("qkT_done"), 1)
        stage()
        n_i = NQ * NT

        def scores(i):
            h, t = i // NT, i % NT
            if i >= 4:
                pe.wait_ge(sem("at_exp"), i - 3)
            pe.matmul(psum[i % 4][:], qkT[:, h, t * P:t * P + P], qkT[:, NQ + h // (NQ // NKV)],
                      start=True, stop=True).then_inc(sem("at_sc"), 1)

        def attend(h):
            pe.wait_ge(sem("at_pT"), NT * (h + 1))
            if h >= 2:
                pe.wait_ge(sem("at_prod"), h - 1)
            for t in range(NT):
                c = (NKV + h // (NQ // NKV)) * HD
                mm = pe.matmul(psum[6 + h % 2][:], kv_tok[:, t, c:c + HD], pT[h % 2][:, t],
                               start=t == 0, stop=t == NT - 1)
            mm.then_inc(sem("at_av"), 1)

        for i in range(3):
            scores(i)
        for i in range(n_i):
            if i + 3 < n_i:
                scores(i + 3)
            pe.wait_ge(sem("at_norm"), i + 1)
            if i >= 2:
                pe.wait_ge(sem("at_pT"), i - 1)
            for k in range(NT):
                tr = pe.transpose(psum[4 + i % 2][:, k * P:k * P + P], probs[i % 4][:, k * P:k * P + P], ident)
            tr.then_inc(sem("at_tr"), 1)
            if i % NT == 1 and i >= NT:
                attend(i // NT - 1)
        attend(NQ - 1)
        stage()
        def mix(k):
            if k < KD:
                return mixf_hi[:, k], mixf_lo[:, k]
            return mixa_hi[:, k - KD], mixa_lo[:, k - KD]
        gemm(pn["even_out"], mix, False)
        stage(wait=False)
        norm("odd")
        gemm(pn["xr"], hT_as_it_comes("odd"), True)
        gemm(pn["r_gate"], hT, True)
        stage()
        for it in range(2 * RB):
            blk, d = it // 2, it % 2
            u = gate_units[blk // 4]
            if it % 8 == 0:
                pe.wait_ge(sem(f"gates_in{blk // 4}"), 16 * 4)
            for g in range(2):
                n = 2 * it + g
                if n >= 8:
                    pe.wait_ge(sem("gate_sig"), n - 7)
                pe.matmul(psum[n % 8][:], raw[u["n"] % RAW][:, 2 * g + d, (blk % 4) * P:(blk % 4) * P + P],
                          xc[:, blk], start=True, stop=True).then_inc(sem("gate_done"), 1)
        stage(wait=False)
        pe.wait_ge(sem("gate_sig"), 4 * RB)

        def rnn_out(k):
            pe.wait_ge(sem("rp_lo"), k // 4 + 1)
            return rp_hi[:, k], rp_lo[:, k]
        gemm(pn["odd_out"], rnn_out, False)
        stage(wait=False)
        norm("mix")
        gemm(pn["qkv2"], hT_as_it_comes("mix"), True)
        pe.wait_ge(sem("ab_lo"), 1)
        last = panels[pn["qkv2"][-2]]
        pe.wait_ge(sem("evac_dve"), last["at"] + last["nj"])
        for k in range(KD):
            ah, al = hT(k)
            for x, (st, mv) in enumerate(((wab_hi[:, k], ah), (wab_lo[:, k], ah), (wab_hi[:, k], al))):
                mm = pe.matmul(psum[ab_base][0:2 * HEADS], st, mv, start=k == 0 and x == 0, stop=k == KD - 1 and x == 2)
        mm.then_inc(sem("ab_done"), 1)
        for f in range(2 * HEADS):
            pe.wait_ge(*after("l2_sq", f + 1))
            for t in range(NT):
                mm = pe.matmul(psum[ab_base + 2][:, f * NT + t:f * NT + t + 1], sq[:, f, t * P:t * P + P], ones[:, 0:1], start=True, stop=True)
            if f == 3:
                pe.wait_ge(sem("ab_act"), 1)
                for t in range(NT):
                    tr = pe.transpose(psum[ab_base + 1][:, t * 16:t * 16 + 16], ab_rows[:, t * P:t * P + P], ident[0:16, 0:16])
                tr.then_inc(sem("ab_done"), 1)
        mm.then_inc(sem("l2_ss"), 1)
        stage()
        pe.wait_ge(*after("g_log", 1))
        pe.matmul(psum[ab_base][:, 0:32], m_le, col(GG, 32), start=True, stop=True).then_inc(sem("g_cum"), 1)
        pe.matmul(psum[ab_base + 1][:, 0:32], m_gt, col(GG, 32), start=True, stop=True).then_inc(sem("g_cum"), 1)
        pe.wait_ge(sem("l2_inv"), 1)
        for f in range(2 * HEADS):
            if f >= 4:
                pe.wait_ge(*after("l2_mul", f - 3))
            for t in range(NT):
                c = L2 + f * NT + t
                tr = pe.transpose(psum[l2_base + f % 4][:, t * P:t * P + P], col(c).to_broadcast([P, P]), ident)
            tr.then_inc(sem("l2_bc"), 1)
        pe.wait_ge(*after("l2_mul", 2 * HEADS))
        pe.wait_ge(sem("g_ready"), 1)
        EE = range(4)

        def bank(e, b):
            return psum[2 * e + b]

        def two(e, b, at, f, inc=None):
            for c in range(2):
                mm = pe.matmul(bank(e, b)[:, at + c * P:at + c * P + P], *f(c), start=True, stop=True)
            if inc:
                mm.then_inc(sem(inc), 1)

        def two_T(e, b, at, f, inc=None):
            for c in range(2):
                mm = pe.transpose(bank(e, b)[:, at + c * P:at + c * P + P], f(c), ident)
            if inc:
                mm.then_inc(sem(inc), 1)

        def head(n, e):
            return (n + e) // 2

        def tile(n, f, e, c):
            t = 2 * (e % 2) + c
            return qkvT[:, f * HEADS + head(n, e), t * P:t * P + P]

        def rows_gram(n):
            for e in EE:
                two(e, 0, 0, lambda c: (col(GG + (2 * (e % 2) + c) * HEADS + head(n, e)).to_broadcast([P, P]), m_le))
                two(e, 0, 256, lambda c: (tile(n, 1, e, c), tile(n, 1, e, c)), "g_gram")

        def keys_queries(n):
            for e in EE:
                if n:
                    pe.wait_ge(sem("g_uw"), 2 * (n - 4 + e) + 2)
                two(e, 1, 0, lambda c: (tile(n, 1, e, c), tile(n, 0, e, c)), "g_qk")

        rows_gram(0)
        keys_queries(0)
        for n in range(0, 2 * HEADS, 4):
            for e in EE:
                pe.wait_ge(sem("g_M"), 2 * (n + e) + 2)
                two_T(e, 0, 0, lambda c: gs[e][2][:, c], "g_NT")
            for e in EE:
                pe.wait_ge(sem("g_N16"), n + e + 1)
                pe.wait_ge(sem("g_M16"), n + e + 1)
                two(e, 1, 0, lambda c: (nm16[e][:, 1, c], nm16[e][:, 0, c]))
                two(e, 1, 256, lambda c: (nm16[e][:, 0, c], nm16[e][:, 1, c]), "g_2pe")
            for e in EE:
                pe.wait_ge(sem("g_2"), n + e + 1)
                two(e, 0, 0, lambda c: (nm2[e][:, 1, c], nm2[e][:, 0, c]))
                two(e, 0, 256, lambda c: (nm2[e][:, 0, c], nm2[e][:, 1, c]), "g_4pe")
                pe.wait_ge(sem("g_R1"), n + e + 1)
                two(e, 1, 0, lambda c: (nm2[e][:, 1, c], gs[e][7][:, c]), "g_R2pe")
            for e in EE:
                pe.wait_ge(sem("g_4"), n + e + 1)
                pe.wait_ge(sem("g_R2"), n + e + 1)
                two(e, 0, 256, lambda c: (nm16[e][:, 0, c], nm16[e][:, 1, c]))
                two(e, 0, 0, lambda c: (nm16[e][:, 1, c], gs[e][7][:, c]), "g_R4pe")
            for e in EE:
                pe.wait_ge(sem("g_8"), n + e + 1)
                pe.wait_ge(sem("g_R4"), n + e + 1)
                two(e, 1, 0, lambda c: (nm2[e][:, 0, c], gs[e][7][:, c]), "g_R8pe")
            for lv in range(3):
                for e in EE:
                    o = (gs[e][0], gs[e][1], nm16[e][:, 0])[lv]
                    pe.wait_ge(sem(("g_R8", "g_J0", "g_J1")[lv]), n + e + 1)
                    pe.wait_ge(sem(("g_M32", "g_M64", "g_M128")[lv]), n + e + 1)
                    two_T(e, 0, 0, lambda c: gs[e][7][:, c])
                    two(e, 0, 256, lambda c: (o[:, c], gs[e][7][:, c]), f"g_TYpe{lv}")
                for e in EE:
                    pe.wait_ge(sem(f"g_TY{lv}"), n + e + 1)
                    two(e, 1, 0, lambda c: (nm2[e][:, 0, c], nm2[e][:, 1, c]), f"g_Jpe{lv}")
            for e in EE:
                two_T(e, 0, 0, lambda c: tile(n, 1, e, c))
                two_T(e, 0, 256, lambda c: tile(n, 2, e, c), "g_kvT")
            for e in EE:
                pe.wait_ge(sem("g_J2"), n + e + 1)
                pe.wait_ge(sem("g_kv"), n + e + 1)
                two(e, 1, 0, lambda c: (gs[e][7][:, c], nm2[e][:, 1, c]))
                two(e, 1, 256, lambda c: (nm2[e][:, 0, c], gs[e][7][:, c]), "g_uwpe")
            if n + 4 < 2 * HEADS:
                rows_gram(n + 4)
                keys_queries(n + 4)
        stage()
        for t in range(NT):
            s_in = gstate[t % 2]
            ts = slice(t * P, t * P + P)
            if t:
                for h in range(HEADS):
                    if h % 4 == 0:
                        pe.wait_ge(*after("s_new", 2 * (t - 1) + h // 4 + 1))
                    mm = pe.matmul(psum[h // 4][:, (h % 4) * P:(h % 4) * P + P], qkvT[:, HEADS + h, ts], s_in[:, h],
                                   start=True, stop=True)
                    if h % 4 == 3:
                        mm.then_inc(sem("s_ws"), 1)
            for h in range(HEADS):
                if h % 4 == 0:
                    pe.wait_ge(*after("s_v", 2 * t + h // 4 + 1))
                    if t:
                        pe.wait_ge(*after("s_o", 2 * (t - 1) + h // 4 + 1))
                out = psum[2 + h // 4][:, (h % 4) * P:(h % 4) * P + P]
                if t:
                    pe.matmul(out, qkvT[:, h, ts], s_in[:, h], start=True, stop=False)
                mm = pe.matmul(out, intraT[:, h, t], vnew[:, h], start=t == 0, stop=True)
                if h % 4 == 3:
                    mm.then_inc(sem("s_ope"), 1)
            if t < NT - 1:
                for h in range(HEADS):
                    mm = pe.matmul(psum[4 + h // 4][:, (h % 4) * P:(h % 4) * P + P], qkvT[:, 2 * HEADS + h, ts], vnew[:, h],
                                   start=True, stop=True)
                    if h % 4 == 3:
                        mm.then_inc(sem("s_ds"), 1)

        def branch(b, w_panels):
            o = u_tok[:].rearrange("p t h d -> p t (h d)") if b == "a" else hintra[:].rearrange("p t h d -> p t (h d)")
            gate = pn["gate_" + b]
            gemm(gate[0:1], hT, True)
            for half in range(2):
                last = panels[(pn["og_" + b] + gate)[1 + half]]
                pe.wait_ge(sem("evac_act"), last["at"] + last["nj"])
                for t in range(NT):
                    pe.wait_ge(sem("y_rows"), t + 1 + (NT if b == "b" else 0))
                    for f in range(4):
                        c = (4 * half + f) * P
                        tr = pe.transpose(psum[4 * (gate[1 - half] % 2) + f][:, t * P:t * P + P], o[:, t, c:c + P], ident)
                        if t == NT - 1:
                            tr.then_inc(sem("y_T"), 1)
            pe.wait_ge(sem("y_lo"), 4 + (KD if b == "b" else 0))
            gemm(gate[1:2], hT, True)
            pe.wait_ge(sem("y_lo"), KD + (KD if b == "b" else 0))
            gemm(w_panels, lambda k: (y_hi[:, k], y_lo[:, k]), True)

        stage()
        pe.wait_ge(sem("hT_back"), 16)
        gemm(pn["og_a"], hT, False)
        branch("a", pn["br_a"])
        stage(wait=False)
        gemm(pn["f"], hT, True)
        gemm(pn["q"], hT, True)
        gemm(pn["i"], hT, False)
        last = panels[pn["i"][-1]]
        pe.wait_ge(sem("evac_act"), last["at"] + last["nj"])
        for h in range(HEADS):
            pe.wait_ge(*after("h_kd", h + 1))
            for t in range(NT):
                tr = pe.transpose(psum[h][:, t * P:t * P + P], forget[:, h, t * P:t * P + P], ident)
            tr.then_inc(sem("h_kdT"), 1)
        for h in range(HEADS):
            pe.wait_ge(*after("h_kdev", h + 1))
            for t in range(NT):
                ts = slice(t * P, t * P + P)
                mm = pe.matmul(psum[h][:, ts], hexp[:, h, ts], hqT[:, h, ts], start=True, stop=True)
            mm.then_inc(sem("h_in"), 1)
        stage()
        for t in range(NT):
            for s in range(2):
                for h in range(HEADS):
                    if h % 4 == 0 and t:
                        pe.wait_ge(*after("hs_S", HEADS * (2 * (t - 1) + s) + 4 * (h // 4) + 4))
                    r = slice(s * QC, s * QC + QC)
                    mm = pe.matmul(psum[2 * s + h // 4][:, (h % 4) * P:(h % 4) * P + P], hkd[r, h, t], hv[r, t, h * P:h * P + P],
                                   start=True, stop=True)
                    if h % 4 == 3:
                        mm.then_inc(sem("hs_kv"), 1)
            for h in range(HEADS):
                bk = psum[4 + 2 * (t % 2) + h // 4]
                cs = slice((h % 4) * P, (h % 4) * P + P)
                if h % 4 == 0 and t >= 2:
                    pe.wait_ge(*after("hs_o", 2 * (t - 2) + h // 4 + 1))
                pe.wait_ge(*after("hs_S", HEADS * 2 * t + h + 1))
                for s in range(2):
                    r = slice(s * QC, s * QC + QC)
                    pe.matmul(bk[r, cs], hqT[:, h, t * P + s * QC:t * P + s * QC + QC], hstate[(2 * t + s) % 3][:, h],
                              start=True, stop=False, skip_group_check=True)
                mm = pe.matmul(bk[:, cs], hintra[:, t, h], hv[:, t, h * P:h * P + P], start=False, stop=True,
                               skip_group_check=True)
                if h % 4 == 3:
                    mm.then_inc(sem("hs_ope"), 1)
        stage()
        gemm(pn["og_b"], hT, False)
        branch("b", pn["br_b"])
        stage(wait=False)
        def merged_in(k):
            if k % 4 == 0:
                pe.wait_ge(*after("mg_lo", k // 4 + 1))
            return mg_hi[:, k], mg_lo[:, k]
        gemm(pn["mix_out"], merged_in, False)
        stage(wait=False)
        last = panels[pn["mix_out"][0]]
        pe.wait_ge(sem("evac_dve"), last["at"] + last["nj"])
        for t in range(MEM // P):
            pe.wait_ge(sem("norm_rows"), rows_at["mem"] + t + 1)
            for f in range(KD):
                tr = pe.transpose(norm_bank("mem", f)[:, t * P:t * P + P], mem_xs[:, t, f * P:f * P + P], ident)
                if t == MEM // P - 1:
                    tr.then_inc(sem("norm_T"), 1)
        pe.wait_ge(sem("norm_lo"), feat_at["mem"] + KD)

        def memT(k):
            return memT_hi[:, k], memT_lo[:, k]
        gemm(pn["xk"], memT, True, MEM)
        gemm(pn["xv"], memT, False)
        last = panels[pn["xv"][-1]]
        pe.wait_ge(sem("evac_act"), last["at"] + last["nj"])
        norm("x")
        gemm(pn["xq"], hT_as_it_comes("x"), True)
        stage(wait=False)
        last = panels[pn["xq"][-1]]
        pe.wait_ge(sem("evac_act"), last["at"] + last["nj"])
        n_x = XH * NT

        def xscores(i):
            h, t = i // NT, i % NT
            if i >= 4:
                pe.wait_ge(*after("xa_exp", i - 3))
            for c in range(2):
                mm = pe.matmul(psum[i % 4][:, 0:MEM], xqT[:, 2 * h + c, t * P:t * P + P], xkT[:, 2 * h + c],
                               start=c == 0, stop=c == 1)
            mm.then_inc(sem("xa_sc"), 1)

        def xattend(h):
            pe.wait_ge(*after("xa_pT", NT * (h + 1)))
            if h:
                pe.wait_ge(*after("xa_lo", 2 * h))
            for c in range(2):
                for m in range(MEM // P):
                    mm = pe.matmul(psum[6 + c][:], xv[:, m, h * XD + c * P:h * XD + c * P + P], xpT[h % 2][:, m],
                                   start=m == 0, stop=m == MEM // P - 1)
                mm.then_inc(sem("xa_av"), 1)

        for i in range(3):
            xscores(i)
        for i in range(n_x):
            if i + 3 < n_x:
                xscores(i + 3)
            pe.wait_ge(*after("xa_norm", i + 1))
            if i >= 2:
                pe.wait_ge(*after("xa_pT", i - 1))
            for m in range(MEM // P):
                tr = pe.transpose(psum[4 + i % 2][:, m * P:m * P + P], xprobs[i % 4][:, m * P:m * P + P], ident)
            tr.then_inc(sem("xa_tr"), 1)
            if i % NT == 1 and i >= NT:
                xattend(i // NT - 1)
        xattend(XH - 1)
        stage()
        gemm(pn["xo"], lambda k: (xo_hi[:, k], xo_lo[:, k]), False)
        stage(wait=False)
        for t in range(NT):
            pe.wait_ge(sem("norm_rows"), rows_at["ffn"] + t + 1)
            for f in range(KD):
                tr = pe.transpose(psum[f][:, t * P:t * P + P], xs[:, t, f * P:f * P + P], ident)
                if t == NT - 1:
                    tr.then_inc(sem("hnT_pe"), 1)
        pe.wait_ge(*after("hnT_act", KD))
        pe.wait_ge(*after("router_in", 16 * 5))
        R = NG + NE
        for t in range(NT):
            for k in range(KD):
                mm = pe.matmul(psum[0][:, t * R:t * R + R], hnT[:, k, t * P:t * P + P], w_router[:, k], start=k == 0, stop=k == KD - 1)
        mm.then_inc(sem("rt_pe"), 1)
        pe.wait_ge(*after("rt_taken", 1))
        for t in range(NT):
            n = 0
            for a in range(2):
                for s in range(t + 1):
                    pe.matmul(psum[1][:, t * NE:t * NE + NE], m_before if s == t else ones, experts[:, a, s],
                              start=n == 0, stop=n == 2 * t + 1)
                    n += 1
        for n in range(2 * NT):
            mm = pe.matmul(psum[2][:, 0:NE], ones, experts[:, n // NT, n % NT], start=n == 0, stop=n == 2 * NT - 1)
        mm.then_inc(sem("rt_pe"), 1)
        pe.wait_ge(*after("rt_taken", 2))
        for n in range(2 * NT):
            mm = pe.matmul(psum[3][0:BLK, 0:BLOCKS + 1], hot_r[:, n], hot_b[:, n], start=n == 0, stop=n == 2 * NT - 1)
        mm.then_inc(sem("rt_pe"), 1)
        stage()

        def rows_T(b, first=False):
            pe.wait_ge(sem("x_rows"), 16 * b + 16)
            if not first:
                pe.wait_ge(sem("x_lo"), b)
            for f in range(KD):
                tr = pe.matmul(psum[2][:, f * BLK:f * BLK + BLK], xg[:, f * P:f * P + P], ident[0:BLK, 0:BLK], start=True, stop=True)
            tr.then_inc(sem("x_T"), 1)

        def three(out, ah, al, k_slot, k, first, last):
            pe.matmul(out, ah, e_hi[k_slot][:, k], start=first, stop=False)
            pe.matmul(out, ah, e_lo[k_slot][:, k], start=False, stop=False)
            return pe.matmul(out, al, e_hi[k_slot][:, k], start=False, stop=last)

        def gate_up(b, first=False):
            if not first:
                pe.wait_ge(sem("e_prod"), b)
            for u in range(4):
                if u == 0:
                    pe.wait_ge(sem("x_lo"), b + 1)
                pe.wait_ge(sem("gu_lo"), 4 * b + u + 1)
                for k in range(4):
                    f = 4 * (u % 2) + k
                    mm = three(psum[u // 2][0:BLK], bT_hi[:, f], bT_lo[:, f], u, k, f == 0, f == KD - 1)
                mm.then_inc(sem("gu_used"), 1)

        def acts_T(b, first=False):
            pe.wait_ge(sem("e_prod"), b + 1)
            if not first:
                pe.wait_ge(sem("h_lo"), b)
            for k in range(FF // P):
                tr = pe.matmul(psum[4][:, k * BLK:k * BLK + BLK], act_h[:, k * P:k * P + P], ident[0:BLK, 0:BLK], start=True, stop=True)
            tr.then_inc(sem("h_T"), 1)

        def down(b, first=False):
            pe.wait_ge(sem("h_lo"), b + 1)
            if not first:
                pe.wait_ge(sem("y_out"), 2 * b)
            for u in range(2):
                pe.wait_ge(sem("d_lo"), 2 * b + u + 1)
                for k in range(4):
                    mm = three(psum[5 + u][0:BLK], aT_hi[:, k], aT_lo[:, k], 4 + u, k, k == 0, k == 3)
                mm.then_inc(sem("d_used"), 1)

        rows_T(0, True)
        gate_up(0, True)
        rows_T(1)
        acts_T(0, True)
        gate_up(1)
        rows_T(2)
        down(0, True)
        acts_T(1)
        with pe.Fori(2, NE - 1) as e:
            gate_up(e)
            rows_T(e + 1)
            down(e - 1)
            acts_T(e)
        gate_up(NE - 1)
        down(NE - 2)
        acts_T(NE - 1)
        down(NE - 1)
        n_over = pe.value_load(over[0:1, OVER:OVER + 1], min_val=0, max_val=OVER)
        with pe.If(n_over > 0):
            with pe.Fori(NE, BLOCKS) as b:
                rows_T(b)
                gate_up(b)
                acts_T(b)
                down(b)

    @block.scalar
    def _(act):
        stage_n = [0]
        next_hi = [0]

        def stage(wait=True):
            stage_n[0] += 1
            act.activation(mark_a[0:1, 0:1], mark_a[0:1, 1:2], ACT.Copy).then_inc(sem("act_stage"), 1)
            if wait:
                together(act, stage_n[0])

        def hi_to(m_end):
            while next_hi[0] < min(m_end, len(split_of)):
                m = next_hi[0]
                n = split_of[m]
                raw_arrived(act, n)
                if m >= SPL:
                    act.wait_ge(sem(unit_free[m - SPL][0]), unit_free[m - SPL][1])
                act.activation(w_hi[m % SPL][:], raw[n % RAW][:], ACT.Copy).then_inc(sem("hi_done"), 1)
                next_hi[0] += 1

        def gemm(ps, evac, ahead=SPL):
            for x, p in enumerate(ps):
                m0 = panels[p]["units"][0]
                hi_to(m0 + 2)
                if x and evac:
                    read(ps[x - 1], x - 1, evac)
                hi_to(m0 + len(panels[p]["units"]))
            if ahead:
                hi_to(next_hi[0] + 1)
            if evac:
                read(ps[-1], len(ps) - 1, evac)
            hi_to(panels[ps[-1]]["units"][-1] + 1 + ahead)

        def read(p, x, evac):
            for j in range(panels[p]["nj"]):
                act.wait_ge(sem("panel_done"), panels[p]["done"] + j + 1)
                ins = evac(x, j, psum[4 * (p % 2) + j])
                if panels[p]["evac"] == "A":
                    ins.then_inc(sem("evac_act"), 1)

        def to(dst, func=ACT.Copy, **kw):
            return lambda x, j, bank: act.activation(dst(x, j), bank[:], func, **kw)

        def norm_rows(name, src, nt=NT, before=None):
            for t in range(nt):
                if before == "final":
                    act.wait_ge(sem("norm_rows"), rows_at["final"] + t + 1)
                elif before == "summed":
                    act.wait_ge(*after("summed", t + 1))
                elif before:
                    act.wait_ge(sem("evac_dve"), panels[before]["at"] + t + 1)
                act.activation((mem_xs if name == "mem" else normed[name])[:, t], src[:, t], ACT.Square,
                               accum_out=col(SS + t)).then_inc(sem("norm_ss"), 1)
            act.wait_ge(sem("norm_var"), norm_at[name] + 1)
            act.activation(col(RS, nt), col(SS, nt), ACT.Sqrt).then_inc(sem("norm_std"), 1)

        def norm_T(name, g, hi, nt=NT):
            for f in range(KD):
                act.wait_ge(sem("norm_T"), feat_at[name] + (f | 1 if name == "mem" else f) + 1)
                bank = norm_bank(name, f)
                act.activation(hi[:, f], bank, ACT.Copy, scale=pcol(g + f)).then_inc(sem("norm_hi"), 1)

        def norm(name, src, g, hi, before=None, ahead=0):
            norm_rows(name, src, before=before)
            hi_to(next_hi[0] + ahead)
            if hi is not None:
                norm_T(name, g, hi)

        act.wait_ge(sem("dve_stage"), 1)
        stage()
        act.wait_ge(sem("x_in"), 16)
        norm_rows("even", resid)
        act.wait_ge(sem("par_T"), 1)
        act.activation(pcol(G_EVEN, KD), psum[0][:, 0:KD], ACT.Copy).then_inc(sem("par_done"), 1)
        hi_to(2)
        norm_T("even", G_EVEN, hT_hi)
        gemm(pn["f_in"], to(lambda x, j: finT[:, 4 * x + j]))
        stage()
        for i in range(0, GROUPS * NT // 2, 2):
            act.wait_ge(sem("z_done"), i + 1)
            for dst, src in z_parts(i):
                act.activation(dst, src, ACT.Copy).then_inc(sem("z_act"), 1)
        for k, (r, n, c) in enumerate(((KD, 104 - KD, KD), (0, 128, PAR1), (0, 96, PAR2))):
            act.wait_ge(sem("par_T"), k + 2)
            act.activation(pcol(c, n), psum[5 + k][:, r:r + n], ACT.Copy).then_inc(sem("par_done"), 1)
        act.wait_ge(sem("lam_abs"), 1)
        act.activation(col(T1, 32), col(T0, 32), ACT.Exp, scale=-1.0).then_inc(sem("lam_exp"), 1)
        act.wait_ge(sem("lb_diff"), 1)
        act.activation(col(T3, 8), col(T2, 8), ACT.Sigmoid).then_inc(sem("lb_sig"), 1)
        for i in range(KD):
            act.wait_ge(sem("y_done"), i + 1)
            act.activation(y_odd[:, i], psum[i][:, HS + 1:SEQ], ACT.Copy).then_inc(sem("y_odd"), 1)
        stage()
        gemm(pn["f_gate"], to(lambda x, j: fgate[:, 4 * x + j], ACT.Silu))
        for i in range(KD):
            act.wait_ge(sem("fw_prod"), i + 1)
            act.activation(mixf_hi[:, i], fgate[:, i], ACT.Copy).then_inc(sem("fw_hi"), 1)
        stage()

        def qkv_out(x, j, bank):
            for h in range(4 if x < 2 else NKV):
                n = j * (NQ + NKV) + 4 * x + h
                act.activation(squares[n // 32][:, n % 32], bank[:, h * HD:h * HD + HD], ACT.Square, accum_out=col(ST + n))
            return act.activation(q_tok[:, j, x * 512:x * 512 + 512] if x < 2 else kv_tok[:, j], bank[:], ACT.Copy)
        gemm(pn["qkv"], qkv_out)
        act.wait_ge(sem("qk_var"), 1)
        act.activation(col(ST, 40), col(ST, 40), ACT.Sqrt).then_inc(sem("qk_std"), 1)
        gemm(pn["a_gate"], to(lambda x, j: agate[:, 4 * x + j], ACT.Silu))
        stage(wait=False)
        for i in range(3 * NT):
            act.wait_ge(sem("qkT_done"), i + 1)
            t, hg = i // 3, i % 3
            n = min(4, NQ + NKV - 4 * hg)
            act.activation(qkT[:, 4 * hg:4 * hg + n, t * P:t * P + P],
                           qkT_bank(i)[:, 0:n * P].rearrange("p (h s) -> p h s", s=P), ACT.Copy).then_inc(sem("qkT_act"), 1)
        stage()
        n_i = NQ * NT

        def evac(i):
            h, t = i // NT, i % NT
            act.wait_ge(sem("at_tr"), i + 1)
            if h >= 2:
                act.wait_ge(sem("at_av"), h - 1)
            act.activation(pT[h % 2][:, :, t * P:t * P + P], psum[4 + i % 2][:].rearrange("p (k s) -> p k s", s=P),
                           ACT.Copy).then_inc(sem("at_pT"), 1)

        def head_hi(h):
            act.wait_ge(sem("at_prod"), h + 1)
            act.activation(mixa_hi[:, h], agate[:, h], ACT.Copy).then_inc(sem("at_hi"), 1)

        for i in range(n_i):
            act.wait_ge(sem("at_max"), i + 1)
            if i >= 4:
                act.wait_ge(sem("at_tr"), i - 3)
            act.activation(probs[i % 4][:], psum[i % 4][:], ACT.Exp, bias=col(T0 + i % 32), scale=HD ** -0.5,
                           accum_out=col(SUMS + i)).then_inc(sem("at_exp"), 1)
            if i >= 2:
                evac(i - 2)
            if i % NT == 0 and i >= 2 * NT:
                head_hi(i // NT - 2)
        evac(n_i - 2)
        evac(n_i - 1)
        head_hi(NQ - 2)
        head_hi(NQ - 1)
        stage()
        gemm(pn["even_out"], None, ahead=1)
        stage(wait=False)
        norm("odd", resid, G_ODD, hT_hi, before=pn["even_out"][-1], ahead=1)

        def conv_base(x, j, bank):
            f = 4 * x + j
            return act.activation(xc[:, f], bank[:], ACT.Identity, scale=pcol(CONV_W + 2 * RB + f),
                                  bias=pcol(CONV_B + f)).then_inc(sem("conv_base"), 1)
        gemm(pn["xr"], conv_base)
        gemm(pn["r_gate"], to(lambda x, j: rgate[:, 4 * x + j], ACT.Silu), ahead=0)
        stage()

        def rnn_hi(k):
            act.wait_ge(sem("rg_prod"), 4 * k + 4)
            act.activation(rp_hi[:, 4 * k:4 * k + 4], rgate[:, 4 * k:4 * k + 4], ACT.Copy).then_inc(sem("rp_hi"), 1)

        for b in range(2 * RB // BATCH):
            its = range(BATCH * b, BATCH * b + BATCH)
            for it in its:
                blk, d = it // 2, it % 2
                for g, dst in enumerate((rr, ri)):
                    act.wait_ge(sem("gate_done"), 2 * it + g + 1)
                    if b >= 2:
                        act.wait_ge(sem("rg_prod"), blk - BATCH + 1)
                    act.activation(dst[:, it % 8], psum[(2 * it + g) % 8][:], ACT.Sigmoid,
                                   bias=pcol((GATE_AB, GATE_XB)[g] + d * RB + blk)).then_inc(sem("gate_sig"), 1)
            for it in its:
                blk, d = it // 2, it % 2
                act.wait_ge(sem("gate_sig"), 2 * it + 1)
                act.activation(rt[:, it % 8], rr[:, it % 8], ACT.Tanh, scale=col(HALF + d * RB + blk)).then_inc(sem("rg_tanh"), 1)
            for it in its:
                blk, d = it // 2, it % 2
                act.wait_ge(sem("rg_tanh"), it + 1)
                act.activation(rr[:, it % 8], rr[:, it % 8], ACT.Exp, scale=col(DECAY + d * RB + blk)).then_inc(sem("rg_a"), 1)
            if b >= 2 and b % 2 == 0:
                rnn_hi(b // 2 - 1)
            if b == 6:
                hi_to(next_hi[0] + SPL)
            act.wait_ge(sem("rg_floor"), b + 1)
            quad = rt[:, its[0] % 8:its[0] % 8 + BATCH]
            act.activation(quad, quad, ACT.Sqrt).then_inc(sem("rg_sqrt"), 1)
        hi_to(next_hi[0] + 1)
        rnn_hi(RB // 4 - 1)
        stage(wait=False)
        gemm(pn["odd_out"], None, ahead=1)
        stage(wait=False)
        norm("final", resid, None, None, before=pn["odd_out"][-1], ahead=1)
        norm("mix", resid, G_MIX, hT_hi, before="final")

        def silu2(x):
            last = panels[pn["qkv2"][x]]
            act.wait_ge(sem("evac_dve"), last["at"] + last["nj"])
            qs = qkvT[:, 4 * x:4 * x + 4]
            act.activation(qs, qs, ACT.Silu).then_inc(sem("silu2"), 1)
            if x == 2:
                act.wait_ge(sem("w_ab_in"), 16)
                act.activation(wab_hi[:], w_ab[:], ACT.Copy).then_inc(sem("ab_hi"), 1)

        def conv2_base(x, j, bank):
            if j == 0 and x:
                silu2(x - 1)
            f = 4 * x + j
            return act.activation(qkvT[:, f], bank[:], ACT.Copy, scale=pcol(CONV2 + 72 + f)).then_inc(sem("conv2_base"), 1)
        gemm(pn["qkv2"], conv2_base)
        act.wait_ge(sem("ab_done"), 1)
        act.activation(ab_rows[:], psum[ab_base][0:2 * HEADS], ACT.Copy).then_inc(sem("ab_act"), 1)
        silu2(5)
        act.wait_ge(sem("ab_done"), 2)
        act.activation(col(ABC, 64), psum[ab_base + 1][:, 0:64], ACT.Copy).then_inc(sem("ab_act"), 1)
        stage()
        ab = col(ABC, 64).rearrange("p (t x) -> p t x", x=2 * HEADS)
        act.wait_ge(*after("late_in", 80))
        act.activation(col(BETA, 32).rearrange("p (t h) -> p t h", h=HEADS), ab[:, :, HEADS:], ACT.Sigmoid).then_inc(sem("g_act"), 1)
        act.activation(col(T3, 8), gdn_par[:, 0], ACT.Exp).then_inc(sem("g_act"), 1)
        act.wait_ge(*after("g_abs", 1))
        act.activation(col(T1, 32), col(T1, 32), ACT.Exp, scale=-1.0).then_inc(sem("g_act"), 1)
        act.wait_ge(*after("l2_var", 1))
        act.activation(col(L2, 64), col(L2, 64), ACT.Sqrt).then_inc(sem("l2_std"), 1)
        act.wait_ge(*after("g_cum", 2))
        act.activation(col(ECUM, 32), psum[ab_base][:, 0:32], ACT.Exp).then_inc(sem("g_ecum"), 1)
        act.activation(col(EREST, 32), psum[ab_base + 1][:, 0:32], ACT.Exp).then_inc(sem("g_ecum"), 1)
        EE = range(4)

        def gbank(e, b, at=0, n=256):
            return psum[2 * e + b][:, at:at + n].rearrange("p (x c j) -> p x c j", c=2, j=P) if n == 512 \
                else psum[2 * e + b][:, at:at + n].rearrange("p (c j) -> p c j", j=P)

        act.wait_ge(sem("hT_saved"), 16)
        for n in range(0, 2 * HEADS, 4):
            for e in EE:
                act.wait_ge(sem("g_gram"), n + e + 1)
                act.activation(gs[e][0][:], gbank(e, 0), ACT.Exp).then_inc(sem("g_EB"), 1)
            for e in EE:
                act.wait_ge(sem("g_D"), 2 * (n + e) + 2)
                act.activation(gs[e][2][:], gs[e][2][:], ACT.Exp, scale=-1.0).then_inc(sem("g_dec"), 1)
                act.activation(gs[e][1][:], gs[e][1][:], ACT.Exp).then_inc(sem("g_dec"), 1)
            for e in EE:
                act.wait_ge(sem("g_2pe"), n + e + 1)
                act.activation(nm2[e][:], gbank(e, 1, 0, 512), ACT.Copy).then_inc(sem("g_2"), 1)
            for e in EE:
                act.wait_ge(sem("g_4pe"), n + e + 1)
                act.wait_ge(sem("g_R1"), n + e + 1)
                act.activation(nm16[e][:], gbank(e, 0, 0, 512), ACT.Copy).then_inc(sem("g_4"), 1)
            for e in EE:
                act.wait_ge(sem("g_R4"), n + e + 1)
                act.activation(nm2[e][:, 0], gbank(e, 0, 256), ACT.Copy).then_inc(sem("g_8"), 1)
            for lv in range(3):
                for e in EE:
                    act.wait_ge(sem(f"g_TYpe{lv}"), n + e + 1)
                    act.activation(nm2[e][:], gbank(e, 0, 0, 512), ACT.Copy).then_inc(sem(f"g_TY{lv}"), 1)
            for e in EE:
                act.wait_ge(sem("g_uwpe"), n + e + 1)
                h, half = (n + e) // 2, e % 2
                act.activation(u_tok[:, 2 * half:2 * half + 2, h], gbank(e, 1), ACT.Copy).then_inc(sem("g_uw"), 1)
                act.activation(qkvT[:, HEADS + h, 256 * half:256 * half + 256], psum[2 * e + 1][:, 256:512], ACT.Copy).then_inc(sem("g_uw"), 1)
        stage()
        for t in range(NT):
            for hg in range(2):
                act.wait_ge(*after("s_ope", 2 * t + hg + 1))
                act.activation(u_tok[:, t, 4 * hg:4 * hg + 4], psum[2 + hg][:].rearrange("p (h d) -> p h d", d=P),
                               ACT.Copy).then_inc(sem("s_o"), 1)

        def branch(b, w_panels):
            act.wait_ge(sem("o_var"), 1 + (1 if b == "b" else 0))
            act.activation(col(ST, 32), col(ST, 32), ACT.Sqrt).then_inc(sem("o_std"), 1)
            gemm(pn["og_" + b], to(lambda x, j: og[:, j, x * 512:x * 512 + 512], ACT.Silu))
            dst = merged if b == "a" else gate_b
            gate = pn["gate_" + b]
            gemm(gate[0:1], to(lambda x, j: dst[:, j], ACT.Sigmoid), ahead=1)
            for f in range(KD):
                if f == 4:
                    hi_to(next_hi[0] + 1)
                act.wait_ge(sem("y_T"), f + 1 + (KD if b == "b" else 0))
                act.activation(y_hi[:, f], psum[4 * (gate[1 - f // 4] % 2) + f % 4][:], ACT.Copy).then_inc(sem("y_hi"), 1)
            gemm(gate[1:2], to(lambda x, j: dst[:, 4 + j], ACT.Sigmoid))
            gemm(w_panels, None, ahead=SPL if b == "a" else 1)
            if b == "b":
                last = panels[w_panels[0]]
                for k in range(2):
                    act.wait_ge(sem("evac_dve"), last["at"] + 4 * k + 4)
                    act.activation(mg_hi[:, 4 * k:4 * k + 4], merged[:, 4 * k:4 * k + 4], ACT.Copy).then_inc(sem("mg_hi"), 1)
                hi_to(next_hi[0] + 1)

        stage()
        branch("a", pn["br_a"])
        stage()
        def exps(hs):
            for h in hs:
                act.wait_ge(*after("h_q", h + 1))
                act.activation(hexp[:, h], hcum[:, h], ACT.Exp, scale=-1.0).then_inc(sem("h_en"), 1)
            for h in hs:
                act.wait_ge(*after("h_d", h + 1))
                act.activation(hcum[:, h], hcum[:, h], ACT.Exp).then_inc(sem("h_ed"), 1)

        H8 = range(HEADS)
        gemm(pn["f"], to(lambda x, j: forget[:, 4 * x + j], ACT.Sigmoid))
        for h in H8:
            act.wait_ge(*after("h_f", h + 1))
            act.activation(hexp[:, h], forget[:, h], ACT.Ln).then_inc(sem("h_ln"), 1)
        for h in H8:
            act.wait_ge(*after("h_cum", h + 1))
            act.activation(hexp[:, h], hcum[:, h], ACT.Exp).then_inc(sem("h_e"), 1)
            act.activation(col(DEC8 + 8 * h, 8), hcum[:, h, QC - 1::QC], ACT.Exp).then_inc(sem("h_dec"), 1)
        gemm(pn["q"], to(lambda x, j: hqT[:, 4 * x + j], ACT.Copy, scale=HD ** -0.5))
        exps(H8[0:4])
        hi_to(next_hi[0] + 2)
        exps(H8[4:8])
        gemm(pn["i"], to(lambda x, j: hv[:, j, x * 512:x * 512 + 512]))
        for h in H8:
            act.wait_ge(sem("h_kdT"), h + 1)
            act.activation(hkd[:, h], psum[h][:].rearrange("p (t d) -> p t d", d=P), ACT.Copy).then_inc(sem("h_kdev"), 1)
        stage()
        for t in range(NT):
            for hg in range(2):
                act.wait_ge(*after("hs_ope", 2 * t + hg + 1))
                act.activation(hintra[:, t, 4 * hg:4 * hg + 4], psum[4 + 2 * (t % 2) + hg][:].rearrange("p (h d) -> p h d", d=P),
                               ACT.Copy).then_inc(sem("hs_o"), 1)
        stage()
        branch("b", pn["br_b"])
        stage()
        act.wait_ge(*after("mem_in", 16))
        norm_rows("mem", mem_tok, MEM // P)
        gemm(pn["mix_out"], None, ahead=1)
        stage(wait=False)
        norm_T("mem", G_MEM, memT_hi, MEM // P)
        hi_to(next_hi[0] + 1)
        last = panels[pn["mix_out"][-1]]
        act.wait_ge(sem("evac_dve"), last["at"] + last["nj"])
        norm_rows("x", resid)
        gemm(pn["xk"], lambda x, j, bank: act.activation(xkT[:, 4 * x + j], bank[:, 0:MEM], ACT.Copy))
        gemm(pn["xv"], to(lambda x, j: xv[:, j, x * 512:x * 512 + 512]))
        norm_T("x", G_X, hT_hi)
        gemm(pn["xq"], to(lambda x, j: xqT[:, 4 * x + j]))
        stage()
        n_x = XH * NT

        def xevac(i):
            h, t = i // NT, i % NT
            act.wait_ge(*after("xa_tr", i + 1))
            if h >= 2:
                act.wait_ge(*after("xa_av", 2 * (h - 2) + 2))
            act.activation(xpT[h % 2][:, :, t * P:t * P + P], psum[4 + i % 2][:, 0:MEM].rearrange("p (k s) -> p k s", s=P),
                           ACT.Copy).then_inc(sem("xa_pT"), 1)

        def xhead_hi(h):
            for c in range(2):
                act.wait_ge(*after("xa_av", 2 * h + c + 1))
                act.activation(xo_hi[:, 2 * h + c], psum[6 + c][:], ACT.Copy).then_inc(sem("xa_hi"), 1)

        for i in range(n_x):
            act.wait_ge(*after("xa_max", i + 1))
            if i >= 4:
                act.wait_ge(*after("xa_tr", i - 3))
            act.activation(xprobs[i % 4][:], psum[i % 4][:, 0:MEM], ACT.Exp, bias=col(T0 + i), scale=XD ** -0.5,
                           accum_out=col(SUMS + i)).then_inc(sem("xa_exp"), 1)
            if i >= 2:
                xevac(i - 2)
            if i % NT == 3 and i >= NT:
                xhead_hi(i // NT - 1)
        xevac(n_x - 2)
        xevac(n_x - 1)
        xhead_hi(XH - 1)
        stage()
        gemm(pn["xo"], None)
        def gu_hi(b, us, first=False):
            for u in us:
                act.wait_ge(*after(f"e_in{u}", 16 * b + 16))
                if not first:
                    act.wait_ge(sem("gu_used"), 4 * b + (u - 3))
                act.activation(e_hi[u][:], eraw[u][:], ACT.Copy).then_inc(sem("gu_hi"), 1)

        stage(wait=False)
        norm("ffn", resid, None, None, before=pn["xo"][-1])
        gu_hi(0, range(3), True)
        for f in range(KD):
            act.wait_ge(*after("hnT_pe", f + 1))
            act.activation(hnT[:, f], psum[f][:], ACT.Copy).then_inc(sem("hnT_act"), 1)
        act.wait_ge(*after("rt_exp", 1))
        act.activation(logits[:, :, 0:NG], logits[:, :, 0:NG], ACT.Exp).then_inc(sem("rt_act"), 1)
        act.wait_ge(*after("rt_exp", 2))
        act.activation(weight[:, 1], weight[:, 1], ACT.Exp).then_inc(sem("rt_act"), 1)
        stage()

        def d_hi(b, u, first=False):
            act.wait_ge(*after(f"e_in{4 + u}", 16 * b + 16))
            if not first:
                act.wait_ge(sem("d_used"), 2 * b + (u - 1))
            act.activation(e_hi[4 + u][:], eraw[4 + u][:], ACT.Copy).then_inc(sem("d_hi"), 1)

        def silu_of_gate(b, first=False):
            act.wait_ge(sem("gu_used"), 4 * b + 2)
            if not first:
                act.wait_ge(sem("e_prod"), b)
            act.activation(silu_g[:], psum[0][0:BLK], ACT.Silu).then_inc(sem("e_silu"), 1)

        def x_hi(b, first=False):
            act.wait_ge(sem("x_T"), b + 1)
            if not first:
                act.wait_ge(sem("gu_used"), 4 * b)
            act.activation(bT_hi[:], psum[2][:].rearrange("p (k r) -> p k r", r=BLK), ACT.Copy).then_inc(sem("x_hi"), 1)

        def h_hi(b, first=False):
            act.wait_ge(sem("h_T"), b + 1)
            if not first:
                act.wait_ge(sem("d_used"), 2 * b)
            act.activation(aT_hi[:], psum[4][:, 0:FF // P * BLK].rearrange("p (k r) -> p k r", r=BLK), ACT.Copy).then_inc(sem("h_hi"), 1)

        def y_half(b, u, first=False):
            act.wait_ge(sem("d_used"), 2 * b + u + 1)
            if not first:
                act.wait_ge(sem("y_saved"), 16 * b)
            act.activation(y_rows[:, 512 * u:512 * u + 512], psum[5 + u][0:BLK], ACT.Copy).then_inc(sem("y_out"), 1)

        def y_save(b):
            act.wait_ge(sem("y_out"), 2 * b + 2)
            act.dma_start(y_dram[bass.ds(b * BLK, BLK)], y_rows[:]).then_inc(sem("y_saved"), 16)

        def step(e, y=True, first=False, ahead=True, last_first=False):
            if ahead:
                gu_hi(e + 1, (0, 1))
            silu_of_gate(e, first)
            if ahead:
                gu_hi(e + 1, (2, 3))
                x_hi(e + 1)
            d_hi(e, 0, first)
            if y:
                y_half(e - 1, 0, last_first)
            d_hi(e, 1, first)
            if y:
                y_half(e - 1, 1, last_first)
            h_hi(e, first)
            if y:
                y_save(e - 1)

        act.wait_ge(sem("hn_saved"), 16)
        gu_hi(0, (3,), True)
        x_hi(0, True)
        step(0, y=False, first=True)
        step(1, last_first=True)
        with act.Fori(2, NE - 1) as e:
            step(e)
        step(NE - 1, ahead=False)
        for u in range(2):
            y_half(NE - 1, u)
        y_save(NE - 1)
        n_over = act.value_load(over[0:1, OVER:OVER + 1], min_val=0, max_val=OVER)
        with act.If(n_over > 0):
            with act.Fori(NE, BLOCKS) as b:
                gu_hi(b, range(4))
                x_hi(b)
                silu_of_gate(b)
                for u in range(2):
                    d_hi(b, u)
                h_hi(b)
                for u in range(2):
                    y_half(b, u)
                y_save(b)
        stage()
        norm("last", resid, None, None, before="summed")

    @block.vector
    def _(dve):
        own = Chain(dve, "dve_own")
        stage_n = [0]
        next_lo = [0]

        def stage(wait=True):
            stage_n[0] += 1
            dve.memset(mark_d[0:1, 0:1], 0.0).then_inc(sem("dve_stage"), 1)
            if wait:
                together(dve, stage_n[0])

        def lo_to(m_end):
            while next_lo[0] < min(m_end, len(split_of)):
                m = next_lo[0]
                dve.wait_ge(sem("hi_done"), m + 1)
                dve.tensor_tensor(w_lo[m % SPL][:], raw[split_of[m] % RAW][:], f32(w_hi[m % SPL][:]),
                                  ALU.subtract).then_inc(sem("lo_done"), 1)
                next_lo[0] += 1

        def gemm(ps, evac, ahead=SPL, before_last=None):
            for x, p in enumerate(ps):
                m0 = panels[p]["units"][0]
                lo_to(m0 + 2)
                if x and evac:
                    read(ps[x - 1], x - 1, evac)
                lo_to(m0 + len(panels[p]["units"]))
            if ahead:
                lo_to(next_lo[0] + 1)
            if before_last:
                before_last()
            if evac:
                read(ps[-1], len(ps) - 1, evac)
            lo_to(panels[ps[-1]]["units"][-1] + 1 + ahead)

        def read(p, x, evac):
            for j in range(panels[p]["nj"]):
                dve.wait_ge(sem("panel_done"), panels[p]["done"] + j + 1)
                evac(x, j, psum[4 * (p % 2) + j]).then_inc(sem("evac_dve"), 1)

        def add_to(dst):
            def evac(x, j, bank):
                d = dst[:, j, x * 512:x * 512 + 512]
                return dve.tensor_tensor(d, bank[:], d, ALU.add)
            return evac

        def norm_rows(name, src, nt=NT, rows=None, gain=None):
            out = rows if rows is not None else (mem_xs if name == "mem" else normed[name])
            dve.wait_ge(sem("norm_ss"), rows_at[name] + nt)
            dve.tensor_scalar(col(SS, nt), col(SS, nt), 1.0 / D, EPS, ALU.mult, ALU.add).then_inc(sem("norm_var"), 1)
            dve.wait_ge(sem("norm_std"), norm_at[name] + 1)
            own.link(dve.reciprocal(col(RS, nt), col(RS, nt)))
            for t in range(nt):
                if gain is None:
                    ins = dve.tensor_scalar(out[:, t], src[:, t], col(RS + t), None, ALU.mult)
                else:
                    ins = dve.scalar_tensor_tensor(out[:, t], src[:, t], col(RS + t), gain[:], ALU.mult, ALU.mult)
                ins.then_inc(sem("norm_rows"), 1)

        def norm_T(name, g, hi, lo, nt=NT):
            for f in range(KD):
                dve.wait_ge(sem("norm_hi"), feat_at[name] + (f | 1 if name == "mem" else f) + 1)
                bank = norm_bank(name, f)
                dve.scalar_tensor_tensor(lo[:, f], bank, pcol(g + f), f32(hi[:, f]), ALU.mult, ALU.subtract).then_inc(sem("norm_lo"), 1)

        def norm(name, src, g, hi, lo, ahead=0, **kw):
            norm_rows(name, src, **kw)
            lo_to(next_lo[0] + ahead)
            if hi is not None:
                norm_T(name, g, hi, lo)

        def softplus(z, e, out, tmp, n):
            own.link(dve.tensor_scalar(tmp, e, 2.0, None, ALU.add))
            own.link(dve.reciprocal(tmp, tmp))
            own.link(dve.tensor_tensor(e, e, tmp, ALU.mult))
            own.link(dve.tensor_tensor(tmp, e, e, ALU.mult))
            own.link(dve.tensor_scalar(out, tmp, 1.0 / 17, None, ALU.mult))
            for k in (15, 13, 11, 9, 7, 5, 3):
                own.link(dve.scalar_tensor_tensor(out, out, 1.0 / k, tmp, ALU.add, ALU.mult))
            own.link(dve.scalar_tensor_tensor(out, out, 1.0, e, ALU.add, ALU.mult))
            own.link(dve.tensor_scalar(tmp, z, 0.0, None, ALU.max))
            own.link(dve.scalar_tensor_tensor(out, out, 2.0, tmp, ALU.mult, ALU.add))

        own(dve.memset(mark_d[:], 0.0))
        own(dve.memset(mark_a[:], 0.0))
        own(dve.memset(small[:], 0.0))
        own(dve.memset(zz[:, :, :, :, 1, 0:1], 0.0))
        own.wait()
        stage()
        dve.wait_ge(sem("x_in"), 16)
        norm_rows("even", resid)
        lo_to(2)
        dve.wait_ge(sem("par_done"), 1)
        norm_T("even", G_EVEN, hT_hi, hT_lo)
        gemm(pn["f_in"], None)
        stage()
        for i in range(1, GROUPS * NT // 2, 2):
            dve.wait_ge(sem("z_done"), i + 1)
            for dst, src in z_parts(i):
                dve.tensor_copy(dst, src).then_inc(sem("z_dve"), 1)
        dve.wait_ge(sem("par_done"), 4)
        dve.scalar_tensor_tensor(col(T0, 32), pcol(LAM, 32), -1.0, pcol(LAM, 32), ALU.mult, ALU.max).then_inc(sem("lam_abs"), 1)
        dve.tensor_tensor(col(T2, 8), pcol(LB, 8), pcol(LB + 8, 8), ALU.subtract).then_inc(sem("lb_diff"), 1)
        dve.wait_ge(sem("lam_exp"), 1)
        own.link(dve.tensor_scalar(col(T0, 32), pcol(LAM, 32), -1.0, None, ALU.mult))
        softplus(col(T0, 32), col(T1, 32), col(DECAY, 32), col(HALF, 32), 32)
        own.link(dve.tensor_scalar(col(HALF, 32), col(DECAY, 32), 4.0, None, ALU.mult))
        own.link(dve.tensor_scalar(col(DECAY, 32), col(DECAY, 32), -8.0, None, ALU.mult))
        dve.wait_ge(sem("lb_sig"), 1)
        own.link(dve.tensor_copy(col(LBC, 8), col(T3, 8)))
        own.link(dve.tensor_scalar(col(OML, 8), col(T3, 8), -1.0, 1.0, ALU.mult, ALU.add))
        for i in range(KD):
            dve.wait_ge(sem("y_odd"), i + 1)
            even, odd = psum[i][:, 1:HS], y_odd[:, i]
            s, back = slice(1, HS), slice(SEQ - 1, HS, -1)
            plus, minus = (s, back) if i % 2 == 0 else (back, s)
            dve.tensor_tensor(ymixT[:, i, plus], even, odd, ALU.add)
            dve.tensor_tensor(ymixT[:, i, minus], even, odd, ALU.subtract)
            dve.tensor_copy(ymixT[:, i, 0:SEQ:HS], psum[i][:, 0:HS + 1:HS])
        stage()
        gemm(pn["f_gate"], None)
        for i in range(KD):
            dve.wait_ge(sem("fw_done"), i + 1)
            dve.tensor_tensor(fgate[:, i], psum[i][:], fgate[:, i], ALU.mult).then_inc(sem("fw_prod"), 1)
        for i in range(KD):
            dve.wait_ge(sem("fw_hi"), i + 1)
            dve.tensor_tensor(mixf_lo[:, i], fgate[:, i], f32(mixf_hi[:, i]), ALU.subtract)
        stage()
        gemm(pn["qkv"], None)
        last = panels[pn["qkv"][-1]]
        dve.wait_ge(sem("evac_act"), last["at"] + last["nj"])
        dve.tensor_scalar(col(ST, 40), col(ST, 40), 1.0 / HD, EPS, ALU.mult, ALU.add).then_inc(sem("qk_var"), 1)
        parts = [(q_tok, 0, NQ, 0), (kv_tok, NQ, NKV, 1)]
        dve.wait_ge(sem("qk_std"), 1)
        own.link(dve.reciprocal(col(ST, 40), col(ST, 40)))
        dve.wait_ge(sem("gain_in"), 32)
        dve.wait_ge(sem("rope_in"), 16)
        for t in range(NT):
            if t in (1, 2):
                lo_to(next_lo[0] + 1)
            for buf, h0, n, gi in parts:
                x = buf[:, t, 0:n * HD].rearrange("p (h d) -> p h d", d=HD)
                rs = col(ST + t * 10 + h0, n).unsqueeze(2).to_broadcast([P, n, HD])
                own.link(dve.tensor_tensor(x, x, rs, ALU.mult))
                own.link(dve.tensor_tensor(x, x, qk_gain[:, gi:gi + 1].to_broadcast([P, n, HD]), ALU.mult))
                own(dve.tensor_tensor(rot1[:, 0:n], x, rope[:, 0, t:t + 1].to_broadcast([P, n, HD]), ALU.mult))
                for ax in range(4):
                    a, o = ax * 32, (ax ^ 1) * 32
                    own(dve.tensor_tensor(rot2[:, 0:n, a:a + 32], x[:, :, o:o + 32],
                                          rope[:, 1, t:t + 1, a:a + 32].to_broadcast([P, n, 32]), ALU.mult))
                own.wait()
                last = dve.tensor_tensor(x, rot1[:, 0:n], rot2[:, 0:n], ALU.add)
                if gi == 0:
                    own(last)
            last.then_inc(sem("rope_done"), 1)
        gemm(pn["a_gate"], None)
        stage()
        stage()
        n_i = NQ * NT

        def row_max(i):
            dve.wait_ge(sem("at_sc"), i + 1)
            own.link(dve.tensor_reduce(col(T0 + i % 32), psum[i % 4][:], AX.X, ALU.max))
            dve.tensor_scalar(col(T0 + i % 32), col(T0 + i % 32), -HD ** -0.5, None, ALU.mult).then_inc(sem("at_max"), 1)

        def head_product(h):
            dve.wait_ge(sem("at_av"), h + 1)
            dve.tensor_tensor(agate[:, h], psum[6 + h % 2][:], agate[:, h], ALU.mult).then_inc(sem("at_prod"), 1)

        def head_lo(h):
            dve.wait_ge(sem("at_hi"), h + 1)
            dve.tensor_tensor(mixa_lo[:, h], agate[:, h], f32(mixa_hi[:, h]), ALU.subtract)

        row_max(0)
        row_max(1)
        for i in range(n_i):
            if i + 2 < n_i:
                row_max(i + 2)
            dve.wait_ge(sem("at_exp"), i + 1)
            own.link(dve.reciprocal(col(SUMS + i), col(SUMS + i)))
            dve.tensor_scalar(probs[i % 4][:], probs[i % 4][:], col(SUMS + i), None, ALU.mult).then_inc(sem("at_norm"), 1)
            if i % NT == 3 and i >= NT:
                head_product(i // NT - 1)
            if i % NT == 1 and i >= 2 * NT:
                head_lo(i // NT - 2)
        head_product(NQ - 1)
        head_lo(NQ - 2)
        head_lo(NQ - 1)
        stage()
        gemm(pn["even_out"], add_to(resid), ahead=1)
        stage(wait=False)
        norm("odd", resid, G_ODD, hT_hi, hT_lo, ahead=1)

        def conv(x, j, bank):
            f = 4 * x + j
            dve.wait_ge(sem("conv_base"), f + 1)
            def tap(n, dst, src):
                return dve.scalar_tensor_tensor(xc[:, f, dst], bank[:, src], pcol(CONV_W + n * RB + f), xc[:, f, dst],
                                                ALU.mult, ALU.add)
            own.link(tap(0, slice(2, SEQ), slice(0, SEQ - 2)))
            own.link(tap(1, slice(1, SEQ), slice(0, SEQ - 1)))
            return tap(3, slice(0, SEQ - 1), slice(1, SEQ))
        gemm(pn["xr"], conv)
        gemm(pn["r_gate"], None, ahead=0)
        stage()

        def rnn_lo(k):
            dve.wait_ge(sem("rp_hi"), k + 1)
            dve.tensor_tensor(rp_lo[:, 4 * k:4 * k + 4], rgate[:, 4 * k:4 * k + 4], f32(rp_hi[:, 4 * k:4 * k + 4]),
                              ALU.subtract).then_inc(sem("rp_lo"), 1)

        for b in range(2 * RB // BATCH):
            its = range(BATCH * b, BATCH * b + BATCH)
            quad = rt[:, its[0] % 8:its[0] % 8 + BATCH]
            dve.wait_ge(sem("rg_tanh"), its[-1] + 1)
            dve.tensor_scalar(quad, quad, 1e-34, None, ALU.max).then_inc(sem("rg_floor"), 1)
            if b >= 2 and b % 2 == 0:
                rnn_lo(b // 2 - 1)
            if b == 6:
                lo_to(next_lo[0] + SPL)
            for it in its:
                a, u, h = rr[:, it % 8], rt[:, it % 8], ri[:, it % 8]
                dve.wait_ge(sem("rg_sqrt"), b + 1)
                dve.wait_ge(sem("rg_a"), it + 1)
                own(dve.scalar_tensor_tensor(u, a, 1.0, u, ALU.add, ALU.mult))
                own.wait()
                dve.wait_ge(sem("ix"), it + 1)
                own.link(dve.tensor_tensor(u, u, h, ALU.mult))
                back = slice(None, None, -1) if it % 2 else slice(None)
                own(dve.tensor_tensor_scan(h[:, back], a[:, back], u[:, back], 0.0, ALU.mult, ALU.add))
                if it % 2:
                    own.wait()
                    own.link(dve.tensor_tensor(h, h, ri[:, it % 8 - 1], ALU.add))
                    dve.tensor_tensor(rgate[:, it // 2], rgate[:, it // 2], h, ALU.mult).then_inc(sem("rg_prod"), 1)
                if it == 2 * RB - 3:
                    lo_to(next_lo[0] + 1)
        rnn_lo(RB // 4 - 1)
        stage(wait=False)
        gemm(pn["odd_out"], add_to(resid), ahead=1)
        stage(wait=False)
        dve.wait_ge(*after("final_in", 16))
        norm("final", resid, None, None, None, rows=resid, gain=final_gain)
        norm("mix", resid, G_MIX, hT_hi, hT_lo, ahead=1)

        def conv2(x, j, bank):
            f = 4 * x + j
            if f == 16:
                dve.wait_ge(sem("ab_hi"), 1)
                dve.tensor_tensor(wab_lo[:], w_ab[:], f32(wab_hi[:]), ALU.subtract).then_inc(sem("ab_lo"), 1)
            dve.wait_ge(sem("conv2_base"), f + 1)
            for back in (1, 2, 3):
                ins = dve.scalar_tensor_tensor(qkvT[:, f, back:SEQ], bank[:, 0:SEQ - back], pcol(CONV2 + (3 - back) * 24 + f),
                                               qkvT[:, f, back:SEQ], ALU.mult, ALU.add)
                if back < 3:
                    own.link(ins)
            return ins
        gemm(pn["qkv2"], conv2)
        dve.wait_ge(*after("h_saved", 16))
        stage()
        dve.wait_ge(*after("late_in", 80))
        dve.wait_ge(sem("ab_act"), 2)
        ab = col(ABC, 64).rearrange("p (t x) -> p t x", x=2 * HEADS)

        def th(c):
            return col(c, 32).rearrange("p (t h) -> p t h", h=HEADS)

        own.link(dve.tensor_tensor(th(T0), ab[:, :, 0:HEADS], gdn_par[:, 1:2].to_broadcast([P, NT, HEADS]), ALU.add))
        dve.scalar_tensor_tensor(col(T1, 32), col(T0, 32), -1.0, col(T0, 32), ALU.mult, ALU.max).then_inc(sem("g_abs"), 1)
        dve.wait_ge(*after("g_act", 3))
        softplus(col(T0, 32), col(T1, 32), col(GG, 32), col(T2, 32), 32)
        own.link(dve.scalar_tensor_tensor(th(GG), th(GG), -1.0, col(T3, 8).unsqueeze(1).to_broadcast([P, NT, HEADS]),
                                          ALU.mult, ALU.mult))
        own(dve.tensor_scalar(col(NBETA, 32), col(BETA, 32), -1.0, None, ALU.mult))
        dve.tensor_copy(col(T0, 1), col(GG, 1)).then_inc(sem("g_log"), 1)
        dve.wait_ge(*after("l2_ss", 1))
        dve.tensor_scalar(col(L2, 64), psum[ab_base + 2][:, 0:64], EPS, None, ALU.add).then_inc(sem("l2_var"), 1)
        dve.wait_ge(*after("l2_std", 1))
        own.link(dve.reciprocal(col(L2, 64), col(L2, 64)))
        dve.tensor_scalar(col(L2, 32), col(L2, 32), HD ** -0.5, None, ALU.mult).then_inc(sem("l2_inv"), 1)
        dve.wait_ge(*after("g_ecum", 2))
        own(dve.tensor_copy(col(CUM, 32), psum[ab_base][:, 0:32]))
        own(dve.tensor_tensor(col(SB, 32), col(BETA, 32), col(ECUM, 32), ALU.mult))
        own.wait()
        for f in range(2 * HEADS):
            dve.wait_ge(*after("l2_bc", f + 1))
            dve.tensor_tensor(qkvT[:, f], psum[l2_base + f % 4][:], qkvT[:, f], ALU.mult).then_inc(sem("l2_mul"), 1)
        dve.wait_ge(*after("l2_mul", 2 * HEADS))
        dve.tensor_copy(col(T0, 1), col(CUM, 1)).then_inc(sem("g_ready"), 1)
        EE = range(4)

        def gbank(e, b, at=0):
            return psum[2 * e + b][:, at:at + 256].rearrange("p (c j) -> p c j", j=P)

        def mask2(m):
            return m.unsqueeze(1).to_broadcast([P, 2, P])

        dve.wait_ge(sem("hT_saved"), 16)
        for n in range(0, 2 * HEADS, 4):
            def head(e):
                return (n + e) // 2

            def per_tok(c, e):
                return th(c)[:, 2 * (e % 2):2 * (e % 2) + 2, head(e):head(e) + 1].to_broadcast([P, 2, P])

            def tokens_of(f, e):
                return qkvT[:, f * HEADS + head(e), 256 * (e % 2):256 * (e % 2) + 256].rearrange("p (c j) -> p c j", j=P)

            for e in EE:
                diff = nm16[e][:, 1]
                dve.wait_ge(sem("g_EB"), n + e + 1)
                if n:
                    dve.wait_ge(sem("g_M128"), n + e - 3)
                own.link(dve.tensor_tensor(diff, gbank(e, 0), per_tok(CUM, e), ALU.subtract))
                dve.tensor_tensor(gs[e][2][:], diff, mask2(m_addS), ALU.add).then_inc(sem("g_D"), 1)
                dve.tensor_tensor(gs[e][1][:], diff, mask2(m_addT), ALU.add).then_inc(sem("g_D"), 1)
                own(dve.tensor_copy(th(ELAST)[:, 2 * (e % 2):2 * (e % 2) + 2, head(e):head(e) + 1], gs[e][0][:, :, P - 1:P]))
            for e in EE:
                dve.wait_ge(sem("g_dec"), 2 * (n + e) + 2)
                for c in range(2):
                    dve.scalar_tensor_tensor(gs[e][2][:, c], gbank(e, 0, 256)[:, c], col(NBETA + (2 * (e % 2) + c) * HEADS + head(e)),
                                             gs[e][2][:, c], ALU.mult, ALU.mult).then_inc(sem("g_M"), 1)
            for e in EE:
                dve.wait_ge(sem("g_qk"), n + e + 1)
                own(dve.tensor_tensor(intraT[:, head(e), 2 * (e % 2):2 * (e % 2) + 2], gbank(e, 1), gs[e][1][:], ALU.mult))
                q = tokens_of(0, e)
                dve.tensor_tensor(q, q, gs[e][0][:], ALU.mult).then_inc(sem("g_qdec"), 1)
            for e in EE:
                dve.wait_ge(sem("g_NT"), n + e + 1)
                dve.tensor_tensor(nm16[e][:, 0], gbank(e, 0), mask2(m_level[0]), ALU.mult).then_inc(sem("g_N16"), 1)
            for e in EE:
                dve.wait_ge(sem("g_N16"), n + e + 1)
                dve.tensor_tensor(gs[e][7][:], nm16[e][:, 0], mask2(ident), ALU.add).then_inc(sem("g_R1"), 1)

            def grow(pe_sem, b, name):
                for e in EE:
                    dve.wait_ge(sem(pe_sem), n + e + 1)
                    dve.tensor_tensor(gs[e][7][:], gbank(e, b), gs[e][7][:], ALU.add).then_inc(sem(name), 1)
            grow("g_R2pe", 1, "g_R2")
            grow("g_R4pe", 0, "g_R4")
            grow("g_R8pe", 1, "g_R8")
            grow("g_Jpe0", 1, "g_J0")
            grow("g_Jpe1", 1, "g_J1")
            grow("g_Jpe2", 1, "g_J2")
            for e in EE:
                dve.wait_ge(sem("g_kvT"), n + e + 1)
                own(dve.tensor_tensor(nm2[e][:, 0], gbank(e, 0), per_tok(SB, e), ALU.mult))
                own(dve.tensor_tensor(tokens_of(2, e), gbank(e, 0), per_tok(EREST, e), ALU.mult))
                dve.tensor_tensor(nm2[e][:, 1], gbank(e, 0, 256), per_tok(BETA, e), ALU.mult).then_inc(sem("g_kv"), 1)
        stage()
        for t in range(NT):
            s_in, s_out = gstate[t % 2], gstate[(t + 1) % 2]
            for hg in range(2):
                hs = slice(4 * hg, 4 * hg + 4)
                if t:
                    dve.wait_ge(*after("s_ws", 2 * (t - 1) + hg + 1))
                    dve.wait_ge(*after("s_ds", 2 * (t - 1) + hg + 1))
                    dve.tensor_tensor(vnew[:, hs], u_tok[:, t, hs], psum[hg][:].rearrange("p (h d) -> p h d", d=P),
                                      ALU.subtract).then_inc(sem("s_v"), 1)
                else:
                    dve.tensor_copy(vnew[:, hs], u_tok[:, t, hs]).then_inc(sem("s_v"), 1)
            if t < NT - 1:
                if t:
                    own(dve.tensor_tensor(s_out[:], s_in[:], th(ELAST)[:, t].unsqueeze(2).to_broadcast([P, HEADS, P]), ALU.mult))
                    own.wait()
                for hg in range(2):
                    hs = slice(4 * hg, 4 * hg + 4)
                    dve.wait_ge(*after("s_ds", 2 * t + hg + 1))
                    ds = psum[4 + hg][:].rearrange("p (h d) -> p h d", d=P)
                    if t:
                        dve.tensor_tensor(s_out[:, hs], ds, s_out[:, hs], ALU.add).then_inc(sem("s_new"), 1)
                    else:
                        dve.tensor_copy(s_out[:, hs], ds).then_inc(sem("s_new"), 1)

        def branch(b, w_panels):
            o = u_tok if b == "a" else hintra
            for t in range(NT):
                own.link(dve.tensor_tensor(osq[b][:], o[:, t], o[:, t], ALU.mult))
                own.link(dve.tensor_reduce(col(ST + HEADS * t, HEADS), osq[b][:], AX.X, ALU.add))
            dve.tensor_scalar(col(ST, 32), col(ST, 32), 1.0 / HD, EPS, ALU.mult, ALU.add).then_inc(sem("o_var"), 1)
            dve.wait_ge(sem("o_std"), 1 + (1 if b == "b" else 0))
            own.link(dve.reciprocal(col(ST, 32), col(ST, 32)))
            w = out_norm[:, 0 if b == "a" else 1].unsqueeze(1).to_broadcast([P, HEADS, HD])
            for t in range(NT):
                own(dve.tensor_tensor(o[:, t], o[:, t], col(ST + HEADS * t, HEADS).unsqueeze(2).to_broadcast([P, HEADS, HD]), ALU.mult))
            own.wait()
            lo_to(next_lo[0] + 1)
            for t in range(NT):
                own(dve.tensor_tensor(o[:, t], o[:, t], w, ALU.mult))
            own.wait()
            gemm(pn["og_" + b], None)
            last = panels[pn["og_" + b][-1]]
            dve.wait_ge(sem("evac_act"), last["at"] + last["nj"])
            for t in range(NT):
                dve.tensor_tensor(o[:, t], o[:, t], og[:, t].rearrange("p (h d) -> p h d", d=HD), ALU.mult).then_inc(sem("y_rows"), 1)
            gate = pn["gate_" + b]
            gemm(gate[0:1], None, ahead=1)
            for f in range(KD):
                if f == 4:
                    lo_to(next_lo[0] + 1)
                dve.wait_ge(sem("y_hi"), f + 1 + (KD if b == "b" else 0))
                dve.tensor_tensor(y_lo[:, f], psum[4 * (gate[1 - f // 4] % 2) + f % 4][:], f32(y_hi[:, f]), ALU.subtract).then_inc(sem("y_lo"), 1)
            gemm(gate[1:2], None)
            if b == "a":
                gemm(w_panels, lambda x, j, bank: dve.tensor_tensor(merged[:, 4 * x + j], bank[:], merged[:, 4 * x + j], ALU.mult))
            else:
                def evac(x, j, bank):
                    f = 4 * x + j
                    own.link(dve.tensor_tensor(gate_b[:, f], bank[:], gate_b[:, f], ALU.mult))
                    return dve.tensor_tensor(merged[:, f], merged[:, f], gate_b[:, f], ALU.add)
                def merged_lo(k):
                    dve.wait_ge(*after("mg_hi", k + 1))
                    dve.tensor_tensor(mg_lo[:, 4 * k:4 * k + 4], merged[:, 4 * k:4 * k + 4], f32(mg_hi[:, 4 * k:4 * k + 4]),
                                      ALU.subtract).then_inc(sem("mg_lo"), 1)
                gemm(w_panels, evac, ahead=1, before_last=lambda: merged_lo(0))
                merged_lo(1)
                lo_to(next_lo[0] + 1)

        stage()
        branch("a", pn["br_a"])
        stage()
        H8 = range(HEADS)

        def scale_keys(hs):
            for h in hs:
                dve.wait_ge(*after("h_e", h + 1))
                dve.tensor_tensor(hqT[:, h], hqT[:, h], hexp[:, h], ALU.mult).then_inc(sem("h_q"), 1)
            for h in hs:
                dve.wait_ge(*after("h_en", h + 1))
                dve.wait_ge(*after("h_dec", h + 1))
                own(dve.tensor_tensor(hexp[:, h], forget[:, h], hexp[:, h], ALU.mult))
                cum = hcum[:, h].rearrange("p (c s) -> p c s", s=QC)
                own(dve.tensor_copy(col(T0 + 8 * h, 8), cum[:, :, QC - 1]))
                own.wait()
                dve.tensor_tensor(cum, col(T0 + 8 * h, 8).unsqueeze(2).to_broadcast([P, SEQ // QC, QC]), cum, ALU.subtract).then_inc(sem("h_d"), 1)
            for h in hs:
                dve.wait_ge(*after("h_ed", h + 1))
                dve.tensor_tensor(forget[:, h], forget[:, h], hcum[:, h], ALU.mult).then_inc(sem("h_kd"), 1)

        gemm(pn["f"], None)
        last = panels[pn["f"][-1]]
        dve.wait_ge(sem("evac_act"), last["at"] + last["nj"])
        for h in H8:
            dve.tensor_scalar(forget[:, h], forget[:, h], col(OML + h), col(LBC + h), ALU.mult, ALU.add).then_inc(sem("h_f"), 1)
        for h in H8:
            dve.wait_ge(*after("h_ln", h + 1))
            dve.tensor_tensor_scan(hcum[:, h], scan_mask[:], hexp[:, h], 0.0, ALU.mult, ALU.add).then_inc(sem("h_cum"), 1)
            own(dve.tensor_scalar(forget[:, h], forget[:, h], -1.0, 1.0, ALU.mult, ALU.add))
        gemm(pn["q"], None)
        own.wait()
        last = panels[pn["q"][-1]]
        dve.wait_ge(sem("evac_act"), last["at"] + last["nj"])
        scale_keys(H8[0:4])
        lo_to(next_lo[0] + 2)
        scale_keys(H8[4:8])
        gemm(pn["i"], None)
        dve.wait_ge(sem("h_kdT"), HEADS)
        for h in H8:
            dve.wait_ge(*after("h_in", h + 1))
            dve.tensor_tensor(hintra[:, :, h], psum[h][:].rearrange("p (t j) -> p t j", j=P),
                              m_hgrn.unsqueeze(1).to_broadcast([P, NT, P]), ALU.mult)
        stage()
        own.link(dve.memset(hstate[0][:], 0.0))
        for t in range(NT):
            for s in range(2):
                n = 2 * t + s
                s_in, s_out = hstate[n % 3], hstate[(n + 1) % 3]
                for h in H8:
                    if h % 4 == 0:
                        dve.wait_ge(*after("hs_kv", 2 * n + h // 4 + 1))
                        if n:
                            dve.wait_ge(*after("hs_S", HEADS * n))
                        if n >= 2:
                            dve.wait_ge(*after("hs_ope", 2 * ((n - 2) // 2) + 2))
                    kv = psum[2 * s + h // 4][:, (h % 4) * P:(h % 4) * P + P]
                    dve.scalar_tensor_tensor(s_out[:, h], s_in[:, h], col(DEC8 + 8 * h + n), kv, ALU.mult, ALU.add).then_inc(sem("hs_S"), 1)
        stage()
        branch("b", pn["br_b"])
        stage()
        dve.wait_ge(*after("mem_in", 16))
        norm_rows("mem", mem_tok, MEM // P)
        dve.wait_ge(sem("h_back"), 16)
        gemm(pn["mix_out"], add_to(resid), ahead=1)
        stage(wait=False)
        norm_T("mem", G_MEM, memT_hi, memT_lo, MEM // P)
        lo_to(next_lo[0] + 1)
        norm_rows("x", resid)
        gemm(pn["xk"], None)
        gemm(pn["xv"], None)
        norm_T("x", G_X, hT_hi, hT_lo)
        gemm(pn["xq"], None)
        stage()
        n_x = XH * NT

        def xrow_max(i):
            dve.wait_ge(*after("xa_sc", i + 1))
            own.link(dve.tensor_reduce(col(T0 + i), psum[i % 4][:, 0:MEM], AX.X, ALU.max))
            dve.tensor_scalar(col(T0 + i), col(T0 + i), -XD ** -0.5, None, ALU.mult).then_inc(sem("xa_max"), 1)

        def xhead_lo(h):
            for c in range(2):
                dve.wait_ge(*after("xa_hi", 2 * h + c + 1))
                dve.tensor_tensor(xo_lo[:, 2 * h + c], psum[6 + c][:], f32(xo_hi[:, 2 * h + c]),
                                  ALU.subtract).then_inc(sem("xa_lo"), 1)

        xrow_max(0)
        xrow_max(1)
        for i in range(n_x):
            if i + 2 < n_x:
                xrow_max(i + 2)
            dve.wait_ge(*after("xa_exp", i + 1))
            own.link(dve.reciprocal(col(SUMS + i), col(SUMS + i)))
            dve.tensor_scalar(xprobs[i % 4][:], xprobs[i % 4][:], col(SUMS + i), None, ALU.mult).then_inc(sem("xa_norm"), 1)
            if i % NT == 3 and i >= NT:
                xhead_lo(i // NT - 1)
        xhead_lo(XH - 1)
        stage()
        gemm(pn["xo"], add_to(resid))
        def gu_lo(b, us):
            for u in us:
                dve.wait_ge(sem("gu_hi"), 4 * b + u + 1)
                dve.tensor_tensor(e_lo[u][:], eraw[u][:], f32(e_hi[u][:]), ALU.subtract).then_inc(sem("gu_lo"), 1)

        stage(wait=False)
        dve.wait_ge(*after("router_in", 16 * 5))
        norm("ffn", resid, None, None, None, gain=ffn_gain)
        gu_lo(0, range(3))
        own.link(dve.tensor_scalar(iota_neg[:], iota[:, 0:EPG], float(-P), None, ALU.add))
        dve.wait_ge(*after("rt_pe", 1))
        R = NG + NE
        own.link(dve.tensor_tensor(logits[:], psum[0][:, 0:NT * R].rearrange("p (t n) -> p t n", n=R),
                                   b_router[:].unsqueeze(1).to_broadcast([P, NT, R]), ALU.add))

        def bc(ap, n):
            return ap.unsqueeze(2).to_broadcast([P, NT, n])

        def first_max(hot, vals, n, top):
            idx, eq = per_t[7][:, 0:NT], over_e[:, 0:NT * n].rearrange("p (t n) -> p t n", n=n)
            own.link(dve.tensor_reduce(top, vals, AX.X, ALU.max))
            own.link(dve.tensor_tensor(eq, vals, bc(top, n), ALU.is_equal))
            own.link(dve.tensor_tensor(eq, eq, iota_neg[:, 0:n].unsqueeze(1).to_broadcast([P, NT, n]), ALU.mult))
            own.link(dve.tensor_reduce(idx, eq, AX.X, ALU.min))
            own.link(dve.tensor_tensor(hot, iota_neg[:, 0:n].unsqueeze(1).to_broadcast([P, NT, n]), bc(idx, n), ALU.is_equal))

        g_max, v1, v2, g_p = (per_t[k][:, 0:NT] for k in range(4))
        first_max(hot_g[:], logits[:, :, 0:NG], NG, g_max)
        for t in range(NT):
            tmp = over_e[:, 0:NE]
            own.link(dve.tensor_tensor(tmp.rearrange("p (g e) -> p g e", e=EPG), logits[:, t, NG:].rearrange("p (g e) -> p g e", e=EPG),
                                       hot_g[:, t].unsqueeze(2).to_broadcast([P, NG, EPG]), ALU.mult))
            own.link(dve.tensor_reduce(chosen[:, t], tmp.rearrange("p (g e) -> p e g", e=EPG), AX.X, ALU.add))
        dve.tensor_tensor(logits[:, :, 0:NG], logits[:, :, 0:NG], bc(g_max, NG), ALU.subtract).then_inc(sem("rt_exp"), 1)
        first_max(hot_e[:, 0], chosen[:], EPG, v1)
        own.link(dve.scalar_tensor_tensor(chosen[:], hot_e[:, 0], -BIG, chosen[:], ALU.mult, ALU.add))
        first_max(hot_e[:, 1], chosen[:], EPG, v2)
        dve.tensor_tensor(weight[:, 1], v2, v1, ALU.subtract).then_inc(sem("rt_exp"), 1)
        for a in range(2):
            for t in range(NT):
                own(dve.tensor_tensor(experts[:, a, t].rearrange("p (g e) -> p g e", e=EPG),
                                      hot_g[:, t].unsqueeze(2).to_broadcast([P, NG, EPG]),
                                      hot_e[:, a, t].unsqueeze(1).to_broadcast([P, NG, EPG]), ALU.mult))
        own.wait()
        dve.tensor_copy(per_t[6][:, 0:1], experts[:, 1, NT - 1, 0:1]).then_inc(sem("rt_taken"), 1)
        dve.wait_ge(*after("rt_pe", 2))
        extra, total, start, _ = per_e
        own.link(dve.tensor_scalar(extra[:], psum[2][:, 0:NE], BLK + 0.5, None, ALU.is_gt))
        for k in range(2, NRB):
            own.link(dve.scalar_tensor_tensor(extra[:], psum[2][:, 0:NE], k * BLK + 0.5, extra[:], ALU.is_gt, ALU.add))
        own.link(dve.tensor_tensor_scan(total[:], ones[:, 0:NE], extra[:], 0.0, ALU.mult, ALU.add))
        own(dve.tensor_tensor(start[:], total[:], extra[:], ALU.subtract))
        own.wait()
        pos, eid, first, further, r = per_t[0:5]
        picks = pick[:].rearrange("p a n -> p (a n)").rearrange("p (n e) -> p n e", e=NE)
        taken = experts[:].rearrange("p a t e -> p (a t) e")
        own.link(dve.tensor_copy(rank[:].rearrange("p t e -> p (t e)"), psum[1][:, 0:NT * NE]))
        own.link(dve.tensor_tensor(pick[:], experts[:].rearrange("p a t e -> p a (t e)"),
                                   rank[:].rearrange("p t e -> p (t e)").unsqueeze(1).to_broadcast([P, 2, NT * NE]), ALU.mult))
        own.link(dve.tensor_reduce(pos[:], picks, AX.X, ALU.add))
        for dst, of in ((eid, iota[:, 0:NE]), (first, start[:])):
            own.link(dve.tensor_tensor(picks, taken, of.unsqueeze(1).to_broadcast([P, 2 * NT, NE]), ALU.mult))
            own.link(dve.tensor_reduce(dst[:], picks, AX.X, ALU.add))
        own.link(dve.tensor_scalar(further[:], pos[:], BLK - 0.5, None, ALU.is_gt))
        for k in range(2, NRB):
            own.link(dve.scalar_tensor_tensor(further[:], pos[:], k * BLK - 0.5, further[:], ALU.is_gt, ALU.add))
        own(dve.scalar_tensor_tensor(r[:], further[:], float(-BLK), pos[:], ALU.mult, ALU.add))
        own.link(dve.tensor_tensor(first[:], first[:], further[:], ALU.add))
        own.link(dve.scalar_tensor_tensor(first[:], first[:], NE - 1.0, eid[:], ALU.add, ALU.subtract))
        own.link(dve.scalar_tensor_tensor(first[:], further[:], 0.5, first[:], ALU.is_gt, ALU.mult))
        own.link(dve.tensor_tensor(first[:], first[:], eid[:], ALU.add))
        own(dve.scalar_tensor_tensor(row_of[:], first[:], float(BLK), r[:], ALU.mult, ALU.add))
        for n in range(2 * NT):
            own(dve.tensor_scalar(hot_r[:, n], iota[:, 0:BLK], r[:, n:n + 1], None, ALU.is_equal))
            own(dve.tensor_scalar(hot_b[:, n], iota[:, 0:BLOCKS + 1], first[:, n:n + 1], tokid[:, n % NT:n % NT + 1], ALU.is_equal, ALU.mult))
        own.wait()
        dve.tensor_copy(per_t[6][:, 0:1], hot_b[:, 0, 0:1]).then_inc(sem("rt_taken"), 1)
        dve.wait_ge(*after("rt_act", 1))
        own.link(dve.tensor_reduce(g_p, logits[:, :, 0:NG], AX.X, ALU.add))
        dve.wait_ge(*after("rt_act", 2))
        own.link(dve.tensor_scalar(v1, weight[:, 1], 1.0, None, ALU.add))
        own.link(dve.tensor_tensor(g_p, g_p, v1, ALU.mult))
        own.link(dve.reciprocal(weight[:, 0], g_p))
        own(dve.tensor_tensor(weight[:, 1], weight[:, 1], weight[:, 0], ALU.mult))
        own(dve.tensor_copy(over[:, OVER:OVER + 1], total[:, NE - 1:NE]))
        tmp = over_e[:, 0:OVER * NE].rearrange("p (i e) -> p i e", e=NE)
        own.link(dve.tensor_tensor(tmp, total[:].unsqueeze(1).to_broadcast([P, OVER, NE]),
                                   iota[:, 0:OVER].unsqueeze(2).to_broadcast([P, OVER, NE]), ALU.is_le))
        own.link(dve.tensor_reduce(over_n[:], tmp, AX.X, ALU.add))
        own.link(dve.tensor_scalar(over[:, 0:OVER], over_n[:], float(NE - 1), None, ALU.min))
        dve.wait_ge(*after("rt_pe", 3))
        own.link(dve.tensor_copy(tok_of[:], psum[3][0:BLK, 0:BLOCKS + 1]))
        stage()

        def d_lo(b):
            for u in range(2):
                dve.wait_ge(sem("d_hi"), 2 * b + u + 1)
                dve.tensor_tensor(e_lo[4 + u][:], eraw[4 + u][:], f32(e_hi[4 + u][:]), ALU.subtract).then_inc(sem("d_lo"), 1)

        def product(b, first=False):
            dve.wait_ge(sem("e_silu"), b + 1)
            dve.wait_ge(sem("gu_used"), 4 * b + 4)
            if not first:
                dve.wait_ge(sem("h_T"), b)
            dve.tensor_tensor(act_h[:], psum[1][0:BLK], silu_g[:], ALU.mult).then_inc(sem("e_prod"), 1)

        def x_lo(b):
            dve.wait_ge(sem("x_hi"), b + 1)
            dve.tensor_tensor(bT_lo[:], psum[2][:].rearrange("p (k r) -> p k r", r=BLK), f32(bT_hi[:]),
                              ALU.subtract).then_inc(sem("x_lo"), 1)

        def h_lo(b):
            dve.wait_ge(sem("h_hi"), b + 1)
            dve.tensor_tensor(aT_lo[:], psum[4][:, 0:FF // P * BLK].rearrange("p (k r) -> p k r", r=BLK), f32(aT_hi[:]),
                              ALU.subtract).then_inc(sem("h_lo"), 1)

        gu_lo(0, (3,))
        x_lo(0)
        gu_lo(1, (0, 1, 2))
        product(0, True)
        gu_lo(1, (3,))
        x_lo(1)
        d_lo(0)
        h_lo(0)
        with dve.Fori(1, NE - 1) as e:
            gu_lo(e + 1, (0, 1, 2))
            product(e)
            gu_lo(e + 1, (3,))
            x_lo(e + 1)
            d_lo(e)
            h_lo(e)
        product(NE - 1)
        d_lo(NE - 1)
        h_lo(NE - 1)
        n_over = dve.value_load(over[0:1, OVER:OVER + 1], min_val=0, max_val=OVER)
        with dve.If(n_over > 0):
            with dve.Fori(NE, BLOCKS) as b:
                gu_lo(b, range(4))
                x_lo(b)
                product(b)
                d_lo(b)
                h_lo(b)
        stage()
        for t in range(NT):
            dve.wait_ge(*after(f"picked{t}", 32))
            own(dve.scalar_tensor_tensor(resid[:, t], picked[t][:, 0], weight[:, 0, t:t + 1], resid[:, t], ALU.mult, ALU.add))
            own.wait()
            dve.scalar_tensor_tensor(resid[:, t], picked[t][:, 1], weight[:, 1, t:t + 1], resid[:, t], ALU.mult, ALU.add).then_inc(sem("summed"), 1)
        dve.wait_ge(*after("last_in", 16))
        norm("last", resid, None, None, None, rows=resid, gain=last_gain)
    ctx.close()


INPUTS = ["x", "even_norm", "even_w_in", "fourier_w", "q_gain", "k_gain", "even_w_out", "odd_norm", "odd_w_in",
          "conv_w", "conv_b", "gate_a_w", "gate_a_b", "gate_x_w", "gate_x_b", "rglru_lambda", "odd_w_out", "final_norm",
          "mem_2", "norm_mix_w_2", "w_in_2", "conv_w_2", "gdn_a_log_2", "gdn_dt_bias_2", "gdn_out_norm_w_2",
          "hgrn_lb_2", "hgrn_out_norm_w_2", "w_branch_a_2", "w_branch_b_2", "w_out_2", "norm_xattn_w_2",
          "norm_mem_w_2", "xattn_wq_2", "xattn_wkv_2", "xattn_wo_2", "norm_ffn_w_2", "router_group_w_2",
          "router_group_b_2", "router_expert_w_2", "router_expert_b_2", "expert_w_gate_2", "expert_w_up_2",
          "expert_w_down_2", "final_norm_w_2"]


def kernel(**inputs):
    from concourse import bacc
    from concourse.bass_utils import run_bass_kernel_spmd

    nc = bacc.Bacc("TRN2", target_bir_lowering=False, num_devices=1)
    arrays = {name: np.ascontiguousarray(inputs[name]) for name in INPUTS}
    arrays.update(constants())
    io = {name: nc.dram_tensor(name, a.shape, mybir.dt.from_np(a.dtype), kind="ExternalInput").ap()
          for name, a in arrays.items()}
    io["out"] = nc.dram_tensor("out", (1, SEQ, D), F32, kind="ExternalOutput").ap()
    build(nc, io)
    result = run_bass_kernel_spmd(nc, [arrays], core_ids=[0])
    return result.results[0]["out"]
```
